# Optimizing a Trainium2 kernel written in Bass

```python
import math
import jax, jax.numpy as jnp
from jax import lax
import numpy as np

D_MODEL = 1024
BATCH = 1
SEQ = 128
DEPTH = 2
DEC_BATCH = 1
DEC_SEQ = 256
PAST_LEN = 128

GRID_W = 64
ROPE_BASE = 10000.0
N_HEADS = 8
N_KV_HEADS = 2
GROUPS = N_HEADS // N_KV_HEADS
HEAD_DIM = 64
WINDOW = 128
BLOCK = 128
Q_DIM = N_HEADS * HEAD_DIM
KV_DIM = N_KV_HEADS * HEAD_DIM
POOL_SIZES = (2, 4, 8, 16)
N_POOL_GROUPS = len(POOL_SIZES)
POOL_DIM = D_MODEL // 2
POOL_GROUP_DIM = POOL_DIM // N_POOL_GROUPS
IN_DIM = Q_DIM + 2 * KV_DIM + POOL_DIM
MIX_OUT = Q_DIM + POOL_DIM
CONV_DIM = D_MODEL
CONV_WIDTH = 31
N_KEYS = 128
N_EXPERTS = N_KEYS * N_KEYS
PEER_HEADS = 8
PEER_QDIM = 256
PEER_HALF = PEER_QDIM // 2
PEER_TOPK = 16
PEER_CHUNK = 128
N_ATTN_LAYERS = (DEPTH + 1) // 2
N_CONV_LAYERS = DEPTH // 2
EPS = 1e-6
NEG = -1e30

kernel_name = "hybrid_prefix_diffusion_step"

def rms_norm(x, g):
    xf = x.astype(jnp.float32)
    y = xf * lax.rsqrt(jnp.mean(xf * xf, axis=-1, keepdims=True) + EPS)
    return (y * g.astype(jnp.float32)).astype(x.dtype)

def layer_norm(x, g, b):
    xf = x.astype(jnp.float32)
    mu = jnp.mean(xf, axis=-1, keepdims=True)
    var = jnp.mean(jnp.square(xf - mu), axis=-1, keepdims=True)
    y = (xf - mu) * lax.rsqrt(var + EPS)
    return (y * g.astype(jnp.float32) + b.astype(jnp.float32)).astype(x.dtype)

def adaln(cvec, w, b):
    m = jax.nn.silu(cvec) @ w + b
    return jnp.split(m[:, None, :], 6, axis=-1)

def modulate(h, shift, scale):
    return h * (1 + scale) + shift

def _rotate(x, ang):
    m = ang.shape[-1]
    cos = jnp.cos(ang)[:, None, :]
    sin = jnp.sin(ang)[:, None, :]
    x1, x2 = x[..., :m], x[..., m:]
    return jnp.concatenate([x1 * cos - x2 * sin, x2 * cos + x1 * sin], axis=-1)

def axial_rope(x):
    S = x.shape[1]
    n_rows = S // GRID_W
    rows = jnp.repeat(jnp.arange(n_rows, dtype=jnp.float32), GRID_W)
    cols = jnp.tile(jnp.arange(GRID_W, dtype=jnp.float32), n_rows)
    half = HEAD_DIM // 2
    quarter = half // 2
    freqs = ROPE_BASE ** (-jnp.arange(quarter, dtype=jnp.float32) / quarter)
    xf = x.astype(jnp.float32)
    xr = _rotate(xf[..., :half], rows[:, None] * freqs[None, :])
    xc = _rotate(xf[..., half:], cols[:, None] * freqs[None, :])
    return jnp.concatenate([xr, xc], axis=-1).astype(x.dtype)

def sink_softmax(logits, sink):
    sk = jnp.broadcast_to(sink.astype(jnp.float32).reshape(N_KV_HEADS, GROUPS)[None, :, :, None, None],
                          logits.shape[:-1] + (1,))
    p = jax.nn.softmax(jnp.concatenate([logits, sk], axis=-1), axis=-1)
    return p[..., :-1]

def context_attention(q, k, v, sink):
    B, S = q.shape[0], q.shape[1]
    nb = S // BLOCK
    scale = HEAD_DIM ** -0.5
    qb = q.reshape(B, nb, BLOCK, N_KV_HEADS, GROUPS, HEAD_DIM).transpose(1, 0, 2, 3, 4, 5)

    def blk(qn):
        s = jnp.einsum('bqkgd,bskd->bkgqs', qn, k).astype(jnp.float32) * scale
        p = sink_softmax(s, sink).astype(v.dtype)
        return jnp.einsum('bkgqs,bskd->bqkgd', p, v)

    o = lax.map(blk, qb)
    return o.transpose(1, 0, 2, 3, 4, 5).reshape(B, S, Q_DIM)

def latent_attention(q, k, v, ck, cv, sink):
    B, S = q.shape[0], q.shape[1]
    nb = S // BLOCK
    P = ck.shape[1]
    scale = HEAD_DIM ** -0.5
    qb = q.reshape(B, nb, BLOCK, N_KV_HEADS, GROUPS, HEAD_DIM).transpose(1, 0, 2, 3, 4, 5)
    pad = ((0, 0), (BLOCK, BLOCK), (0, 0), (0, 0))
    kp = jnp.pad(k, pad).reshape(B, nb + 2, BLOCK, N_KV_HEADS, HEAD_DIM)
    vp = jnp.pad(v, pad).reshape(B, nb + 2, BLOCK, N_KV_HEADS, HEAD_DIM)
    kw = jnp.concatenate([kp[:, :-2], kp[:, 1:-1], kp[:, 2:]], axis=2).transpose(1, 0, 2, 3, 4)
    vw = jnp.concatenate([vp[:, :-2], vp[:, 1:-1], vp[:, 2:]], axis=2).transpose(1, 0, 2, 3, 4)
    qpos = jnp.arange(nb)[:, None] * BLOCK + jnp.arange(BLOCK)[None, :]
    kpos = (jnp.arange(nb)[:, None] - 1) * BLOCK + jnp.arange(3 * BLOCK)[None, :]
    valid = ((jnp.abs(qpos[:, :, None] - kpos[:, None, :]) <= WINDOW)
             & (kpos >= 0)[:, None, :] & (kpos < S)[:, None, :])

    def blk(args):
        qn, kn, vn, mn = args
        s_ctx = jnp.einsum('bqkgd,bpkd->bkgqp', qn, ck).astype(jnp.float32) * scale
        s_loc = jnp.einsum('bqkgd,bskd->bkgqs', qn, kn).astype(jnp.float32) * scale
        s_loc = jnp.where(mn[None, None, None], s_loc, NEG)
        p = sink_softmax(jnp.concatenate([s_ctx, s_loc], axis=-1), sink).astype(vn.dtype)
        return (jnp.einsum('bkgqp,bpkd->bqkgd', p[..., :P], cv)
                + jnp.einsum('bkgqs,bskd->bqkgd', p[..., P:], vn))

    o = lax.map(blk, (qb, kw, vw, valid))
    return o.transpose(1, 0, 2, 3, 4, 5).reshape(B, S, Q_DIM)

def multiscale_pool(u, w_pool, pool_scale):
    B, S, _ = u.shape
    uf = u.astype(jnp.float32)
    cs = jnp.pad(lax.cumsum(uf, axis=1), ((0, 0), (1, 0), (0, 0)))
    t = jnp.arange(S)
    outs = []
    for g, w in enumerate(POOL_SIZES):
        lo = jnp.clip(t - w // 2, 0, S)
        hi = jnp.clip(t + (w - w // 2), 0, S)
        sl = slice(g * POOL_GROUP_DIM, (g + 1) * POOL_GROUP_DIM)
        csg = cs[:, :, sl]
        mean = (csg[:, hi] - csg[:, lo]) / (hi - lo).astype(jnp.float32)[None, :, None]
        outs.append(mean - uf[:, :, sl])
    pooled = jnp.stack(outs, axis=2).astype(u.dtype)
    mixed = jnp.einsum('bsgc,gcd->bsgd', pooled, w_pool).reshape(B, S, POOL_DIM)
    return mixed * pool_scale

def _split_in(proj):
    q = proj[..., :Q_DIM]
    k = proj[..., Q_DIM:Q_DIM + KV_DIM]
    v = proj[..., Q_DIM + KV_DIM:Q_DIM + 2 * KV_DIM]
    u = proj[..., Q_DIM + 2 * KV_DIM:]
    return q, k, v, u

def attn_pool_context(h, w_in, sink, w_pool, pool_scale, w_out):
    B, S, _ = h.shape
    q, k, v, u = _split_in(h @ w_in)
    q = q.reshape(B, S, N_HEADS, HEAD_DIM)
    k = k.reshape(B, S, N_KV_HEADS, HEAD_DIM)
    v = v.reshape(B, S, N_KV_HEADS, HEAD_DIM)
    att = context_attention(q, k, v, sink)
    pool = multiscale_pool(u, w_pool, pool_scale)
    out = jnp.concatenate([att, pool], axis=-1) @ w_out
    return out, k, v

def attn_pool_latent(h, ck, cv, w_in, sink, w_pool, pool_scale, w_out):
    B, S, _ = h.shape
    q, k, v, u = _split_in(h @ w_in)
    q = axial_rope(q.reshape(B, S, N_HEADS, HEAD_DIM))
    k = axial_rope(k.reshape(B, S, N_KV_HEADS, HEAD_DIM))
    v = v.reshape(B, S, N_KV_HEADS, HEAD_DIM)
    att = latent_attention(q, k, v, ck, cv, sink)
    pool = multiscale_pool(u, w_pool, pool_scale)
    return jnp.concatenate([att, pool], axis=-1) @ w_out

def conformer_conv(h, w1, b1, w_dw, b_dw, ln_g, ln_b, w2, b2):
    a = h @ w1 + b1
    a = a[..., :CONV_DIM] * jax.nn.sigmoid(a[..., CONV_DIM:])
    a = lax.conv_general_dilated(a, w_dw[:, None, :].astype(a.dtype), window_strides=(1,),
                                 padding=((CONV_WIDTH // 2, CONV_WIDTH // 2),),
                                 dimension_numbers=('NWC', 'WIO', 'NWC'),
                                 feature_group_count=CONV_DIM) + b_dw
    a = jax.nn.silu(layer_norm(a, ln_g, ln_b))
    return a @ w2 + b2

def peer(h, w_q, sub_keys, u_tab, v_tab):
    B, S, D = h.shape
    T = B * S
    x = h.reshape(T, D)
    q = (x @ w_q).reshape(T, PEER_HEADS, 2, PEER_HALF)
    s = jnp.einsum('thpc,hpnc->thpn', q, sub_keys).astype(jnp.float32)
    s1, i1 = lax.top_k(s[:, :, 0], PEER_TOPK)
    s2, i2 = lax.top_k(s[:, :, 1], PEER_TOPK)
    cand = (s1[..., :, None] + s2[..., None, :]).reshape(T, PEER_HEADS, PEER_TOPK * PEER_TOPK)
    cidx = (i1[..., :, None] * N_KEYS + i2[..., None, :]).reshape(T, PEER_HEADS, PEER_TOPK * PEER_TOPK)
    top_s, pos = lax.top_k(cand, PEER_TOPK)
    idx = jnp.take_along_axis(cidx, pos, axis=-1).reshape(T, PEER_HEADS * PEER_TOPK)
    g = jax.nn.softmax(top_s, axis=-1).reshape(T, PEER_HEADS * PEER_TOPK).astype(x.dtype)
    nc = T // PEER_CHUNK

    def chunk_fn(args):
        xc, ic, gc = args
        uc = jnp.take(u_tab, ic, axis=0)
        a = jnp.einsum('cd,ckd->ck', xc, uc)
        wgt = gc * jax.nn.gelu(a, approximate=False)
        vc = jnp.take(v_tab, ic, axis=0)
        return jnp.einsum('ck,ckd->cd', wgt, vc)

    y = lax.map(chunk_fn, (x.reshape(nc, PEER_CHUNK, D),
                           idx.reshape(nc, PEER_CHUNK, -1),
                           g.reshape(nc, PEER_CHUNK, -1)))
    return y.reshape(B, S, D)

def setup_inputs(seed: int = 0) -> dict:
    key = jax.random.key(seed)
    ks = iter(jax.random.split(key, 40))
    nrm = lambda shape, s=1.0: jax.random.normal(next(ks), shape, jnp.float32) * s
    D = D_MODEL
    L, LA, LC = DEPTH, N_ATTN_LAYERS, N_CONV_LAYERS
    return {
        'x_prompt': nrm((BATCH, SEQ, D)),
        'x_sample': nrm((DEC_BATCH, DEC_SEQ, D)),
        'c': nrm((DEC_BATCH, D)),
        'cache_k': nrm((DEC_BATCH, LA, PAST_LEN, N_KV_HEADS, HEAD_DIM)),
        'cache_v': nrm((DEC_BATCH, LA, PAST_LEN, N_KV_HEADS, HEAD_DIM)),
        'c_ctx': nrm((D,)),
        'mod_w': nrm((L, D, 6 * D), 0.5 * D ** -0.5),
        'mod_b': nrm((L, 6 * D), 0.02),
        'norm_mix_g': 1.0 + nrm((L, D), 0.1),
        'norm_ffn_g': 1.0 + nrm((L, D), 0.1),
        'w_in': nrm((LA, D, IN_DIM), D ** -0.5),
        'attn_sink': nrm((LA, N_HEADS)),
        'w_pool': nrm((LA, N_POOL_GROUPS, POOL_GROUP_DIM, POOL_GROUP_DIM), POOL_GROUP_DIM ** -0.5),
        'pool_scale': 1.0 + nrm((LA, POOL_DIM), 0.1),
        'w_out': nrm((LA, MIX_OUT, D), MIX_OUT ** -0.5),
        'conv_w1': nrm((LC, D, 2 * CONV_DIM), D ** -0.5),
        'conv_b1': nrm((LC, 2 * CONV_DIM), 0.02),
        'conv_dw': nrm((LC, CONV_WIDTH, CONV_DIM), CONV_WIDTH ** -0.5),
        'conv_dw_b': nrm((LC, CONV_DIM), 0.02),
        'conv_ln_g': 1.0 + nrm((LC, CONV_DIM), 0.1),
        'conv_ln_b': nrm((LC, CONV_DIM), 0.02),
        'conv_w2': nrm((LC, CONV_DIM, D), CONV_DIM ** -0.5),
        'conv_b2': nrm((LC, D), 0.02),
        'peer_wq': nrm((L, D, PEER_HEADS * PEER_QDIM), D ** -0.5),
        'peer_keys': nrm((L, PEER_HEADS, 2, N_KEYS, PEER_HALF), PEER_HALF ** -0.5),
        'peer_u': nrm((L, N_EXPERTS, D), D ** -0.5),
        'peer_v': nrm((L, N_EXPERTS, D), 1.0),
        'final_norm_g': 1.0 + nrm((D,), 0.1),
    }

def reference(x_prompt, x_sample, c, cache_k, cache_v, c_ctx, mod_w, mod_b, norm_mix_g, norm_ffn_g,
              w_in, attn_sink, w_pool, pool_scale, w_out, conv_w1, conv_b1, conv_dw, conv_dw_b,
              conv_ln_g, conv_ln_b, conv_w2, conv_b2, peer_wq, peer_keys, peer_u, peer_v, final_norm_g):
    xp = x_prompt
    xs = x_sample
    new_k = []
    new_v = []
    for l in range(DEPTH):
        j = l // 2
        mp = adaln(c_ctx[None, :], mod_w[l], mod_b[l])
        ms = adaln(c, mod_w[l], mod_b[l])
        hp = modulate(rms_norm(xp, norm_mix_g[l]), mp[0], mp[1])
        hs = modulate(rms_norm(xs, norm_mix_g[l]), ms[0], ms[1])
        if l % 2 == 0:
            op, kc, vc = attn_pool_context(hp, w_in[j], attn_sink[j], w_pool[j], pool_scale[j], w_out[j])
            os_ = attn_pool_latent(hs, cache_k[:, j], cache_v[:, j], w_in[j], attn_sink[j],
                                   w_pool[j], pool_scale[j], w_out[j])
            new_k.append(kc)
            new_v.append(vc)
        else:
            op = conformer_conv(hp, conv_w1[j], conv_b1[j], conv_dw[j], conv_dw_b[j],
                                conv_ln_g[j], conv_ln_b[j], conv_w2[j], conv_b2[j])
            os_ = conformer_conv(hs, conv_w1[j], conv_b1[j], conv_dw[j], conv_dw_b[j],
                                 conv_ln_g[j], conv_ln_b[j], conv_w2[j], conv_b2[j])
        xp = xp + mp[2] * op
        xs = xs + ms[2] * os_
        hp = modulate(rms_norm(xp, norm_ffn_g[l]), mp[3], mp[4])
        hs = modulate(rms_norm(xs, norm_ffn_g[l]), ms[3], ms[4])
        xp = xp + mp[5] * peer(hp, peer_wq[l], peer_keys[l], peer_u[l], peer_v[l])
        xs = xs + ms[5] * peer(hs, peer_wq[l], peer_keys[l], peer_u[l], peer_v[l])
    y_prompt = rms_norm(xp, final_norm_g)
    y_sample = rms_norm(xs, final_norm_g)
    state_k = jnp.stack(new_k, axis=1)
    state_v = jnp.stack(new_v, axis=1)
    return (y_prompt, y_sample, state_k, state_v)


_drawn_inputs = setup_inputs


def setup_inputs(seed=0):
    import zlib

    import numpy as np

    out = dict(_drawn_inputs(seed))
    spreads = {}
    factors = {'attn_sink': 6.1,
     'conv_b1': 4.651,
     'conv_dw_b': 3.775,
     'conv_ln_b': 4.989,
     'conv_b2': 3.75}
    for name, (base, spread) in spreads.items():
        noise = np.random.default_rng([zlib.crc32(name.encode()), seed]).standard_normal(out[name].shape)
        drawn = base * np.exp(spread * noise) if base else spread * noise
        out[name] = __import__('jax').numpy.asarray(drawn.astype(out[name].dtype))
    for name, factor in factors.items():
        out[name] = (out[name] * factor).astype(out[name].dtype)
    return out
```

```python
from contextlib import ExitStack

import concourse.bass as bass
from concourse import mybir
import numpy as np

ALU = mybir.AluOpType
ACT = mybir.ActivationFunctionType
AX = mybir.AxisListType
F32 = mybir.dt.float32
F32R = mybir.dt.float32r
BF16 = mybir.dt.bfloat16
U32 = mybir.dt.uint32

P = 128
D = 1024
KC = D // P
CTX = 128
LAT = 256
T = CTX + LAT
NT = T // P
DEPTH = 2
EPS = 1e-6
NEG = -1e30
GRID_W = 64
HEAD_DIM = 64
N_HEADS = 8
PAIRS = N_HEADS // 2
SCALE = HEAD_DIM ** -0.5
WINDOW = 128
PAST = 128
POOL_SIZES = (2, 4, 8, 16)
NG = len(POOL_SIZES)
PAD = max(POOL_SIZES) // 2
POOL_W = PAD + CTX + PAD + LAT + PAD
CONV_WIDTH = 31
CPAD = CONV_WIDTH // 2
CONV_IN = CPAD + CTX + CPAD + LAT + CPAD
CONV_OUT = CONV_IN - 2 * CPAD
N_KEYS = 128
PEER_HEADS = 8
HS = 2 * PEER_HEADS
TOPK = 16
LOWEST = -3.0e38

TOK = 8
CHUNK = 32
NCHUNK = T // CHUNK
GBLOCKS = T // TOK
UBLOCKS = N_KEYS - GBLOCKS
EXP_AT = UBLOCKS - 16
QUAD = 4

WORK = 16600

RING = 4
LEAD = 2
MOD_BLOCKS = DEPTH * 6 * KC

SEGMENTS = [("in", 10), ("out", 8), ("wq0", HS), ("u0", N_KEYS), ("v0", N_KEYS),
            ("w1", 16), ("w2", 8), ("wq1", HS), ("u1", N_KEYS), ("v1", N_KEYS)]
M0, R0 = {}, {}
_m = _r = 0
for _name, _count in SEGMENTS:
    M0[_name], R0[_name] = _m, _r
    _m += _count
    _r += 0 if _name[0] == "v" else _count
BLOCKS = _m

SEGS = ((0, 0, CTX), (1, CTX, LAT))


def since(engine, semaphore, count):
    if isinstance(count, int) and count <= 0:
        return
    engine.wait_ge(semaphore, count)


def rounds(engine, count, body, peel=False):
    if peel:
        body(0)
    with engine.Fori(int(peel), count) as i:
        body(i)


def constants():
    quarter = HEAD_DIM // 4
    freqs = (np.float32(10000.0) ** (-np.arange(quarter, dtype=np.float32) / np.float32(quarter))).astype(np.float32)
    t = np.arange(LAT)
    rows = (t // GRID_W).astype(np.float32)[None, :] * freqs[:, None]
    cols = (t % GRID_W).astype(np.float32)[None, :] * freqs[:, None]
    ang = np.concatenate([rows, rows, cols, cols, rows, rows, cols, cols], 0).astype(np.float32)
    turn = np.zeros((P, P), np.float32)
    for base in range(0, P, 2 * quarter):
        for j in range(quarter):
            turn[base + quarter + j, base + j] = -1.0
            turn[base + j, base + quarter + j] = 1.0
    q = np.arange(P)[:, None]
    keys = np.arange(LAT)[None, :]
    mask = np.zeros((P, 2, PAST + LAT), np.float32)
    for b in range(2):
        mask[:, b, PAST:] = np.where(np.abs(q + b * P - keys) <= WINDOW, 0.0, NEG)
    inv = np.zeros((P, NG, T), np.float32)
    for g, w in enumerate(POOL_SIZES):
        for _, start, n in SEGS:
            s = np.arange(n)
            count = np.clip(s + (w - w // 2), 0, n) - np.clip(s - w // 2, 0, n)
            inv[:, g, start:start + n] = (np.float32(1.0) / count.astype(np.float32))[None, :]
    return {
        "c_cos": np.cos(ang).astype(np.float32), "c_sin": np.sin(ang).astype(np.float32), "c_turn": turn,
        "c_ident": np.eye(P, dtype=np.float32), "c_mask": mask, "c_inv": inv,
    }


def build(nc, io):
    ctx = ExitStack()
    with ctx:
        def sb(name, shape, dt=F32):
            return ctx.enter_context(nc.sbuf_tensor(name, shape, dt))

        def sem(name):
            return ctx.enter_context(nc.semaphore(name))

        x = sb("x", [P, KC, T])
        hf = sb("hf", [P, KC, T])
        h_hi = sb("h_hi", [P, KC, T], F32R)
        h_lo = sb("h_lo", [P, KC, T], F32R)
        raw = sb("raw", [P, RING, D])
        w_hi = sb("w_hi", [P, RING, D], F32R)
        w_lo = sb("w_lo", [P, RING, D], F32R)
        ga = sb("ga", [P, 4, T])
        g_hi = sb("g_hi", [P, 2, T], F32R)
        g_lo = sb("g_lo", [P, 2, T], F32R)
        oh2 = sb("oh2", [P, 2, TOK, P], BF16)
        oh1 = sb("oh1", [P, 2, 3, TOK, P], BF16)
        keys = sb("keys", [P, HS, N_KEYS])
        mod = sb("mod", [P, MOD_BLOCKS, 2])
        mod_b = sb("mod_b", [P, MOD_BLOCKS])
        gains = sb("gains", [P, 2 * DEPTH + 1, KC])
        scales = sb("scales", [P, 2 * DEPTH, KC, 2])
        cvec = sb("cvec", [P, KC, 2])
        sink = sb("sink", [P, N_HEADS])
        pool_scale = sb("pool_scale", [P, NG])
        b1 = sb("b1", [P, 2 * KC])
        dw = sb("dw", [P, KC, CONV_WIDTH])
        cvecs = sb("cvecs", [P, 4, KC])
        gb2 = sb("gb2", [P, KC, 2])
        turn = sb("turn", [P, P])
        ident = sb("ident", [P, P])
        ones = sb("ones", [P, P])
        iota_b = sb("iota_b", [P, P], BF16)
        iota16 = sb("iota16", [P, TOPK])
        stat = sb("stat", [P, 4, CONV_OUT])
        work = sb("work", [P, WORK])
        ps = ctx.enter_context(nc.psum_tensor("ps", [P, 8, 512], F32))
        PROJ = 0
        ACC = 2

        place = [0]

        def region(*shape, at=None):
            if at is not None:
                place[0] = at
            n = int(np.prod(shape))
            v = work[:, place[0]:place[0] + n]
            place[0] += n
            assert place[0] <= WORK, place[0]
            names = "abcd"[:len(shape)]
            return v if len(shape) == 1 else v.rearrange(
                f"p ({' '.join(names)}) -> p {' '.join(names)}", **dict(zip(names, shape)))

        cos = region(LAT, at=0)
        sin = region(LAT)
        mask = region(2, PAST + LAT)
        inv = region(NG, T)
        w_pool = region(NG, P)
        cache_k = region(PAST)
        cache_v = region(P)
        qk = region(5, T)
        turned = region(5, LAT)
        v_nat = region(NT, P)
        u_pad = region(NG, POOL_W)
        sum_a = region(NG, POOL_W)
        sum_b = region(NG, POOL_W)
        logits = region(2, CTX + 2 * (PAST + LAT))
        p_t = region(CTX + 2 * (PAST + LAT))
        sm = region(2, 5, 3)
        pooled = region(NG, T)
        a_pad = region(KC, CONV_IN, at=0)
        conv = region(KC, CONV_OUT)
        conv_sq = region(KC, CONV_OUT)
        glu = region(2, 2, T)
        stage = region(2, N_KEYS, CHUNK, at=0)
        s_all = region(NT, HS, N_KEYS, at=0)
        val = region(HS, TOPK)
        key_u = region(HS, TOPK)
        key_f = region(HS, TOPK)
        pos_u = region(3, P)
        pos_f = region(2, P)
        top = region(P)
        after_topk = place[0]
        sel = region(4, NT, P, at=max(after_topk, 2 * N_KEYS * CHUNK))
        gsum = region(2, NT * PEER_HEADS)
        col_key = region(2, T)
        col_g = region(3, T)
        col_b = region(T // 2).bitcast(BF16)
        cand = hf[:, :, :].rearrange("p k t -> p (k t)")[:, 0:PEER_HEADS * TOPK * TOPK].rearrange(
            "p (h a b) -> p h a b", h=PEER_HEADS, a=TOPK)
        a_in = region(4, T, at=0)
        g_in = region(2, NCHUNK, QUAD * CHUNK)
        wf = region(2, T)
        y_gated = region(KC, T)
        y_nat = hf[:, :, :].rearrange("p k t -> p (k t)").rearrange("p (n d) -> p n d", n=NT)

        small_loaded = sem("small_loaded")
        keys_loaded = sem("keys_loaded")
        mod_raw = [sem(f"mod_raw{j}") for j in range(RING)]
        raw_ready = [sem(f"raw_ready{j}") for j in range(RING)]
        consts_ready = sem("consts_ready")
        pads_ready = sem("pads_ready")
        iota_ready = sem("iota_ready")
        c_ready = sem("c_ready")
        mod_done = sem("mod_done")
        mod_taken = sem("mod_taken")
        hi_ready = sem("hi_ready")
        lo_ready = sem("lo_ready")
        block_done = sem("block_done")
        proj_taken = sem("proj_taken")
        sq_ready = sem("sq_ready")
        stat_ready = sem("stat_ready")
        var_ready = sem("var_ready")
        std_ready = sem("std_ready")
        xn_ready = sem("xn_ready")
        hi_part = sem("hi_part")
        operand_ready = sem("operand_ready")
        dve_order = sem("dve_order")
        act_order = sem("act_order")
        turn_done = sem("turn_done")
        roped = sem("roped")
        logits_done = sem("logits_done")
        max_ready = sem("max_ready")
        exp_ready = sem("exp_ready")
        logits_read = sem("logits_read")
        p_ready = sem("p_ready")
        pt_done = sem("pt_done")
        pt_copied = sem("pt_copied")
        att_done = sem("att_done")
        att_taken = sem("att_taken")
        pooled_ready = sem("pooled_ready")
        mixed_done = sem("mixed_done")
        state_out = sem("state_out")
        s_done = sem("s_done")
        s_taken = sem("s_taken")
        gelu_done = sem("gelu_done")
        a_stored = [sem(f"a_stored{j}") for j in range(4)]
        top_ready = sem("top_ready")
        exp_done = sem("exp_done")
        sel_ready = sem("sel_ready")
        cols_done = sem("cols_done")
        hot_ready = sem("hot_ready")
        g_done = sem("g_done")
        g_taken = sem("g_taken")
        g_stored = [sem(f"g_stored{j}") for j in range(2)]
        a_loaded = [sem(f"a_loaded{j}") for j in range(4)]
        g_loaded = [sem(f"g_loaded{j}") for j in range(2)]
        w_ready = sem("w_ready")
        whi_ready = sem("whi_ready")
        wlo_ready = sem("wlo_ready")
        y_copied = sem("y_copied")
        yt_done = sem("yt_done")
        yt_taken = sem("yt_taken")
        glu_in = sem("glu_in")
        glu_out = sem("glu_out")
        conv_ready = sem("conv_ready")
        mean_done = sem("mean_done")
        out_ready = sem("out_ready")
        out_stored = sem("out_stored")

        a_dram = nc.dram_tensor("a_dram", (N_KEYS, P, T), F32).ap()
        g_dram = nc.dram_tensor("g_dram", (NCHUNK, P, N_KEYS * CHUNK), F32).ap()
        g_quads = g_dram.rearrange("c p (q i t) -> p q c (i t)", i=QUAD, t=CHUNK)

        def one(ap, n):
            return ap[bass.ds(n, 1)].rearrange("a p n -> (a p) n")

        def mod_col(layer, part, k, group):
            return mod[:, (layer * 6 + part) * KC + k, group:group + 1]

        NORMS = [(l, w) for l in range(DEPTH) for w in range(2)]

        small = [
            (x[:, :, :], io["x"]), (cvec[:, :, :], io["c"]), (mod_b[:, :], io["mod_b"]),
            (gains[:, :, :], io["gains"]), (sink[:, :], io["sink"]), (pool_scale[:, :], io["pool_scale"]),
            (b1[:, :], io["b1"]), (dw[:, :, :], io["dw"]), (cvecs[:, :, :], io["cvecs"]),
            (turn[:, :], io["c_turn"]), (ident[:, :], io["c_ident"]), (cos, io["c_cos"]), (sin, io["c_sin"]),
            (mask, io["c_mask"]), (inv, io["c_inv"]), (w_pool, io["w_pool"]), (cache_k, io["cache_k"]),
            (cache_v, io["cache_v"]),
        ]

        block = ctx.enter_context(nc.Block())

        @block.sync
        def _(sp):
            for dst, src in small:
                sp.dma_start(dst, src).then_inc(small_loaded, 16)
            sp.dma_start(keys[:, :, :], io["keys"][0]).then_inc(keys_loaded, 16)

            for q in range(RING):
                sp.dma_start(raw[:, q, :], one(io["mod_w"], q)).then_inc(mod_raw[q], 16)
            with sp.Fori(0, MOD_BLOCKS // RING - 1) as i:
                for j in range(RING):
                    sp.wait_ge(mod_done, i * RING + j + 1)
                    sp.dma_start(raw[:, j, :], one(io["mod_w"], i * RING + RING + j)).then_inc(mod_raw[j], 16)

            def load(name, n, m_mod):
                sp.dma_start(raw[:, m_mod % RING, :], one(io[name], n)).then_inc(raw_ready[m_mod % RING], 16)

            for m in range(RING):
                sp.wait_ge(mod_done, MOD_BLOCKS - RING + m + 1)
                load("in", m, m)

            def stream(name, first, count, body):
                m0 = M0[name] + first
                if count == body:
                    for j in range(body):
                        sp.wait_ge(lo_ready, m0 + j - RING + 1)
                        load(name, first + j, m0 + j)
                    return
                with sp.Fori(0, count // body) as i:
                    for j in range(body):
                        sp.wait_ge(lo_ready, i * body + (m0 + j - RING + 1))
                        load(name, i * body + (first + j), m0 + j)

            stream("in", RING, 10 - RING, 10 - RING)
            stream("out", 0, 8, 4)
            for layer in range(DEPTH):
                stream(f"wq{layer}", 0, HS, 4)
                stream(f"u{layer}", 0, N_KEYS, 4)
                name, v0 = f"v{layer}", M0[f"v{layer}"]
                after = ["w1", None][layer]
                stream(name, 0, RING, RING)
                for j in range(4):
                    sp.wait_ge(a_stored[j], 16 * (layer + 1) * (N_KEYS // 4))
                for s in range(2):
                    sp.wait_ge(g_stored[s], 16 * (layer + 1) * (NCHUNK // 2))
                for j in range(4):
                    sp.dma_start(a_in[:, j, :], one(a_dram, j)).then_inc(a_loaded[j], 16)
                for s in range(2):
                    sp.dma_start(g_in[:, s], g_quads[:, s]).then_inc(g_loaded[s], 16)
                if layer == 0:
                    sp.wait_ge(s_done, HS)
                    sp.dma_start(keys[:, :, :], io["keys"][1]).then_inc(keys_loaded, 16)

                def beside(i, j, more):
                    sp.wait_ge(lo_ready, i * 8 + (v0 + j + 1))
                    if more or j < 8 - RING:
                        load(name, i * 8 + (j + RING), v0 + j)
                    elif after:
                        load(after, j - (8 - RING), v0 + j)
                    if more or j < 4:
                        sp.wait_ge(w_ready, i * 8 + (layer * N_KEYS + j + 1))
                        sp.dma_start(a_in[:, j % 4, :], one(a_dram, i * 8 + (j + 4))).then_inc(a_loaded[j % 4], 16)
                    if more and j % 4 == 3:
                        s = j // 4
                        sp.dma_start(g_in[:, s].unsqueeze(1),
                                     g_quads[:, bass.ds(i * 2 + (s + 2), 1)]).then_inc(g_loaded[s], 16)

                with sp.Fori(0, N_KEYS // 8 - 1) as i:
                    for j in range(8):
                        beside(i, j, True)
                for j in range(8):
                    if j < 8 - RING or after:
                        beside(N_KEYS // 8 - 1, j, False)
                if layer == 0:
                    stream("w1", RING, 16 - RING, 4)
                    stream("w2", 0, 8, 4)

            sp.wait_ge(out_ready, 1)
            sp.dma_start(io["y"], hf[:, :, :]).then_inc(out_stored, 16)
            sp.wait_ge(out_stored, 16)
            sp.wait_ge(state_out, 32)

        @block.gpsimd
        def _(pool):
            nc.gpsimd.iota(iota_b[:, :], pattern=[[1, P]], base=0, channel_multiplier=0,
                           allow_small_or_imprecise_dtypes=True).then_inc(iota_ready, 1)
            nc.gpsimd.iota(iota16[:, :], pattern=[[1, TOPK]], base=0, channel_multiplier=0,
                           allow_small_or_imprecise_dtypes=True).then_inc(iota_ready, 1)

            def low(m, j):
                pool.wait_ge(hi_ready, m + 1)
                nc.gpsimd.tensor_tensor(w_lo[:, j % RING, :], raw[:, j % RING, :],
                                        w_hi[:, j % RING, :].bitcast(F32), ALU.subtract).then_inc(lo_ready, 1)

            with pool.Fori(0, BLOCKS // 8) as i:
                for j in range(8):
                    low(i * 8 + j, j)
            for m in range(BLOCKS // 8 * 8, BLOCKS):
                low(m, m)

        @block.scalar
        def _(act):
            order = [0]

            def settle(ins):
                order[0] += 1
                ins.then_inc(act_order, 1)
                act.wait_ge(act_order, order[0])

            def high(i, step, m, wait_free=True):
                count = i * (16 * step // RING) + 16 * (m // RING + 1)
                act.wait_ge(raw_ready[m % RING], count)
                if wait_free:
                    act.wait_ge(block_done, i * step + (m - RING + 1))
                nc.scalar.activation(w_hi[:, m % RING, :], raw[:, m % RING, :], ACT.Copy).then_inc(hi_ready, 1)

            def ahead(i, step, m):
                if m + LEAD < BLOCKS:
                    high(i, step, m + LEAD, wait_free=m + LEAD >= RING)

            def projected(i, step, m):
                act.wait_ge(block_done, i * step + (m + 1))

            def by_group(out_of, in_of, scale_of, bias_of=None):
                for g, start, n in SEGS:
                    last = nc.scalar.activation(out_of(start, n), in_of(start, n), ACT.Identity,
                                                scale=scale_of(g), bias=bias_of(g) if bias_of else 0.0)
                return last

            act.wait_ge(small_loaded, 16 * len(small))
            nc.scalar.activation(cvec[:, :, :], cvec[:, :, :], ACT.Silu).then_inc(c_ready, 1)
            for m in range(LEAD):
                high(0, 0, m, wait_free=False)

            roots = [0]

            def normalise(n):
                roots[0] += 1
                act.wait_ge(var_ready, roots[0])
                nc.scalar.activation(stat[:, 1, 0:T], stat[:, 0, 0:T], ACT.Sqrt).then_inc(std_ready, 1)
                act.wait_ge(xn_ready, n + 1)
                if n == 2 * DEPTH:
                    for k in range(KC):
                        last = nc.scalar.activation(hf[:, k, :], hf[:, k, :], ACT.Identity,
                                                    scale=gains[:, n, k:k + 1])
                    last.then_inc(out_ready, 1)
                    return
                layer, which = NORMS[n]
                for k in range(KC):
                    last = by_group(lambda s, c: hf[:, k, s:s + c], lambda s, c: hf[:, k, s:s + c],
                                    lambda g: scales[:, n, k, g:g + 1],
                                    lambda g: mod_col(layer, 3 * which, k, g))
                settle(last)

            def high_operand():
                nc.scalar.activation(h_hi[:, :, :], hf[:, :, :], ACT.Copy).then_inc(hi_part, 1)

            def gated(name, layer, part):
                m0 = M0[name]
                with act.Fori(0, 2) as i:
                    for j in range(4):
                        ahead(i, 4, m0 + j)
                        projected(i, 4, m0 + j)
                        for g, start, n in SEGS:
                            k = i * 4 + j
                            col = bass.ds(i * 4 + ((layer * 6 + part) * KC + j), 1)
                            bias = gb2[:, bass.ds(k, 1), g:g + 1].rearrange("p a b -> p (a b)") if name == "w2" else 0.0
                            last = nc.scalar.activation(
                                hf[:, bass.ds(k, 1), start:start + n],
                                ps[:, PROJ + (R0[name] + j) % 2, start:start + n].unsqueeze(1), ACT.Identity,
                                scale=mod[:, col, g:g + 1].rearrange("p a b -> p (a b)"), bias=bias)
                        last.then_inc(proj_taken, 1)

            def attention():
                for c in range(10):
                    ahead(0, 0, M0["in"] + c)
                    if c == 0:
                        act.wait_ge(pads_ready, 1)
                    projected(0, 0, M0["in"] + c)
                    src = ps[:, PROJ + (R0["in"] + c) % 2, :]
                    if c < 5:
                        last = nc.scalar.activation(qk[:, c, :], src[:, 0:T], ACT.Copy)
                    elif c < 9:
                        for g, start, n in SEGS:
                            at = PAD * (g + 1) + start
                            last = nc.scalar.activation(u_pad[:, c - 5, at:at + n], src[:, start:start + n], ACT.Copy)
                    else:
                        last = nc.scalar.activation(v_nat.rearrange("p n d -> p (n d)"), src[:, 0:T], ACT.Copy)
                    last.then_inc(proj_taken, 1)
                act.wait_ge(proj_taken, R0["in"] + 10)
                act.dma_start(io["state_k"], qk[:, 4, 0:CTX]).then_inc(state_out, 16)
                act.dma_start(io["state_v"], v_nat[:, 0, :]).then_inc(state_out, 16)

                def transposed(n):
                    act.wait_ge(pt_done, n + 1)
                    if n >= 1:
                        act.wait_ge(att_done, n)
                    nc.scalar.activation(p_t, ps[:, 6:8, :].rearrange("p a b -> p (a b)")[:, 0:CTX + 2 * T],
                                         ACT.Copy).then_inc(pt_copied, 1)

                def pair(c):
                    act.wait_ge(att_done, 2 * c + 2)
                    nc.scalar.activation(hf[:, c, :], ps[:, PROJ + c % 2, 0:T], ACT.Copy).then_inc(att_taken, 1)

                for n in range(N_HEADS):
                    b = n % 2
                    head = n // 2 + PAIRS * (n % 2)
                    act.wait_ge(max_ready, n + 1)
                    start = 0
                    for piece, width in enumerate((CTX, T, T)):
                        part = logits[:, b, start:start + width]
                        nc.scalar.activation(part, part, ACT.Exp, bias=sm[:, b, 1, piece:piece + 1],
                                             accum_out=sm[:, b, 2, piece:piece + 1])
                        start += width
                    nc.scalar.activation(sm[:, b, 3, :], sm[:, b, 1, :], ACT.Exp,
                                         bias=sink[:, head:head + 1]).then_inc(exp_ready, 1)
                    if n >= 1:
                        transposed(n - 1)
                        if n % 2 == 0:
                            pair(n // 2 - 1)
                transposed(N_HEADS - 1)
                pair(PAIRS - 1)
                for g in range(NG):
                    act.wait_ge(mixed_done, g + 1)
                    last = nc.scalar.activation(hf[:, PAIRS + g, :], ps[:, ACC + g, 0:T], ACT.Identity,
                                                scale=pool_scale[:, g:g + 1])
                settle(last)
                high_operand()
                gated("out", 0, 2)

            def convolution():
                def gates(i):
                    for j in range(4):
                        ahead(i, 4, M0["w1"] + j)
                        projected(i, 4, M0["w1"] + j)
                        src = ps[:, PROJ + (R0["w1"] + j) % 2, 0:T]
                        s = j // 2
                        if j % 2 == 0:
                            since(act, glu_out, i * 2)
                            nc.scalar.activation(glu[:, s, 0, :], src, ACT.Sigmoid,
                                                 bias=b1[:, bass.ds(i * 2 + (KC + s), 1)]).then_inc(proj_taken, 1)
                        else:
                            nc.scalar.activation(glu[:, s, 1, :], src, ACT.Identity,
                                                 bias=b1[:, bass.ds(i * 2 + s, 1)]).then_inc(proj_taken, 1)

                rounds(act, 4, gates, peel=True)
                roots[0] += 1
                act.wait_ge(var_ready, roots[0])
                nc.scalar.activation(stat[:, 1, :], stat[:, 0, :], ACT.Sqrt).then_inc(std_ready, 1)
                act.wait_ge(conv_ready, 3)
                for k in range(KC):
                    for g, start, n in SEGS:
                        at = start + g * CPAD
                        last = nc.scalar.activation(hf[:, k, start:start + n], conv[:, k, at:at + n], ACT.Silu,
                                                    scale=cvecs[:, 1, k:k + 1], bias=cvecs[:, 2, k:k + 1])
                settle(last)
                high_operand()
                gated("w2", 1, 2)

            def scores(layer):
                m0, r0 = M0[f"wq{layer}"], R0[f"wq{layer}"]
                for j in range(4 if layer else 0):
                    act.wait_ge(a_stored[j], 16 * (N_KEYS // 4))
                if layer == 0:
                    act.wait_ge(state_out, 32)
                def queries(i):
                    def query(j):
                        ahead(i, 4, m0 + j)
                        projected(i, 4, m0 + j)
                        if j == 0:
                            since(act, s_done, i * 4 + layer * HS)
                        nc.scalar.activation(ga[:, j, :], ps[:, PROJ + (r0 + j) % 2, 0:T],
                                             ACT.Copy).then_inc(proj_taken, 1)

                    def take(j):
                        act.wait_ge(s_done, i * 4 + (layer * HS + j + 1))
                        nc.scalar.activation(
                            s_all[:, :, bass.ds(i * 4 + j, 1), :].rearrange("p n a k -> p n (a k)"),
                            ps[:, ACC + j, 0:T].rearrange("p (n k) -> p n k", n=NT), ACT.Copy).then_inc(s_taken, 1)

                    query(0)
                    query(1)
                    take(0)
                    query(2)
                    take(1)
                    query(3)
                    take(2)
                    take(3)

                rounds(act, HS // 4, queries, peel=layer == 0)

            def gelu(layer, i, step, m, r, count):
                j = count % 4
                projected(i, step, m)
                since(act, a_stored[j], i * (4 * step) + 16 * (layer * N_KEYS // 4 + count // 4))
                nc.scalar.activation(ga[:, j, :], ps[:, PROJ + r % 2, 0:T], ACT.Gelu).then_inc(proj_taken, 1)
                act.wait_ge(proj_taken, i * step + (r + 1))
                act.dma_start(one(a_dram, i * step + count), ga[:, j, :]).then_inc(a_stored[j], 16)

            def experts(layer):
                m0, r0 = M0[f"u{layer}"], R0[f"u{layer}"]
                def plain(i, first=0):
                    for j in range(first, first + 4):
                        ahead(i, 4, m0 + j)
                        gelu(layer, i, 4, m0 + j, r0 + j, j)

                rounds(act, EXP_AT // 4, plain, peel=layer == 0)
                act.wait_ge(top_ready, layer + 1)
                nc.scalar.activation(sel[:, 3], sel[:, 0], ACT.Exp).then_inc(exp_done, 1)
                rounds(act, (UBLOCKS - EXP_AT) // 4, lambda i: plain(i, EXP_AT))

                def with_table(i):
                    for j in range(8):
                        b = UBLOCKS + j
                        ahead(i, 8, m0 + b)
                        gelu(layer, i, 8, m0 + b, r0 + b, b)
                        s = j // 4
                        if j % 4 == 0:
                            since(act, g_stored[s], i * 16 + layer * 16 * (NCHUNK // 2))
                        act.wait_ge(g_done, i * 8 + (layer * GBLOCKS + j + 1))
                        for half in range(2):
                            tok = (j % 4) * TOK + half * (TOK // 2)
                            last = nc.scalar.activation(
                                stage[:, s, :, tok:tok + TOK // 2].rearrange("p k t -> p t k"),
                                ps[:, ACC + 2 * (j % 2) + half, :].rearrange("p (t k) -> p t k", k=N_KEYS), ACT.Copy)
                        last.then_inc(g_taken, 1)
                        if j % 4 == 3:
                            act.wait_ge(g_taken, i * 8 + (layer * GBLOCKS + j + 1))
                            act.dma_start(one(g_dram, i * 2 + s),
                                          stage[:, s].rearrange("p k t -> p (k t)")).then_inc(g_stored[s], 16)

                rounds(act, GBLOCKS // 8, with_table, peel=layer == 0)

                v0 = M0[f"v{layer}"]

                def sweep(i, j, more=True):
                    act.wait_ge(block_done, i * 8 + (v0 + j - 1))
                    act.wait_ge(w_ready, i * 8 + (layer * N_KEYS + j + 1))
                    nc.scalar.activation(g_hi[:, j % 2, :], wf[:, j % 2, :], ACT.Copy).then_inc(whi_ready, 1)
                    if more:
                        high(i, 8, v0 + j + LEAD)

                with act.Fori(0, N_KEYS // 8 - 1) as i:
                    for j in range(8):
                        sweep(i, j)
                for j in range(8):
                    sweep(N_KEYS // 8 - 1, j, more=layer == 0 or j + LEAD < 8)
                act.wait_ge(block_done, v0 + N_KEYS)
                for t in range(NT):
                    last = nc.scalar.activation(y_nat[:, t, :], ps[:, ACC + 2 * t:ACC + 2 * t + 2, :].rearrange(
                        "p a b -> p (a b)"), ACT.Copy)
                last.then_inc(y_copied, 1)
                for k in range(KC):
                    act.wait_ge(yt_done, layer * KC + k + 1)
                    last = by_group(lambda s, c: y_gated[:, k, s:s + c], lambda s, c: ps[:, PROJ + k % 2, s:s + c],
                                    lambda g: mod_col(layer, 5, k, g))
                    last.then_inc(yt_taken, 1)

            for layer in range(DEPTH):
                normalise(2 * layer)
                high_operand()
                [attention, convolution][layer]()
                normalise(2 * layer + 1)
                high_operand()
                scores(layer)
                experts(layer)
            normalise(2 * DEPTH)

        @block.vector
        def _(dve):
            order = [0]

            def settle(ins):
                order[0] += 1
                ins.then_inc(dve_order, 1)
                dve.wait_ge(dve_order, order[0])

            tt = nc.vector.tensor_tensor
            ts = nc.vector.tensor_scalar
            stt = nc.vector.scalar_tensor_tensor

            def broad(ap, shape, *axes):
                for a in axes:
                    ap = ap.unsqueeze(a)
                return ap.broadcast_to(shape)

            nc.vector.memset(ones[:, :], 1.0).then_inc(consts_ready, 1)
            nc.vector.memset(u_pad, 0.0).then_inc(pads_ready, 1)
            dve.wait_ge(small_loaded, 16 * len(small))

            def mod_sum(i, half):
                q = i * 8 + 4 * half
                dve.wait_ge(mod_done, q + 4)
                tt(mod[:, bass.ds(q, 4), :], ps[:, ACC + half, 0:8].rearrange("p (a b) -> p a b", b=2),
                   broad(mod_b[:, bass.ds(q, 4)], [P, 4, 2], 2), ALU.add).then_inc(mod_taken, 1)

            with dve.Fori(0, MOD_BLOCKS // 8) as i:
                for half in range(2):
                    mod_sum(i, half)
            dve.wait_ge(mod_taken, MOD_BLOCKS // 4)
            for n, (layer, which) in enumerate(NORMS):
                at = (layer * 6 + 3 * which + 1) * KC
                last = stt(scales[:, n], mod[:, at:at + KC, :], 1.0, broad(gains[:, n, :], [P, KC, 2], 2),
                           ALU.add, ALU.mult)
            at = (6 + 2) * KC
            settle(tt(gb2[:, :, :], mod[:, at:at + KC, :], broad(cvecs[:, 3, :], [P, KC, 2], 2), ALU.mult))

            def inverse_root(n, width):
                v, r, t = (stat[:, s, 0:width] for s in (0, 2, 3))
                dve.wait_ge(std_ready, n + 1)
                settle(nc.vector.reciprocal(r, stat[:, 1, 0:width]))
                settle(tt(t, r, r, ALU.mult))
                settle(tt(t, t, v, ALU.mult))
                settle(ts(t, t, -0.5, 1.5, ALU.mult, ALU.add))
                settle(tt(r, r, t, ALU.mult))

            roots = [0]

            def normalise(n):
                tt(hf[:, :, :], x[:, :, :], x[:, :, :], ALU.mult).then_inc(sq_ready, 1)
                dve.wait_ge(stat_ready, n + 1)
                ts(stat[:, 0, 0:T], ps[:, ACC, 0:T], 1.0 / D, EPS, ALU.mult, ALU.add).then_inc(var_ready, 1)
                inverse_root(roots[0], T)
                roots[0] += 1
                tt(hf[:, :, :], x[:, :, :], broad(stat[:, 2, 0:T], [P, KC, T], 1), ALU.mult).then_inc(xn_ready, 1)

            parts = [0]

            def low_operand():
                parts[0] += 1
                dve.wait_ge(hi_part, parts[0])
                tt(h_lo[:, :, :], hf[:, :, :], h_hi[:, :, :].bitcast(F32), ALU.subtract).then_inc(operand_ready, 1)

            def residual(name):
                for k in range(KC):
                    dve.wait_ge(proj_taken, R0[name] + k + 1)
                    last = tt(x[:, k, :], x[:, k, :], hf[:, k, :], ALU.add)
                settle(last)

            def attention():
                dve.wait_ge(turn_done, 1)
                rot = ps[:, ACC:ACC + 3, :].rearrange("p a b -> p (a b)")[:, 0:5 * LAT].rearrange(
                    "p (c t) -> p c t", c=5)
                tt(turned, rot, broad(sin, [P, 5, LAT], 1), ALU.mult)
                settle(tt(qk[:, :, CTX:T], qk[:, :, CTX:T], broad(cos, [P, 5, LAT], 1), ALU.mult))
                tt(qk[:, :, CTX:T], qk[:, :, CTX:T], turned, ALU.add).then_inc(roped, 1)

                dve.wait_ge(proj_taken, R0["in"] + 9)
                src, dst = u_pad, sum_a
                lo = 0
                for g, w in enumerate(POOL_SIZES):
                    half = w // 2
                    back, fore = (1, 0) if w == 2 else (half // 2, half // 2)
                    settle(tt(dst[:, g:NG, half:POOL_W - half + 1], src[:, g:NG, half - back:POOL_W - half + 1 - back],
                              src[:, g:NG, half + fore:POOL_W - half + 1 + fore], ALU.add))
                    for s, start, n in SEGS:
                        at = PAD * (s + 1) + start
                        settle(tt(pooled[:, g, start:start + n], dst[:, g, at:at + n], inv[:, g, start:start + n], ALU.mult))
                        last = tt(pooled[:, g, start:start + n], pooled[:, g, start:start + n],
                                  u_pad[:, g, at:at + n], ALU.subtract)
                    last.then_inc(pooled_ready, 1)
                    src, dst = dst, (sum_b if dst is sum_a else sum_a)

                def front(n):
                    b = n % 2
                    head = n // 2 + PAIRS * (n % 2)
                    dve.wait_ge(logits_done, n + 1)
                    if n >= 2:
                        dve.wait_ge(pt_done, n - 1)
                    bank = ACC + 2 * b
                    ts(logits[:, b, 0:CTX], ps[:, bank, 0:CTX], SCALE, None, ALU.mult)
                    stt(logits[:, b, CTX:CTX + T], ps[:, bank, CTX:CTX + T], SCALE, mask[:, 0, :], ALU.mult, ALU.add)
                    stt(logits[:, b, CTX + T:CTX + 2 * T], ps[:, bank + 1, 0:T], SCALE, mask[:, 1, :],
                        ALU.mult, ALU.add).then_inc(logits_read, 1)
                    dve.wait_ge(logits_read, n + 1)
                    nc.vector.tensor_reduce(sm[:, b, 0, 0:1], logits[:, b, 0:CTX], AX.X, ALU.max)
                    settle(nc.vector.tensor_reduce(sm[:, b, 0, 1:3], logits[:, b, CTX:].rearrange(
                        "p (a k) -> p a k", a=2), AX.X, ALU.max))
                    settle(ts(sm[:, b, 1, :], sm[:, b, 0, :], sink[:, head:head + 1], None, ALU.max))
                    ts(sm[:, b, 1, :], sm[:, b, 1, :], -1.0, None, ALU.mult).then_inc(max_ready, 1)

                def back(n):
                    b = n % 2
                    dve.wait_ge(exp_ready, n + 1)
                    settle(tt(sm[:, b, 4, :], sm[:, b, 2, :], sm[:, b, 3, :], ALU.add))
                    settle(nc.vector.reciprocal(sm[:, b, 4, :], sm[:, b, 4, :]))
                    start = 0
                    for piece, width in enumerate((CTX, T, T)):
                        part = logits[:, b, start:start + width]
                        last = ts(part, part, sm[:, b, 4, piece:piece + 1], None, ALU.mult)
                        start += width
                    last.then_inc(p_ready, 1)

                front(0)
                for n in range(1, N_HEADS):
                    front(n)
                    back(n - 1)
                back(N_HEADS - 1)
                low_operand()
                residual("out")

            def convolution():
                settle(nc.vector.memset(a_pad, 0.0))
                with dve.Fori(0, 4) as i:
                    for s in range(2):
                        dve.wait_ge(proj_taken, i * 4 + (R0["w1"] + 2 * s + 2))
                        for g, start, n in SEGS:
                            at = CPAD * (g + 1) + start
                            last = tt(a_pad[:, bass.ds(i * 2 + s, 1), at:at + n],
                                      glu[:, s, 0:1, start:start + n], glu[:, s, 1:2, start:start + n], ALU.mult)
                        last.then_inc(glu_out, 1)
                dve.wait_ge(glu_out, KC)
                for k in range(KC):
                    last = ts(conv[:, k, :], a_pad[:, k, 0:CONV_OUT], dw[:, k, 0:1], cvecs[:, 0, k:k + 1],
                              ALU.mult, ALU.add)
                settle(last)
                for j in range(1, CONV_WIDTH):
                    for k in range(KC):
                        last = stt(conv[:, k, :], a_pad[:, k, j:j + CONV_OUT], dw[:, k, j:j + 1], conv[:, k, :],
                                   ALU.mult, ALU.add)
                    if j < CONV_WIDTH - 1:
                        settle(last)
                last.then_inc(conv_ready, 1)
                dve.wait_ge(mean_done, 1)
                settle(ts(stat[:, 0, :], ps[:, ACC, 0:CONV_OUT], 1.0 / D, None, ALU.mult))
                settle(tt(conv, conv, broad(stat[:, 0, :], [P, KC, CONV_OUT], 1), ALU.subtract))
                tt(conv_sq, conv, conv, ALU.mult).then_inc(conv_ready, 1)
                dve.wait_ge(mean_done, 2)
                ts(stat[:, 0, :], ps[:, ACC + 1, 0:CONV_OUT], 1.0 / D, EPS, ALU.mult, ALU.add).then_inc(var_ready, 1)
                inverse_root(roots[0], CONV_OUT)
                roots[0] += 1
                tt(conv, conv, broad(stat[:, 2, :], [P, KC, CONV_OUT], 1), ALU.mult).then_inc(conv_ready, 1)
                low_operand()
                residual("w2")

            def top_keys(layer):
                dve.wait_ge(iota_ready, 2)
                dve.wait_ge(s_taken, (layer + 1) * HS)
                for t in range(NT):
                    s = s_all[:, t]
                    for c in range(HS):
                        last = nc.vector.max(val[:, c, 0:8], s[:, c, :])
                    settle(last)
                    for c in range(HS):
                        last = nc.vector.max_index(key_u[:, c, 0:8].bitcast(U32), val[:, c, 0:8], s[:, c, :])
                    settle(last)
                    for c in range(HS):
                        last = nc.vector.match_replace(s[:, c, :], val[:, c, 0:8], s[:, c, :], LOWEST)
                    settle(last)
                    for c in range(HS):
                        last = nc.vector.max(val[:, c, 8:16], s[:, c, :])
                    settle(last)
                    for c in range(HS):
                        last = nc.vector.max_index(key_u[:, c, 8:16].bitcast(U32), val[:, c, 8:16], s[:, c, :])
                    settle(last)
                    nc.vector.tensor_copy(key_f, key_u.bitcast(U32))
                    pairs = val.rearrange("p (h s) k -> p h s k", s=2)
                    shape = [P, PEER_HEADS, TOPK, TOPK]
                    settle(tt(cand, broad(pairs[:, :, 0, :], shape, 3), broad(pairs[:, :, 1, :], shape, 2), ALU.add))
                    pos = pos_u.bitcast(U32)
                    flat = cand.rearrange("p h a b -> p h (a b)")
                    for h in range(PEER_HEADS):
                        last = nc.vector.max(top[:, h * TOPK:h * TOPK + 8], flat[:, h, :])
                    settle(last)
                    for h in range(PEER_HEADS):
                        last = nc.vector.max_index(pos[:, 0, h * TOPK:h * TOPK + 8], top[:, h * TOPK:h * TOPK + 8],
                                                   flat[:, h, :])
                    settle(last)
                    for h in range(PEER_HEADS):
                        last = nc.vector.match_replace(flat[:, h, :], top[:, h * TOPK:h * TOPK + 8], flat[:, h, :], LOWEST)
                    settle(last)
                    for h in range(PEER_HEADS):
                        last = nc.vector.max(top[:, h * TOPK + 8:(h + 1) * TOPK], flat[:, h, :])
                    settle(last)
                    for h in range(PEER_HEADS):
                        last = nc.vector.max_index(pos[:, 0, h * TOPK + 8:(h + 1) * TOPK],
                                                   top[:, h * TOPK + 8:(h + 1) * TOPK], flat[:, h, :])
                    settle(last)
                    ts(pos[:, 1, :], pos[:, 0, :], 4, None, ALU.logical_shift_right)
                    settle(ts(pos[:, 2, :], pos[:, 0, :], TOPK - 1, None, ALU.bitwise_and))
                    settle(nc.vector.tensor_copy(pos_f, pos[:, 1:3, :]))
                    keys_of = key_f.rearrange("p (h s) k -> p h s k", s=2)
                    hot = cand
                    for side in range(2):
                        rank = pos_f[:, side, :].rearrange("p (h k) -> p h k", h=PEER_HEADS)
                        iota = iota16[:, :].unsqueeze(1).unsqueeze(1).broadcast_to(shape)
                        settle(tt(hot, broad(rank, shape, 3), iota, ALU.is_equal))
                        settle(tt(hot, hot, broad(keys_of[:, :, side, :], shape, 2), ALU.mult))
                        settle(nc.vector.tensor_reduce(sel[:, 1 + side, t, :].rearrange("p (h k) -> p h k", h=PEER_HEADS),
                                                       hot, AX.X, ALU.add))
                    best = top.rearrange("p (h k) -> p h k", h=PEER_HEADS)
                    last = tt(sel[:, 0, t, :].rearrange("p (h k) -> p h k", h=PEER_HEADS), best,
                              best[:, :, 0:1].broadcast_to([P, PEER_HEADS, TOPK]), ALU.subtract)
                    if t < NT - 1:
                        settle(last)
                last.then_inc(top_ready, 1)
                dve.wait_ge(exp_done, layer + 1)
                e = sel[:, 3].rearrange("p n (h k) -> p (n h) k", k=TOPK)
                settle(nc.vector.tensor_reduce(gsum[:, 0, :], e, AX.X, ALU.add))
                settle(nc.vector.reciprocal(gsum[:, 1, :], gsum[:, 0, :]))
                tt(e, e, broad(gsum[:, 1, :], [P, NT * PEER_HEADS, TOPK], 2), ALU.mult).then_inc(sel_ready, 1)
                dve.wait_ge(cols_done, layer + 1)
                for s in range(2):
                    nc.vector.tensor_copy(col_key[:, s, :], ps[:, ACC + s, 0:T])
                g = ps[:, ACC + 2, 0:T]
                settle(nc.vector.tensor_copy(col_b, g))
                settle(nc.vector.tensor_copy(col_g[:, 0, :], col_b))
                settle(tt(col_g[:, 2, :], g, col_g[:, 0, :], ALU.subtract))
                settle(nc.vector.tensor_copy(col_b, col_g[:, 2, :]))
                settle(nc.vector.tensor_copy(col_g[:, 1, :], col_b))
                settle(tt(col_g[:, 2, :], col_g[:, 2, :], col_g[:, 1, :], ALU.subtract))

            def one_hots(layer):
                base = layer * GBLOCKS

                def table_rows(i):
                    for j in range(8):
                        b = j % 2
                        since(dve, g_done, i * 8 + (base + j - 1))
                        for q in range(TOK):
                            tok = bass.ds(i * (8 * TOK) + (j * TOK + q), 1)
                            ts(oh2[:, b, q, :], iota_b[:, :], col_key[:, 1, tok], None, ALU.is_equal)
                            for part in range(3):
                                last = ts(oh1[:, b, part, q, :], iota_b[:, :], col_key[:, 0, tok],
                                          col_g[:, part, tok], ALU.is_equal, ALU.mult)
                        last.then_inc(hot_ready, 1)

                rounds(dve, GBLOCKS // 8, table_rows, peel=layer == 0)

            def sweep(layer):
                base = layer * N_KEYS
                with dve.Fori(0, N_KEYS // 8) as i:
                    for j in range(8):
                        dve.wait_ge(a_loaded[j % 4], i * 32 + (16 * (base // 4 + j // 4 + 1)))
                        if j % 4 == 0:
                            dve.wait_ge(g_loaded[j // 4], i * 16 + 16 * (base // 8 + 1))
                        tt(wf[:, j % 2, :].rearrange("p (c t) -> p c t", t=CHUNK),
                           a_in[:, j % 4, :].rearrange("p (c t) -> p c t", t=CHUNK),
                           g_in[:, j // 4, :, (j % 4) * CHUNK:(j % 4 + 1) * CHUNK], ALU.mult).then_inc(w_ready, 1)
                        dve.wait_ge(whi_ready, i * 8 + (base + j + 1))
                        tt(g_lo[:, j % 2, :], wf[:, j % 2, :], g_hi[:, j % 2, :].bitcast(F32),
                           ALU.subtract).then_inc(wlo_ready, 1)
                for k in range(KC):
                    dve.wait_ge(yt_taken, layer * KC + k + 1)
                    last = tt(x[:, k, :], x[:, k, :], y_gated[:, k, :], ALU.add)
                settle(last)

            for layer in range(DEPTH):
                normalise(2 * layer)
                low_operand()
                [attention, convolution][layer]()
                normalise(2 * layer + 1)
                low_operand()
                top_keys(layer)
                one_hots(layer)
                sweep(layer)
            normalise(2 * DEPTH)

        @block.tensor
        def _(pe):
            mm = nc.tensor.matmul
            pe.wait_ge(c_ready, 1)
            pe.wait_ge(small_loaded, 16 * len(small))
            pe.wait_ge(consts_ready, 1)

            def modulation(i):
                for j in range(8):
                    pe.wait_ge(mod_raw[j % RING], i * 32 + 16 * (j // RING + 1))
                    if j % 4 == 0:
                        since(pe, mod_taken, i * 2)
                    for k in range(KC):
                        last = mm(ps[:, ACC + j // 4, 2 * (j % 4):2 * (j % 4) + 2], raw[:, j % RING, k * P:(k + 1) * P],
                                  cvec[:, k, :], start=k == 0, stop=k == KC - 1)
                    last.then_inc(mod_done, 1)

            rounds(pe, MOD_BLOCKS // 8, modulation, peel=True)

            operands = [0]

            def operand():
                operands[0] += 1
                pe.wait_ge(operand_ready, operands[0])

            def project(i, step, m, r):
                pe.wait_ge(lo_ready, i * step + (m + 1))
                if r >= 2:
                    pe.wait_ge(proj_taken, i * step + (r - 1))
                out, s = ps[:, PROJ + r % 2, 0:T], m % RING
                for k in range(KC):
                    cols = slice(k * P, (k + 1) * P)
                    mm(out, w_hi[:, s, cols], h_hi[:, k, :], start=k == 0, stop=False)
                    mm(out, w_hi[:, s, cols], h_lo[:, k, :], start=False, stop=False)
                    last = mm(out, w_lo[:, s, cols], h_hi[:, k, :], start=False, stop=k == KC - 1)
                last.then_inc(block_done, 1)

            def column_sums(n):
                pe.wait_ge(sq_ready, n + 1)
                for k in range(KC):
                    last = mm(ps[:, ACC, 0:T], ones[:, :], hf[:, k, :], start=k == 0, stop=k == KC - 1)
                last.then_inc(stat_ready, 1)

            def attention():
                for c in range(9):
                    project(0, 0, M0["in"] + c, R0["in"] + c)
                m, r = M0["in"] + 9, R0["in"] + 9
                pe.wait_ge(lo_ready, m + 1)
                pe.wait_ge(proj_taken, r - 1)
                for t in range(NT):
                    out = ps[:, PROJ + r % 2, t * P:(t + 1) * P]
                    rows = slice(t * P, (t + 1) * P)
                    for k in range(KC):
                        cols = slice(k * P, (k + 1) * P)
                        mm(out, h_hi[:, k, rows], w_hi[:, m % RING, cols], start=k == 0, stop=False)
                        mm(out, h_hi[:, k, rows], w_lo[:, m % RING, cols], start=False, stop=False)
                        last = mm(out, h_lo[:, k, rows], w_hi[:, m % RING, cols], start=False, stop=k == KC - 1)
                last.then_inc(block_done, 1)
                pe.wait_ge(proj_taken, R0["in"] + 5)
                for c in range(5):
                    last = mm(ps[:, ACC + c // 2, (c % 2) * LAT:(c % 2 + 1) * LAT], turn[:, :], qk[:, c, CTX:T],
                              start=True, stop=True)
                last.then_inc(turn_done, 1)
                pe.wait_ge(proj_taken, R0["in"] + 10)
                pe.wait_ge(roped, 1)

                def scores_of(n):
                    c, kv = n // 2, n % 2
                    rows = slice(HEAD_DIM * kv, HEAD_DIM * (kv + 1))
                    if n >= 2:
                        pe.wait_ge(logits_read, n - 1)
                    bank = ACC + 2 * (n % 2)
                    mm(ps[:, bank, 0:CTX], qk[rows, c, 0:CTX], qk[rows, 4, 0:CTX], start=True, stop=True)
                    for b in range(2):
                        out = ps[:, bank, CTX:CTX + T] if b == 0 else ps[:, bank + 1, 0:T]
                        q = qk[rows, c, CTX + b * P:CTX + (b + 1) * P]
                        mm(out[:, 0:PAST], q, cache_k[rows, :], start=True, stop=True)
                        last = mm(out[:, PAST:], q, qk[rows, 4, CTX:T], start=True, stop=True)
                    last.then_inc(logits_done, 1)

                def values_of(n):
                    c, kv = n // 2, n % 2
                    rows = slice(HEAD_DIM * kv, HEAD_DIM * (kv + 1))
                    pe.wait_ge(p_ready, n + 1)
                    if n >= 1:
                        pe.wait_ge(pt_copied, n)
                    flat = ps[:, 6:8, :].rearrange("p a b -> p (a b)")
                    for s in range(7):
                        last = nc.tensor.transpose(flat[:, s * P:(s + 1) * P], logits[:, n % 2, s * P:(s + 1) * P],
                                                   ident[:, :])
                    last.then_inc(pt_done, 1)
                    pe.wait_ge(pt_copied, n + 1)
                    if kv == 0 and c >= 2:
                        pe.wait_ge(att_taken, c - 1)
                    lat = (cache_v[:, rows], v_nat[:, 1, rows], v_nat[:, 2, rows])
                    s = 0
                    for piece, vs in enumerate(((v_nat[:, 0, rows],), lat, lat)):
                        for a, v in enumerate(vs):
                            last = mm(ps[rows, PROJ + c % 2, piece * P:(piece + 1) * P], v, p_t[:, s * P:(s + 1) * P],
                                      start=a == 0, stop=a == len(vs) - 1)
                            s += 1
                    last.then_inc(att_done, 1)

                scores_of(0)
                for n in range(1, N_HEADS):
                    scores_of(n)
                    values_of(n - 1)
                values_of(N_HEADS - 1)
                pe.wait_ge(logits_read, N_HEADS)
                for g in range(NG):
                    pe.wait_ge(pooled_ready, g + 1)
                    mm(ps[:, ACC + g, 0:T], w_pool[:, g, :], pooled[:, g, :],
                       start=True, stop=True).then_inc(mixed_done, 1)
                operand()
                with pe.Fori(0, 2) as i:
                    for j in range(4):
                        project(i, 4, M0["out"] + j, R0["out"] + j)

            def convolution():
                with pe.Fori(0, 4) as i:
                    for j in range(4):
                        project(i, 4, M0["w1"] + j, R0["w1"] + j)
                for n, src in enumerate((conv, conv_sq)):
                    pe.wait_ge(conv_ready, n + 1)
                    for k in range(KC):
                        last = mm(ps[:, ACC + n, 0:CONV_OUT], ones[:, :], src[:, k, :], start=k == 0, stop=k == KC - 1)
                    last.then_inc(mean_done, 1)
                operand()
                with pe.Fori(0, 2) as i:
                    for j in range(4):
                        project(i, 4, M0["w2"] + j, R0["w2"] + j)

            def scores(layer):
                m0, r0 = M0[f"wq{layer}"], R0[f"wq{layer}"]
                pe.wait_ge(keys_loaded, 16 * (layer + 1))
                def queries(i):
                    def score(j):
                        pe.wait_ge(proj_taken, i * 4 + (r0 + j + 1))
                        if j == 0:
                            since(pe, s_taken, i * 4 + layer * HS)
                        for t in range(NT):
                            last = mm(ps[:, ACC + j, t * P:(t + 1) * P], ga[:, j, t * P:(t + 1) * P],
                                      keys[:, bass.ds(i * 4 + j, 1), :].rearrange("p a k -> p (a k)"),
                                      start=True, stop=True)
                        last.then_inc(s_done, 1)

                    project(i, 4, m0, r0)
                    for j in range(1, 4):
                        project(i, 4, m0 + j, r0 + j)
                        score(j - 1)
                    score(3)

                rounds(pe, HS // 4, queries, peel=layer == 0)

            def experts(layer):
                m0, r0 = M0[f"u{layer}"], R0[f"u{layer}"]
                with pe.Fori(0, UBLOCKS // 4) as i:
                    for j in range(4):
                        project(i, 4, m0 + j, r0 + j)
                pe.wait_ge(sel_ready, layer + 1)
                for a, s in enumerate((1, 2, 3)):
                    for t in range(NT):
                        last = nc.tensor.transpose(ps[:, ACC + a, t * P:(t + 1) * P], sel[:, s, t, :], ident[:, :])
                last.then_inc(cols_done, 1)
                def with_table(i):
                    for j in range(8):
                        project(i, 8, m0 + UBLOCKS + j, r0 + UBLOCKS + j)
                        b = j % 2
                        base = layer * GBLOCKS + j
                        pe.wait_ge(hot_ready, i * 8 + (base + 1))
                        since(pe, g_taken, i * 8 + (base - 1))
                        for q in range(TOK):
                            out = ps[:, ACC + 2 * b + q // 4, (q % 4) * P:(q % 4 + 1) * P]
                            for part in range(3):
                                last = mm(out, oh2[:, b, q, :], oh1[:, b, part, q, :], start=part == 0, stop=part == 2)
                        last.then_inc(g_done, 1)

                rounds(pe, GBLOCKS // 8, with_table, peel=layer == 0)
                pe.wait_ge(g_taken, (layer + 1) * GBLOCKS)
                v0 = M0[f"v{layer}"]

                def block_of(i, j, first=False, final=False):
                    s, b = (v0 + j) % RING, j % 2
                    pe.wait_ge(lo_ready, i * 8 + (v0 + j + 1))
                    pe.wait_ge(wlo_ready, i * 8 + (layer * N_KEYS + j + 1))
                    for t in range(NT):
                        rows = slice(t * P, (t + 1) * P)
                        for w, v, begins, ends in ((g_hi, w_hi, True, False), (g_hi, w_lo, False, False),
                                                   (g_lo, w_hi, False, True)):
                            for half in range(2):
                                last = mm(ps[:, ACC + 2 * t + half, :], w[:, b, rows],
                                          v[:, s, half * 512:(half + 1) * 512],
                                          start=first and begins, stop=final and ends)
                    last.then_inc(block_done, 1)

                for j in range(8):
                    block_of(0, j, first=j == 0)
                with pe.Fori(1, N_KEYS // 8 - 1) as i:
                    for j in range(8):
                        block_of(i, j)
                for j in range(8):
                    block_of(N_KEYS // 8 - 1, j, final=j == 7)
                pe.wait_ge(y_copied, layer + 1)
                for k in range(KC):
                    if layer or k >= 2:
                        pe.wait_ge(yt_taken, layer * KC + k - 1)
                    for t in range(NT):
                        last = nc.tensor.transpose(ps[:, PROJ + k % 2, t * P:(t + 1) * P],
                                                   y_nat[:, t, k * P:(k + 1) * P], ident[:, :])
                    last.then_inc(yt_done, 1)

            for layer in range(DEPTH):
                column_sums(2 * layer)
                operand()
                [attention, convolution][layer]()
                column_sums(2 * layer + 1)
                operand()
                scores(layer)
                experts(layer)
            column_sums(2 * DEPTH)


def laid_out(i):
    def chunks(w):
        rows, cols = w.shape
        return w.reshape(KC, P, cols // P, P).transpose(2, 1, 0, 3).reshape(cols // P, P, rows)

    def columns(v):
        return np.moveaxis(v.reshape(v.shape[:-1] + (KC, P)), -1, 0)

    heads = [h for c in range(PAIRS) for h in (c, c + PAIRS)]
    w_in = i["w_in"][0]
    q = w_in[:, :512].reshape(D, N_HEADS, HEAD_DIM)[:, heads].reshape(D, 512)
    w_in = np.concatenate([q, w_in[:, 512:640], w_in[:, 768:], w_in[:, 640:768]], 1)
    w_out = i["w_out"][0]
    w_out = np.concatenate([w_out[:512].reshape(N_HEADS, HEAD_DIM, D)[heads].reshape(512, D), w_out[512:]], 0)
    w1 = i["conv_w1"][0].reshape(D, 2, KC, P)[:, ::-1].transpose(0, 2, 1, 3).reshape(D, 2 * D)
    x = np.concatenate([i["x_prompt"][0], i["x_sample"][0]], 0)
    gains = np.stack([i["norm_mix_g"][0], i["norm_ffn_g"][0], i["norm_mix_g"][1], i["norm_ffn_g"][1], i["final_norm_g"]])
    a = {
        "x": x.T.reshape(KC, P, T).transpose(1, 0, 2),
        "c": columns(np.stack([i["c_ctx"], i["c"][0]])).transpose(0, 2, 1),
        "mod_b": columns(i["mod_b"].reshape(DEPTH, 6, D)).reshape(P, MOD_BLOCKS),
        "gains": columns(gains),
        "sink": np.tile(i["attn_sink"][0][None, :], (P, 1)),
        "pool_scale": i["pool_scale"][0].reshape(NG, P).T,
        "b1": columns(i["conv_b1"][0].reshape(2, D)).reshape(P, 2 * KC),
        "dw": i["conv_dw"][0].reshape(CONV_WIDTH, KC, P).transpose(2, 1, 0),
        "cvecs": columns(np.stack([i["conv_dw_b"][0], i["conv_ln_g"][0], i["conv_ln_b"][0], i["conv_b2"][0]])),
        "w_pool": i["w_pool"][0].transpose(1, 0, 2),
        "cache_k": i["cache_k"][0, 0].reshape(PAST, P).T,
        "cache_v": i["cache_v"][0, 0].reshape(PAST, P),
        "keys": i["peer_keys"].reshape(DEPTH, HS, N_KEYS, P).transpose(0, 3, 1, 2),
        "mod_w": np.concatenate([chunks(w) for w in i["mod_w"]], 0),
        "in": chunks(w_in), "out": chunks(w_out), "w1": chunks(w1), "w2": chunks(i["conv_w2"][0]),
    }
    for layer in range(DEPTH):
        a[f"wq{layer}"] = chunks(i["peer_wq"][layer])
        a[f"u{layer}"] = i["peer_u"][layer].reshape(N_KEYS, P, KC, P).transpose(0, 3, 2, 1).reshape(N_KEYS, P, D)
        a[f"v{layer}"] = i["peer_v"][layer].reshape(N_KEYS, P, D)
    a.update(constants())
    return {n: np.ascontiguousarray(v) for n, v in a.items()}


OUTS = {"y": (P, KC, T), "state_k": (P, CTX), "state_v": (CTX, P)}


def kernel(**inputs):
    import concourse.bacc as bacc
    from concourse.bass_utils import run_bass_kernel_spmd

    arrays = laid_out({n: np.asarray(v) for n, v in inputs.items()})
    nc = bacc.Bacc("TRN2", target_bir_lowering=False, num_devices=1)
    io = {n: nc.dram_tensor(f"in_{n}", a.shape, mybir.dt.from_np(a.dtype), kind="ExternalInput").ap()
          for n, a in arrays.items()}
    for n, shape in OUTS.items():
        io[n] = nc.dram_tensor(f"out_{n}", shape, F32, kind="ExternalOutput").ap()
    build(nc, io)
    r = run_bass_kernel_spmd(nc, [{f"in_{n}": a for n, a in arrays.items()}], core_ids=[0]).results[0]
    y = r["out_y"].transpose(1, 0, 2).reshape(D, T).T
    state_k = r["out_state_k"].T.reshape(1, 1, CTX, 2, HEAD_DIM)
    state_v = r["out_state_v"].reshape(1, 1, CTX, 2, HEAD_DIM)
    return (np.ascontiguousarray(y[None, :CTX]), np.ascontiguousarray(y[None, CTX:]),
            np.ascontiguousarray(state_k), np.ascontiguousarray(state_v))
```

```python
from contextlib import ExitStack

import concourse.bass as bass
from concourse import mybir
import numpy as np

ALU = mybir.AluOpType
ACT = mybir.ActivationFunctionType
AX = mybir.AxisListType
F32 = mybir.dt.float32
F32R = mybir.dt.float32r
BF16 = mybir.dt.bfloat16
U32 = mybir.dt.uint32

P = 128
D = 1024
KC = D // P
CTX = 128
LAT = 256
T = CTX + LAT
NT = T // P
DEPTH = 2
EPS = 1e-6
NEG = -1e30
GRID_W = 64
HEAD_DIM = 64
N_HEADS = 8
PAIRS = N_HEADS // 2
SCALE = HEAD_DIM ** -0.5
WINDOW = 128
PAST = 128
POOL_SIZES = (2, 4, 8, 16)
NG = len(POOL_SIZES)
PAD = max(POOL_SIZES) // 2
POOL_W = PAD + CTX + PAD + LAT + PAD
CONV_WIDTH = 31
CPAD = CONV_WIDTH // 2
CONV_IN = CPAD + CTX + CPAD + LAT + CPAD
CONV_OUT = CONV_IN - 2 * CPAD
CONV_DVE = 6
N_KEYS = 128
PEER_HEADS = 8
HS = 2 * PEER_HEADS
TOPK = 16
LOWEST = -3.0e38

TOK = 4
CHUNK = 32
NCHUNK = T // CHUNK
GBLOCKS = T // TOK
TAIL = 2
UBLOCKS = N_KEYS - GBLOCKS - TAIL
QUAD = 4
HOTS = 4
SETS = CHUNK // TOK

WORK = 16600

RING = 4
LEAD = 2
MOD_BLOCKS = DEPTH * 6 * KC
MSLOTS = 4
MOD_EARLY = 5 * KC
MOD_FIRST = 2 * KC
MOD_ROUNDS = (MOD_BLOCKS - MOD_EARLY) // MSLOTS

SEGMENTS = [("in", 10), ("out", 8), ("wq0", HS), ("u0", N_KEYS), ("v0", N_KEYS),
            ("w1", 16), ("w2", 8), ("wq1", HS), ("u1", N_KEYS), ("v1", N_KEYS)]
M0, R0 = {}, {}
_m = _r = 0
for _name, _count in SEGMENTS:
    M0[_name], R0[_name] = _m, _r
    _m += _count
    _r += 0 if _name[0] == "v" else _count
BLOCKS = _m

SEGS = ((0, 0, CTX), (1, CTX, LAT))


def since(engine, semaphore, count):
    if isinstance(count, int) and count <= 0:
        return
    engine.wait_ge(semaphore, count)


def rounds(engine, count, body, peel=False):
    if peel:
        body(0)
    with engine.Fori(int(peel), count) as i:
        body(i)


def constants():
    quarter = HEAD_DIM // 4
    freqs = (np.float32(10000.0) ** (-np.arange(quarter, dtype=np.float32) / np.float32(quarter))).astype(np.float32)
    t = np.arange(LAT)
    rows = (t // GRID_W).astype(np.float32)[None, :] * freqs[:, None]
    cols = (t % GRID_W).astype(np.float32)[None, :] * freqs[:, None]
    ang = np.concatenate([rows, rows, cols, cols, rows, rows, cols, cols], 0).astype(np.float32)
    turn = np.zeros((P, P), np.float32)
    for base in range(0, P, 2 * quarter):
        for j in range(quarter):
            turn[base + quarter + j, base + j] = -1.0
            turn[base + j, base + quarter + j] = 1.0
    q = np.arange(P)[:, None]
    keys = np.arange(LAT)[None, :]
    mask = np.zeros((P, 2, PAST + LAT), np.float32)
    for b in range(2):
        mask[:, b, PAST:] = np.where(np.abs(q + b * P - keys) <= WINDOW, 0.0, NEG)
    inv = np.zeros((P, NG, T), np.float32)
    for g, w in enumerate(POOL_SIZES):
        for _, start, n in SEGS:
            s = np.arange(n)
            count = np.clip(s + (w - w // 2), 0, n) - np.clip(s - w // 2, 0, n)
            inv[:, g, start:start + n] = (np.float32(1.0) / count.astype(np.float32))[None, :]
    return {
        "c_cos": np.cos(ang).astype(np.float32), "c_sin": np.sin(ang).astype(np.float32), "c_turn": turn,
        "c_ident": np.eye(P, dtype=np.float32), "c_mask": mask, "c_inv": inv,
    }


def build(nc, io):
    ctx = ExitStack()
    with ctx:
        def sb(name, shape, dt=F32):
            return ctx.enter_context(nc.sbuf_tensor(name, shape, dt))

        def sem(name):
            return ctx.enter_context(nc.semaphore(name))

        x = sb("x", [P, KC, T])
        hf = sb("hf", [P, KC, T])
        h_hi = sb("h_hi", [P, KC, T], F32R)
        h_lo = sb("h_lo", [P, KC, T], F32R)
        raw = sb("raw", [P, RING, D])
        w_hi = sb("w_hi", [P, RING, D], F32R)
        w_lo = sb("w_lo", [P, RING, D], F32R)
        ga = sb("ga", [P, 4, T])
        g_hi = sb("g_hi", [P, 2, T], F32R)
        g_lo = sb("g_lo", [P, 2, T], F32R)
        hots = sb("hots", [P, HOTS * D])
        sums = sb("sums", [P, MSLOTS, 2])
        keys = sb("keys", [P, HS, N_KEYS])
        mod = sb("mod", [P, MOD_BLOCKS, 2])
        mod_b = sb("mod_b", [P, MOD_BLOCKS])
        gains = sb("gains", [P, 2 * DEPTH + 1, KC])
        scales = sb("scales", [P, 2 * DEPTH, KC, 2])
        sink = sb("sink", [P, N_HEADS])
        pool_scale = sb("pool_scale", [P, NG])
        b1 = sb("b1", [P, 2 * KC])
        dw = sb("dw", [P, KC, CONV_WIDTH])
        cvecs = sb("cvecs", [P, 4, KC])
        gb2 = sb("gb2", [P, KC, 2])
        turn = sb("turn", [P, P])
        ident = sb("ident", [P, P])
        ones = sb("ones", [P, P])
        iota_b = sb("iota_b", [P, P], BF16)
        iota16 = sb("iota16", [P, TOPK])
        stat = sb("stat", [P, 4, CONV_OUT])
        work = sb("work", [P, WORK])
        ps = ctx.enter_context(nc.psum_tensor("ps", [P, 8, 512], F32))
        PROJ = 0
        ACC = 2

        oh2 = hots[:, 0:D].bitcast(BF16).rearrange("p (b q k) -> p b q k", b=HOTS, k=P)
        oh1 = hots[:, D:4 * D].bitcast(BF16).rearrange("p (b a q k) -> p b a q k", b=HOTS, a=3, k=P)
        diag = hots[:, 0:CONV_WIDTH * P].rearrange("p (j k) -> p j k", k=P)
        mod_w = hots[:, :].rearrange("p (s d) -> p s d", s=MSLOTS)
        c_all = keys[:, :, :].rearrange("p a k -> p (a k)").rearrange("p (g d) -> p g d", g=2)
        unread = ga[:, :, :].rearrange("p a t -> p (a t)")[:, 0:D].bitcast(BF16).rearrange("p (g d) -> p g d", g=2)

        place = [0]

        def region(*shape, at=None):
            if at is not None:
                place[0] = at
            n = int(np.prod(shape))
            v = work[:, place[0]:place[0] + n]
            place[0] += n
            assert place[0] <= WORK, place[0]
            names = "abcd"[:len(shape)]
            return v if len(shape) == 1 else v.rearrange(
                f"p ({' '.join(names)}) -> p {' '.join(names)}", **dict(zip(names, shape)))

        cos = region(LAT, at=0)
        sin = region(LAT)
        mask = region(2, PAST + LAT)
        inv = region(NG, T)
        w_pool = region(NG, P)
        cache_k = region(PAST)
        cache_v = region(P)
        qk = region(5, T)
        turned = region(5, LAT)
        v_nat = region(NT, P)
        u_pad = region(NG, POOL_W)
        sum_a = region(NG, POOL_W)
        sum_b = region(NG, POOL_W)
        logits = region(2, CTX + 2 * (PAST + LAT))
        p_t = region(CTX + 2 * (PAST + LAT))
        sm = region(2, 5, 3)
        pooled = region(NG, T)
        a_pad = region(KC, CONV_IN, at=0)
        conv = region(KC, CONV_OUT)
        conv_sq = region(KC, CONV_OUT)
        glu = region(2, 2, T)
        odd = region(2, CONV_OUT)
        stage = region(2, N_KEYS, CHUNK, at=0)
        s_all = region(NT, HS, N_KEYS, at=0)
        vals = region(NT, HS, TOPK)
        key_us = region(NT, HS, TOPK)
        key_f = region(HS, TOPK)
        pos_u = region(3, P)
        pos_f = region(2, P)
        top = region(P)
        after_topk = place[0]
        sel = region(4, NT, P, at=max(after_topk, 2 * N_KEYS * CHUNK))
        gsum = region(2, NT * PEER_HEADS)
        col_key = region(2, T)
        col_g = region(3, T)
        col_b = region(T // 2).bitcast(BF16)
        after_cols = place[0]
        cand = hf[:, :, :].rearrange("p k t -> p (k t)")[:, 0:PEER_HEADS * TOPK * TOPK].rearrange(
            "p (h a b) -> p h a b", h=PEER_HEADS, a=TOPK)
        g_in = region(2, NCHUNK, QUAD * CHUNK, at=after_cols)
        wf = region(2, T)
        a_in = region(4, T, at=2 * N_KEYS * CHUNK)

        small_loaded = sem("small_loaded")
        keys_loaded = sem("keys_loaded")
        first_loaded = sem("first_loaded")
        c_loaded = sem("c_loaded")
        mod_raw = [sem(f"mod_raw{j}") for j in range(MSLOTS)]
        raw_ready = [sem(f"raw_ready{j}") for j in range(RING)]
        consts_ready = sem("consts_ready")
        pads_ready = sem("pads_ready")
        iota_ready = sem("iota_ready")
        c_ready = sem("c_ready")
        mod_summed = sem("mod_summed")
        mod_ready = sem("mod_ready")
        scales_ready = sem("scales_ready")
        hi_ready = sem("hi_ready")
        lo_ready = sem("lo_ready")
        block_done = sem("block_done")
        proj_taken = sem("proj_taken")
        sq_ready = sem("sq_ready")
        stat_ready = sem("stat_ready")
        var_ready = sem("var_ready")
        std_ready = sem("std_ready")
        z_ready = sem("z_ready")
        hi_part = sem("hi_part")
        operand_ready = sem("operand_ready")
        dve_order = sem("dve_order")
        act_order = sem("act_order")
        turn_done = sem("turn_done")
        roped = sem("roped")
        logits_done = sem("logits_done")
        max_ready = sem("max_ready")
        exp_ready = sem("exp_ready")
        logits_read = sem("logits_read")
        p_ready = sem("p_ready")
        pt_done = sem("pt_done")
        pt_copied = sem("pt_copied")
        att_done = sem("att_done")
        att_taken = sem("att_taken")
        pooled_ready = sem("pooled_ready")
        mixed_done = sem("mixed_done")
        state_out = sem("state_out")
        s_done = sem("s_done")
        s_taken = sem("s_taken")
        gelu_done = sem("gelu_done")
        a_stored = [sem(f"a_stored{j}") for j in range(4)]
        top_ready = sem("top_ready")
        exp_done = sem("exp_done")
        sel_ready = sem("sel_ready")
        cols_done = sem("cols_done")
        hot_ready = sem("hot_ready")
        g_done = sem("g_done")
        g_taken = sem("g_taken")
        g_stored = [sem(f"g_stored{j}") for j in range(2)]
        a_loaded = [sem(f"a_loaded{j}") for j in range(4)]
        g_loaded = [sem(f"g_loaded{j}") for j in range(2)]
        w_ready = sem("w_ready")
        whi_ready = sem("whi_ready")
        wlo_ready = sem("wlo_ready")
        y_done = sem("y_done")
        x_ready = sem("x_ready")
        glu_in = sem("glu_in")
        glu_out = sem("glu_out")
        tap_done = sem("tap_done")
        conv_ready = sem("conv_ready")
        diag_ready = sem("diag_ready")
        diag_used = sem("diag_used")
        conv_done = sem("conv_done")
        conv_taken = sem("conv_taken")
        mean_done = sem("mean_done")
        centred = sem("centred")
        csq_ready = sem("csq_ready")
        out_ready = sem("out_ready")
        out_stored = sem("out_stored")

        a_dram = nc.dram_tensor("a_dram", (N_KEYS, P, T), F32).ap()
        g_dram = nc.dram_tensor("g_dram", (NCHUNK, P, N_KEYS * CHUNK), F32).ap()
        g_quads = g_dram.rearrange("c p (q i t) -> p q c (i t)", i=QUAD, t=CHUNK)

        def one(ap, n):
            return ap[bass.ds(n, 1)].rearrange("a p n -> (a p) n")

        def mod_col(layer, part, k, group):
            return mod[:, (layer * 6 + part) * KC + k, group:group + 1]

        NORMS = [(l, w) for l in range(DEPTH) for w in range(2)]

        small = [
            (sink[:, :], io["sink"]), (pool_scale[:, :], io["pool_scale"]),
            (b1[:, :], io["b1"]), (dw[:, :, :], io["dw"]), (cvecs[:, :, :], io["cvecs"]),
            (turn[:, :], io["c_turn"]), (ident[:, :], io["c_ident"]), (cos, io["c_cos"]), (sin, io["c_sin"]),
            (mask, io["c_mask"]), (inv, io["c_inv"]), (w_pool, io["w_pool"]), (cache_k, io["cache_k"]),
            (cache_v, io["cache_v"]),
        ]

        block = ctx.enter_context(nc.Block())

        @block.sync
        def _(sp):
            def conditioning():
                sp.dma_start(c_all, io["c"]).then_inc(c_loaded, 16)

            def mod_load(n):
                if n >= MSLOTS:
                    sp.wait_ge(mod_summed, 2 * (n - MSLOTS + 1))
                sp.dma_start(mod_w[:, n % MSLOTS, :], one(io["mod_w"], n)).then_inc(mod_raw[n % MSLOTS], 16)

            def load(name, n, m_mod):
                sp.dma_start(raw[:, m_mod % RING, :], one(io[name], n)).then_inc(raw_ready[m_mod % RING], 16)

            def stream(name, first, count, body):
                m0 = M0[name] + first
                if count == body:
                    for j in range(body):
                        sp.wait_ge(lo_ready, m0 + j - RING + 1)
                        load(name, first + j, m0 + j)
                    return
                with sp.Fori(0, count // body) as i:
                    for j in range(body):
                        sp.wait_ge(lo_ready, i * body + (m0 + j - RING + 1))
                        load(name, i * body + (first + j), m0 + j)

            def mod_load_late(k):
                sp.dma_start(mod_w[:, k, :], one(io["mod_w"], MOD_EARLY + k)).then_inc(mod_raw[k], 16)

            conditioning()
            mod_load(0)
            mod_load(1)
            sp.dma_start(x[:, :, :], io["x"]).then_inc(first_loaded, 16)
            sp.dma_start(mod_b[:, :], io["mod_b"]).then_inc(first_loaded, 16)
            sp.dma_start(gains[:, :, :], io["gains"]).then_inc(first_loaded, 16)
            for n in range(2, 8):
                mod_load(n)
            load("in", 0, 0)
            load("in", 1, 1)
            for n in range(8, MOD_FIRST):
                mod_load(n)
            load("in", 2, 2)
            load("in", 3, 3)
            for dst, src in small:
                sp.dma_start(dst, src).then_inc(small_loaded, 16)
            n = MOD_FIRST
            for m in range(RING, 10):
                for _ in range(2):
                    mod_load(n)
                    n += 1
                stream("in", m, 1, 1)
            for m in range(RING):
                if n < MOD_EARLY - 8:
                    mod_load(n)
                    n += 1
                stream("out", m, 1, 1)
            for m in range(n, MOD_EARLY):
                mod_load(m)
            sp.wait_ge(mod_summed, 2 * MOD_EARLY)
            sp.dma_start(keys[:, :, :], io["keys"][0]).then_inc(keys_loaded, 16)
            stream("out", RING, RING, RING)
            for layer in range(DEPTH):
                stream(f"wq{layer}", 0, HS, 4)
                stream(f"u{layer}", 0, N_KEYS, 4)
                name, v0 = f"v{layer}", M0[f"v{layer}"]
                after = ["w1", None][layer]
                stream(name, 0, RING, RING)
                for s in range(2):
                    sp.wait_ge(g_stored[s], 16 * (layer + 1) * (NCHUNK // 2))
                for s in range(2):
                    sp.dma_start(g_in[:, s], g_quads[:, s]).then_inc(g_loaded[s], 16)
                for j in range(4):
                    sp.dma_start(a_in[:, j, :], one(a_dram, j)).then_inc(a_loaded[j], 16)
                for j in range(4):
                    sp.wait_ge(a_stored[j], 16 * (layer + 1) * (N_KEYS // 4))
                if layer == 0:
                    sp.wait_ge(s_done, HS)
                    conditioning()
                    for k in range(MSLOTS):
                        mod_load_late(k)

                def beside(i, j, more):
                    sp.wait_ge(lo_ready, i * 8 + (v0 + j + 1))
                    if more or j < 8 - RING:
                        load(name, i * 8 + (j + RING), v0 + j)
                    elif after:
                        load(after, j - (8 - RING), v0 + j)
                    if more or j < 4:
                        sp.wait_ge(w_ready, i * 8 + (layer * N_KEYS + j + 1))
                        sp.dma_start(a_in[:, j % 4, :], one(a_dram, i * 8 + (j + 4))).then_inc(a_loaded[j % 4], 16)
                    if more and j % 4 == 3:
                        s = j // 4
                        sp.dma_start(g_in[:, s].unsqueeze(1),
                                     g_quads[:, bass.ds(i * 2 + (s + 2), 1)]).then_inc(g_loaded[s], 16)

                if layer == 0:
                    for j in range(8):
                        beside(0, j, True)
                    with sp.Fori(1, MOD_ROUNDS) as i:
                        for j in range(8):
                            beside(i, j, True)
                            if j % 2:
                                sp.wait_ge(mod_summed, i * 8 + (2 * MOD_EARLY - 8 + j + 1))
                                sp.dma_start(mod_w[:, j // 2, :], one(io["mod_w"], i * MSLOTS + (MOD_EARLY + j // 2))
                                             ).then_inc(mod_raw[j // 2], 16)
                with sp.Fori(0 if layer else MOD_ROUNDS, N_KEYS // 8 - 1) as i:
                    for j in range(8):
                        beside(i, j, True)
                for j in range(8):
                    if j < 8 - RING or after:
                        beside(N_KEYS // 8 - 1, j, False)
                if layer == 0:
                    sp.wait_ge(mod_summed, 2 * MOD_BLOCKS)
                    sp.dma_start(keys[:, :, :], io["keys"][1]).then_inc(keys_loaded, 16)
                    stream("w1", RING, 16 - RING, 4)
                    stream("w2", 0, 8, 4)

            for k in range(0, KC, 2):
                sp.wait_ge(out_ready, k + 2)
                sp.dma_start(io["y"][:, k:k + 2], hf[:, k:k + 2, :]).then_inc(out_stored, 16)
            sp.wait_ge(out_stored, 16 * KC // 2)
            sp.wait_ge(state_out, 32)

        @block.gpsimd
        def _(pool):
            nc.gpsimd.iota(iota_b[:, :], pattern=[[1, P]], base=0, channel_multiplier=0,
                           allow_small_or_imprecise_dtypes=True).then_inc(iota_ready, 1)
            nc.gpsimd.iota(iota16[:, :], pattern=[[1, TOPK]], base=0, channel_multiplier=0,
                           allow_small_or_imprecise_dtypes=True).then_inc(iota_ready, 1)

            def low(m, j):
                pool.wait_ge(hi_ready, m + 1)
                nc.gpsimd.tensor_tensor(w_lo[:, j % RING, :], raw[:, j % RING, :],
                                        w_hi[:, j % RING, :].bitcast(F32), ALU.subtract).then_inc(lo_ready, 1)

            with pool.Fori(0, BLOCKS // 8) as i:
                for j in range(8):
                    low(i * 8 + j, j)
            for m in range(BLOCKS // 8 * 8, BLOCKS):
                low(m, m)

        @block.scalar
        def _(act):
            order = [0]

            def settle(ins):
                order[0] += 1
                ins.then_inc(act_order, 1)
                act.wait_ge(act_order, order[0])

            def high(i, step, m, wait_free=True):
                count = i * (16 * step // RING) + 16 * (m // RING + 1)
                act.wait_ge(raw_ready[m % RING], count)
                if wait_free:
                    act.wait_ge(block_done, i * step + (m - RING + 1))
                nc.scalar.activation(w_hi[:, m % RING, :], raw[:, m % RING, :], ACT.Copy).then_inc(hi_ready, 1)

            def ahead(i, step, m):
                if m + LEAD < BLOCKS:
                    high(i, step, m + LEAD, wait_free=m + LEAD >= RING)

            def projected(i, step, m):
                act.wait_ge(block_done, i * step + (m + 1))

            def conditioning(n):
                act.wait_ge(c_loaded, 16 * n)
                nc.scalar.activation(c_all, c_all, ACT.Silu).then_inc(c_ready, 1)

            conditioning(1)
            roots = [0]

            def root(width):
                roots[0] += 1
                act.wait_ge(var_ready, roots[0])
                nc.scalar.activation(stat[:, 1, 0:width], stat[:, 0, 0:width], ACT.Sqrt).then_inc(std_ready, 1)

            def normalise(n):
                root(T)
                if n == 0:
                    for m in range(LEAD):
                        high(0, 0, m, wait_free=False)
                if n == 2 * DEPTH:
                    return
                layer, which = NORMS[n]
                for k in range(KC):
                    act.wait_ge(z_ready, (n + n // 3) * KC + k + 1)
                    for g, start, count in SEGS:
                        last = nc.scalar.activation(h_hi[:, k, start:start + count], hf[:, k, start:start + count],
                                                    ACT.Identity, bias=mod_col(layer, 3 * which, k, g))
                    last.then_inc(hi_part, 1)

            def high_operand(k):
                nc.scalar.activation(h_hi[:, k, :], hf[:, k, :], ACT.Copy).then_inc(hi_part, 1)

            def gated(name, layer, part):
                m0 = M0[name]
                act.wait_ge(mod_ready, [MOD_EARLY - 2 * KC, MOD_BLOCKS][layer] // MSLOTS)
                with act.Fori(0, 2) as i:
                    for j in range(4):
                        ahead(i, 4, m0 + j)
                        projected(i, 4, m0 + j)
                        for g, start, n in SEGS:
                            k = i * 4 + j
                            col = bass.ds(i * 4 + ((layer * 6 + part) * KC + j), 1)
                            bias = gb2[:, bass.ds(k, 1), g:g + 1].rearrange("p a b -> p (a b)") if name == "w2" else 0.0
                            last = nc.scalar.activation(
                                hf[:, bass.ds(k, 1), start:start + n],
                                ps[:, PROJ + (R0[name] + j) % 2, start:start + n].unsqueeze(1), ACT.Identity,
                                scale=mod[:, col, g:g + 1].rearrange("p a b -> p (a b)"), bias=bias)
                        last.then_inc(proj_taken, 1)

            def attention():
                act.wait_ge(small_loaded, 16 * len(small))
                for c in range(10):
                    ahead(0, 0, M0["in"] + c)
                    if c == 0:
                        act.wait_ge(pads_ready, 1)
                    projected(0, 0, M0["in"] + c)
                    src = ps[:, PROJ + (R0["in"] + c) % 2, :]
                    if c < 5:
                        last = nc.scalar.activation(qk[:, c, :], src[:, 0:T], ACT.Copy)
                    elif c < 9:
                        for g, start, n in SEGS:
                            at = PAD * (g + 1) + start
                            last = nc.scalar.activation(u_pad[:, c - 5, at:at + n], src[:, start:start + n], ACT.Copy)
                    else:
                        last = nc.scalar.activation(v_nat.rearrange("p n d -> p (n d)"), src[:, 0:T], ACT.Copy)
                    last.then_inc(proj_taken, 1)
                act.wait_ge(proj_taken, R0["in"] + 10)
                act.dma_start(io["state_k"], qk[:, 4, 0:CTX]).then_inc(state_out, 16)
                act.dma_start(io["state_v"], v_nat[:, 0, :]).then_inc(state_out, 16)

                def transposed(n):
                    act.wait_ge(pt_done, n + 1)
                    if n >= 1:
                        act.wait_ge(att_done, n)
                    nc.scalar.activation(p_t, ps[:, 6:8, :].rearrange("p a b -> p (a b)")[:, 0:CTX + 2 * T],
                                         ACT.Copy).then_inc(pt_copied, 1)

                def pair(c):
                    act.wait_ge(att_done, 2 * c + 2)
                    nc.scalar.activation(hf[:, c, :], ps[:, PROJ + c % 2, 0:T], ACT.Copy).then_inc(att_taken, 1)
                    act.wait_ge(att_taken, c + 1)
                    high_operand(c)

                for n in range(N_HEADS):
                    b = n % 2
                    head = n // 2 + PAIRS * (n % 2)
                    act.wait_ge(max_ready, n + 1)
                    start = 0
                    for piece, width in enumerate((CTX, T, T)):
                        part = logits[:, b, start:start + width]
                        nc.scalar.activation(part, part, ACT.Exp, bias=sm[:, b, 1, piece:piece + 1],
                                             accum_out=sm[:, b, 2, piece:piece + 1])
                        start += width
                    nc.scalar.activation(sm[:, b, 3, :], sm[:, b, 1, :], ACT.Exp,
                                         bias=sink[:, head:head + 1]).then_inc(exp_ready, 1)
                    if n >= 1:
                        transposed(n - 1)
                        if n % 2 == 0:
                            pair(n // 2 - 1)
                transposed(N_HEADS - 1)
                pair(PAIRS - 1)
                for g in range(NG):
                    act.wait_ge(mixed_done, g + 1)
                    settle(nc.scalar.activation(hf[:, PAIRS + g, :], ps[:, ACC + g, 0:T], ACT.Identity,
                                                scale=pool_scale[:, g:g + 1]))
                    high_operand(PAIRS + g)
                gated("out", 0, 2)

            def convolution():
                def gates(i):
                    for j in range(4):
                        ahead(i, 4, M0["w1"] + j)
                        projected(i, 4, M0["w1"] + j)
                        src = ps[:, PROJ + (R0["w1"] + j) % 2, 0:T]
                        s = j // 2
                        if j % 2 == 0:
                            since(act, glu_out, i * 2)
                            nc.scalar.activation(glu[:, s, 0, :], src, ACT.Sigmoid,
                                                 bias=b1[:, bass.ds(i * 2 + (KC + s), 1)]).then_inc(proj_taken, 1)
                        else:
                            nc.scalar.activation(glu[:, s, 1, :], src, ACT.Identity,
                                                 bias=b1[:, bass.ds(i * 2 + s, 1)]).then_inc(proj_taken, 1)

                rounds(act, 4, gates, peel=True)
                for c in range(KC - CONV_DVE):
                    for j in range(CONV_WIDTH):
                        if c and j < CONV_WIDTH - 1:
                            act.wait_ge(diag_used, (c - 1) * (CONV_WIDTH - 1) + j + 1)
                        elif c:
                            act.wait_ge(conv_done, c)
                        nc.scalar.activation(diag[:, j, :], ident[:, :], ACT.Copy,
                                             scale=dw[:, CONV_DVE + c, j:j + 1]).then_inc(diag_ready, 1)
                for c in range(KC - CONV_DVE):
                    k = CONV_DVE + c
                    act.wait_ge(conv_done, c + 1)
                    nc.scalar.activation(conv[:, k, :], ps[:, ACC + 2 + c, 0:CONV_OUT], ACT.Identity,
                                         bias=cvecs[:, 0, k:k + 1]).then_inc(conv_taken, 1)
                for k in range(KC):
                    act.wait_ge(centred, k + 1)
                    nc.scalar.activation(conv_sq[:, k, :], conv[:, k, :], ACT.Square).then_inc(csq_ready, 1)
                root(CONV_OUT)
                for k in range(KC):
                    act.wait_ge(z_ready, 2 * KC + KC + k + 1)
                    for g, start, n in SEGS:
                        at = start + g * CPAD
                        last = nc.scalar.activation(hf[:, k, start:start + n], conv[:, k, at:at + n], ACT.Silu,
                                                    scale=cvecs[:, 1, k:k + 1], bias=cvecs[:, 2, k:k + 1])
                    settle(last)
                    high_operand(k)
                gated("w2", 1, 2)

            def scores(layer):
                m0, r0 = M0[f"wq{layer}"], R0[f"wq{layer}"]
                for j in range(4 if layer else 0):
                    act.wait_ge(a_stored[j], 16 * (N_KEYS // 4))
                if layer == 0:
                    act.wait_ge(state_out, 32)
                def queries(i):
                    def query(j):
                        ahead(i, 4, m0 + j)
                        projected(i, 4, m0 + j)
                        if j == 0:
                            since(act, s_done, i * 4 + layer * HS)
                        nc.scalar.activation(ga[:, j, :], ps[:, PROJ + (r0 + j) % 2, 0:T],
                                             ACT.Copy).then_inc(proj_taken, 1)

                    def take(j):
                        act.wait_ge(s_done, i * 4 + (layer * HS + j + 1))
                        nc.scalar.activation(
                            s_all[:, :, bass.ds(i * 4 + j, 1), :].rearrange("p n a k -> p n (a k)"),
                            ps[:, ACC + j, 0:T].rearrange("p (n k) -> p n k", n=NT), ACT.Copy).then_inc(s_taken, 1)

                    query(0)
                    query(1)
                    take(0)
                    query(2)
                    take(1)
                    query(3)
                    take(2)
                    take(3)

                rounds(act, HS // 4, queries, peel=layer == 0)

            def gelu(layer, i, step, m, r, count):
                j = count % 4
                projected(i, step, m)
                since(act, a_stored[j], i * (4 * step) + 16 * (layer * N_KEYS // 4 + count // 4))
                nc.scalar.activation(ga[:, j, :], ps[:, PROJ + r % 2, 0:T], ACT.Gelu).then_inc(proj_taken, 1)
                act.wait_ge(proj_taken, i * step + (r + 1))
                act.dma_start(one(a_dram, i * step + count), ga[:, j, :]).then_inc(a_stored[j], 16)

            def experts(layer):
                m0, r0 = M0[f"u{layer}"], R0[f"u{layer}"]
                def plain(i, first=0, count=4):
                    for j in range(first, first + count):
                        ahead(i, 4, m0 + j)
                        gelu(layer, i, 4, m0 + j, r0 + j, j)

                rounds(act, UBLOCKS // 4, plain, peel=layer == 0)
                plain(0, UBLOCKS // 4 * 4, UBLOCKS % 4)
                act.wait_ge(top_ready, layer + 1)
                nc.scalar.activation(sel[:, 3], sel[:, 0], ACT.Exp).then_inc(exp_done, 1)

                def with_table(i):
                    for j in range(2 * SETS):
                        b = UBLOCKS + j
                        ahead(i, 2 * SETS, m0 + b)
                        gelu(layer, i, 2 * SETS, m0 + b, r0 + b, b)
                        s = j // SETS
                        if j % SETS == 0:
                            since(act, g_stored[s], i * 16 + layer * 16 * (NCHUNK // 2))
                        act.wait_ge(g_done, i * (2 * SETS) + (layer * GBLOCKS + j + 1))
                        tok = (j % SETS) * TOK
                        nc.scalar.activation(
                            stage[:, s, :, tok:tok + TOK].rearrange("p k t -> p t k"),
                            ps[:, ACC + j % HOTS, :].rearrange("p (t k) -> p t k", k=N_KEYS), ACT.Copy).then_inc(g_taken, 1)
                        if j % SETS == SETS - 1:
                            act.wait_ge(g_taken, i * (2 * SETS) + (layer * GBLOCKS + j + 1))
                            act.dma_start(one(g_dram, i * 2 + s),
                                          stage[:, s].rearrange("p k t -> p (k t)")).then_inc(g_stored[s], 16)

                rounds(act, GBLOCKS // (2 * SETS), with_table, peel=layer == 0)
                plain(0, UBLOCKS + GBLOCKS, TAIL)

                v0 = M0[f"v{layer}"]

                def sweep(i, j, more=True):
                    act.wait_ge(block_done, i * 8 + (v0 + j - 1))
                    act.wait_ge(w_ready, i * 8 + (layer * N_KEYS + j + 1))
                    nc.scalar.activation(g_hi[:, j % 2, :], wf[:, j % 2, :], ACT.Copy).then_inc(whi_ready, 1)
                    if more:
                        high(i, 8, v0 + j + LEAD)

                if layer == 0:
                    for j in range(8):
                        sweep(0, j)
                    conditioning(2)
                with act.Fori(1 - layer, N_KEYS // 8 - 1) as i:
                    for j in range(8):
                        sweep(i, j)
                for j in range(8):
                    sweep(N_KEYS // 8 - 1, j, more=layer == 0 or j + LEAD < 8)
                for k in range(KC):
                    act.wait_ge(x_ready, layer * KC + k + 1)
                    nc.scalar.activation(hf[:, k, :], x[:, k, :], ACT.Square).then_inc(sq_ready, 1)

            for layer in range(DEPTH):
                normalise(2 * layer)
                [attention, convolution][layer]()
                normalise(2 * layer + 1)
                scores(layer)
                experts(layer)
            normalise(2 * DEPTH)

        @block.vector
        def _(dve):
            order = [0]

            def settle(ins):
                order[0] += 1
                ins.then_inc(dve_order, 1)
                dve.wait_ge(dve_order, order[0])

            tt = nc.vector.tensor_tensor
            ts = nc.vector.tensor_scalar
            stt = nc.vector.scalar_tensor_tensor

            def broad(ap, shape, *axes):
                for a in axes:
                    ap = ap.unsqueeze(a)
                return ap.broadcast_to(shape)

            nc.vector.memset(ones[:, :], 1.0).then_inc(consts_ready, 1)
            nc.vector.memset(u_pad, 0.0).then_inc(pads_ready, 1)
            dve.wait_ge(first_loaded, 3 * 16)

            def mod_group(i, step, block, k, g):
                if k == 0 and g == 0:
                    since(dve, mod_ready, i * (step // MSLOTS) + block // MSLOTS)
                if g == 0:
                    dve.wait_ge(mod_raw[k], i * (16 * step // MSLOTS) + 16 * (block // MSLOTS + 1))
                since(dve, mod_summed, i * (2 * step) + (2 * (block + k) + g - 1))
                nc.vector.tensor_tensor_reduce(unread[:, g, :], mod_w[:, k, :], c_all[:, g, :], 1.0, 0.0,
                                               ALU.mult, ALU.add, accum_out=sums[:, k, g:g + 1]).then_inc(mod_summed, 1)

            def mod_bias(i, step, block):
                dve.wait_ge(mod_summed, i * (2 * step) + (2 * (block + MSLOTS)))
                at = bass.ds(i * step + block, MSLOTS)
                tt(mod[:, at, :], sums[:, :, :], broad(mod_b[:, at], [P, MSLOTS, 2], 2), ALU.add).then_inc(mod_ready, 1)

            def mod_four(i):
                for k in range(MSLOTS):
                    for g in range(2):
                        mod_group(i, MSLOTS, 0, k, g)
                mod_bias(i, MSLOTS, 0)

            def mod_scales(norms):
                for n in norms:
                    layer, which = NORMS[n]
                    at = (layer * 6 + 3 * which + 1) * KC
                    last = stt(scales[:, n], mod[:, at:at + KC, :], 1.0, broad(gains[:, n, :], [P, KC, 2], 2),
                               ALU.add, ALU.mult)
                last.then_inc(scales_ready, 1)

            parts = [0]

            def pipelined(first, second):
                for k in range(KC + 1):
                    if k < KC:
                        first(k)
                    if k:
                        second(k - 1)

            def inverse_root(n, width):
                v, r, t = (stat[:, s, 0:width] for s in (0, 2, 3))
                dve.wait_ge(std_ready, n + 1)
                settle(nc.vector.reciprocal(r, stat[:, 1, 0:width]))
                settle(stt(t, r, -0.5, r, ALU.mult, ALU.mult))
                settle(tt(t, t, v, ALU.mult))
                settle(stt(r, t, 1.5, r, ALU.add, ALU.mult))

            roots = [0]

            def scale_of(bank, width):
                ts(stat[:, 0, 0:width], ps[:, bank, 0:width], 1.0 / D, EPS, ALU.mult, ALU.add).then_inc(var_ready, 1)
                inverse_root(roots[0], width)
                roots[0] += 1

            def normalise(n):
                dve.wait_ge(stat_ready, n + 1)
                scale_of(ACC, T)
                r = stat[:, 2, 0:T]
                if n == 2 * DEPTH:
                    for k in range(KC):
                        stt(hf[:, k, :], x[:, k, :], gains[:, n, k:k + 1], r, ALU.mult, ALU.mult).then_inc(out_ready, 1)
                    return
                if n == 0:
                    dve.wait_ge(c_ready, 1)
                    rounds(dve, MOD_FIRST // MSLOTS, mod_four, peel=True)
                    dve.wait_ge(mod_ready, MOD_FIRST // MSLOTS)
                    mod_scales([0])
                dve.wait_ge(scales_ready, min(n, 2) + 1)
                layer, which = NORMS[n]

                def scaled(k):
                    for g, start, count in SEGS:
                        cols = slice(start, start + count)
                        last = stt(hf[:, k, cols], x[:, k, cols], scales[:, n, k, g:g + 1], r[:, cols], ALU.mult, ALU.mult)
                    last.then_inc(z_ready, 1)

                def low(k):
                    parts[0] += 1
                    dve.wait_ge(hi_part, parts[0])
                    for g, start, count in SEGS:
                        cols = slice(start, start + count)
                        last = stt(h_lo[:, k, cols], hf[:, k, cols], mod_col(layer, 3 * which, k, g),
                                   h_hi[:, k, cols].bitcast(F32), ALU.add, ALU.subtract)
                    last.then_inc(operand_ready, 1)

                pipelined(scaled, low)

            def low_operand(k):
                parts[0] += 1
                dve.wait_ge(hi_part, parts[0])
                tt(h_lo[:, k, :], hf[:, k, :], h_hi[:, k, :].bitcast(F32), ALU.subtract).then_inc(operand_ready, 1)

            def square(k):
                tt(hf[:, k, :], x[:, k, :], x[:, k, :], ALU.mult).then_inc(sq_ready, 1)

            def residual(name):
                for k in range(KC):
                    dve.wait_ge(proj_taken, R0[name] + k + 1)
                    settle(tt(x[:, k, :], x[:, k, :], hf[:, k, :], ALU.add))
                    square(k)

            def attention():
                with dve.Fori(MOD_FIRST // MSLOTS, (MOD_EARLY - 8) // MSLOTS) as i:
                    mod_four(i)
                dve.wait_ge(small_loaded, 16 * len(small))
                dve.wait_ge(turn_done, 1)
                rot = ps[:, ACC:ACC + 3, :].rearrange("p a b -> p (a b)")[:, 0:5 * LAT].rearrange(
                    "p (c t) -> p c t", c=5)
                tt(turned, rot, broad(sin, [P, 5, LAT], 1), ALU.mult)
                settle(tt(qk[:, :, CTX:T], qk[:, :, CTX:T], broad(cos, [P, 5, LAT], 1), ALU.mult))
                tt(qk[:, :, CTX:T], qk[:, :, CTX:T], turned, ALU.add).then_inc(roped, 1)

                dve.wait_ge(proj_taken, R0["in"] + 9)
                src, dst = u_pad, sum_a
                lo = 0
                for g, w in enumerate(POOL_SIZES):
                    half = w // 2
                    back, fore = (1, 0) if w == 2 else (half // 2, half // 2)
                    settle(tt(dst[:, g:NG, half:POOL_W - half + 1], src[:, g:NG, half - back:POOL_W - half + 1 - back],
                              src[:, g:NG, half + fore:POOL_W - half + 1 + fore], ALU.add))
                    for s, start, n in SEGS:
                        at = PAD * (s + 1) + start
                        settle(tt(pooled[:, g, start:start + n], dst[:, g, at:at + n], inv[:, g, start:start + n], ALU.mult))
                        last = tt(pooled[:, g, start:start + n], pooled[:, g, start:start + n],
                                  u_pad[:, g, at:at + n], ALU.subtract)
                    last.then_inc(pooled_ready, 1)
                    src, dst = dst, (sum_b if dst is sum_a else sum_a)

                def front(n):
                    b = n % 2
                    head = n // 2 + PAIRS * (n % 2)
                    dve.wait_ge(logits_done, n + 1)
                    if n >= 2:
                        dve.wait_ge(pt_done, n - 1)
                    bank = ACC + 2 * b
                    ts(logits[:, b, 0:CTX], ps[:, bank, 0:CTX], SCALE, None, ALU.mult)
                    stt(logits[:, b, CTX:CTX + T], ps[:, bank, CTX:CTX + T], SCALE, mask[:, 0, :], ALU.mult, ALU.add)
                    stt(logits[:, b, CTX + T:CTX + 2 * T], ps[:, bank + 1, 0:T], SCALE, mask[:, 1, :],
                        ALU.mult, ALU.add).then_inc(logits_read, 1)
                    dve.wait_ge(logits_read, n + 1)
                    nc.vector.tensor_reduce(sm[:, b, 0, 0:1], logits[:, b, 0:CTX], AX.X, ALU.max)
                    settle(nc.vector.tensor_reduce(sm[:, b, 0, 1:3], logits[:, b, CTX:].rearrange(
                        "p (a k) -> p a k", a=2), AX.X, ALU.max))
                    settle(ts(sm[:, b, 1, :], sm[:, b, 0, :], sink[:, head:head + 1], None, ALU.max))
                    ts(sm[:, b, 1, :], sm[:, b, 1, :], -1.0, None, ALU.mult).then_inc(max_ready, 1)

                def back(n):
                    b = n % 2
                    dve.wait_ge(exp_ready, n + 1)
                    settle(tt(sm[:, b, 4, :], sm[:, b, 2, :], sm[:, b, 3, :], ALU.add))
                    settle(nc.vector.reciprocal(sm[:, b, 4, :], sm[:, b, 4, :]))
                    start = 0
                    for piece, width in enumerate((CTX, T, T)):
                        part = logits[:, b, start:start + width]
                        last = ts(part, part, sm[:, b, 4, piece:piece + 1], None, ALU.mult)
                        start += width
                    last.then_inc(p_ready, 1)

                front(0)
                for n in range(1, N_HEADS):
                    front(n)
                    back(n - 1)
                back(N_HEADS - 1)
                for k in range(KC):
                    low_operand(k)
                with dve.Fori((MOD_EARLY - 8) // MSLOTS, MOD_EARLY // MSLOTS) as i:
                    mod_four(i)
                dve.wait_ge(mod_ready, MOD_EARLY // MSLOTS)
                mod_scales([1])
                residual("out")

            def convolution():
                def product(i, s):
                    dve.wait_ge(proj_taken, i * 4 + (R0["w1"] + 2 * s + 2))
                    for g, start, n in SEGS:
                        at = CPAD * (g + 1) + start
                        last = tt(a_pad[:, bass.ds(i * 2 + s, 1), at:at + n],
                                  glu[:, s, 0:1, start:start + n], glu[:, s, 1:2, start:start + n], ALU.mult)
                    last.then_inc(glu_out, 1)

                def taps(k, first, end):
                    if first == 0:
                        dve.wait_ge(glu_out, k + 1)
                    for j in range(first, end):
                        src = a_pad[:, bass.ds(k, 1), j:j + CONV_OUT]
                        out = odd[:, 0:1, :] if j % 2 else conv[:, bass.ds(k, 1), :]
                        w = dw[:, bass.ds(k, 1), j:j + 1].rearrange("p a b -> p (a b)")
                        if j == 1:
                            since(dve, conv_ready, k)
                        since(dve, tap_done, k * CONV_WIDTH + (j - 1))
                        if j == 0:
                            last = ts(out, src, w, cvecs[:, 0, bass.ds(k, 1)], ALU.mult, ALU.add)
                        elif j == 1:
                            last = ts(out, src, w, None, ALU.mult)
                        else:
                            last = stt(out, src, w, out, ALU.mult, ALU.add)
                        last.then_inc(tap_done, 1)

                def joined(k):
                    dve.wait_ge(tap_done, (k + 1) * CONV_WIDTH)
                    tt(conv[:, bass.ds(k, 1), :], conv[:, bass.ds(k, 1), :], odd[:, 0:1, :], ALU.add).then_inc(conv_ready, 1)

                def beside(i):
                    product(i, 0)
                    taps(i, 0, CONV_WIDTH // 2)
                    product(i, 1)
                    taps(i, CONV_WIDTH // 2, CONV_WIDTH)
                    joined(i)

                def alone(i):
                    taps(i, 0, CONV_WIDTH)
                    joined(i)

                rounds(dve, KC // 2, beside, peel=True)
                with dve.Fori(KC // 2, CONV_DVE) as i:
                    alone(i)
                dve.wait_ge(mean_done, 1)
                settle(ts(stat[:, 0, :], ps[:, ACC, 0:CONV_OUT], 1.0 / D, None, ALU.mult))
                for k in range(KC):
                    tt(conv[:, k, :], conv[:, k, :], stat[:, 0, :], ALU.subtract).then_inc(centred, 1)
                dve.wait_ge(mean_done, 2)
                scale_of(ACC + 1, CONV_OUT)

                def scaled(k):
                    tt(conv[:, k, :], conv[:, k, :], stat[:, 2, :], ALU.mult).then_inc(z_ready, 1)

                pipelined(scaled, low_operand)
                residual("w2")

            def top_keys(layer):
                dve.wait_ge(iota_ready, 2)
                key_u = key_us.bitcast(U32)
                for q in range(HS // 4):
                    dve.wait_ge(s_taken, layer * HS + 4 * (q + 1))
                    each = [(t, c) for t in range(NT) for c in range(4 * q, 4 * q + 4)]
                    for t, c in each:
                        last = nc.vector.max(vals[:, t, c, 0:8], s_all[:, t, c, :])
                    settle(last)
                    for t, c in each:
                        last = nc.vector.max_index(key_u[:, t, c, 0:8], vals[:, t, c, 0:8], s_all[:, t, c, :])
                    settle(last)
                    for t, c in each:
                        last = nc.vector.match_replace(s_all[:, t, c, :], vals[:, t, c, 0:8], s_all[:, t, c, :], LOWEST)
                    settle(last)
                    for t, c in each:
                        last = nc.vector.max(vals[:, t, c, 8:16], s_all[:, t, c, :])
                    settle(last)
                    for t, c in each:
                        last = nc.vector.max_index(key_u[:, t, c, 8:16], vals[:, t, c, 8:16], s_all[:, t, c, :])
                    settle(last)
                for t in range(NT):
                    val = vals[:, t]
                    nc.vector.tensor_copy(key_f, key_u[:, t])
                    pairs = val.rearrange("p (h s) k -> p h s k", s=2)
                    shape = [P, PEER_HEADS, TOPK, TOPK]
                    settle(tt(cand, broad(pairs[:, :, 0, :], shape, 3), broad(pairs[:, :, 1, :], shape, 2), ALU.add))
                    pos = pos_u.bitcast(U32)
                    flat = cand.rearrange("p h a b -> p h (a b)")
                    for h in range(PEER_HEADS):
                        last = nc.vector.max(top[:, h * TOPK:h * TOPK + 8], flat[:, h, :])
                    settle(last)
                    for h in range(PEER_HEADS):
                        last = nc.vector.max_index(pos[:, 0, h * TOPK:h * TOPK + 8], top[:, h * TOPK:h * TOPK + 8],
                                                   flat[:, h, :])
                    settle(last)
                    for h in range(PEER_HEADS):
                        last = nc.vector.match_replace(flat[:, h, :], top[:, h * TOPK:h * TOPK + 8], flat[:, h, :], LOWEST)
                    settle(last)
                    for h in range(PEER_HEADS):
                        last = nc.vector.max(top[:, h * TOPK + 8:(h + 1) * TOPK], flat[:, h, :])
                    settle(last)
                    for h in range(PEER_HEADS):
                        last = nc.vector.max_index(pos[:, 0, h * TOPK + 8:(h + 1) * TOPK],
                                                   top[:, h * TOPK + 8:(h + 1) * TOPK], flat[:, h, :])
                    settle(last)
                    ts(pos[:, 1, :], pos[:, 0, :], 4, None, ALU.logical_shift_right)
                    settle(ts(pos[:, 2, :], pos[:, 0, :], TOPK - 1, None, ALU.bitwise_and))
                    settle(nc.vector.tensor_copy(pos_f, pos[:, 1:3, :]))
                    keys_of = key_f.rearrange("p (h s) k -> p h s k", s=2)
                    hot = cand
                    for side in range(2):
                        rank = pos_f[:, side, :].rearrange("p (h k) -> p h k", h=PEER_HEADS)
                        iota = iota16[:, :].unsqueeze(1).unsqueeze(1).broadcast_to(shape)
                        settle(tt(hot, broad(rank, shape, 3), iota, ALU.is_equal))
                        settle(tt(hot, hot, broad(keys_of[:, :, side, :], shape, 2), ALU.mult))
                        settle(nc.vector.tensor_reduce(sel[:, 1 + side, t, :].rearrange("p (h k) -> p h k", h=PEER_HEADS),
                                                       hot, AX.X, ALU.add))
                    best = top.rearrange("p (h k) -> p h k", h=PEER_HEADS)
                    last = tt(sel[:, 0, t, :].rearrange("p (h k) -> p h k", h=PEER_HEADS), best,
                              best[:, :, 0:1].broadcast_to([P, PEER_HEADS, TOPK]), ALU.subtract)
                    if t < NT - 1:
                        settle(last)
                last.then_inc(top_ready, 1)
                dve.wait_ge(exp_done, layer + 1)
                e = sel[:, 3].rearrange("p n (h k) -> p (n h) k", k=TOPK)
                settle(nc.vector.tensor_reduce(gsum[:, 0, :], e, AX.X, ALU.add))
                settle(nc.vector.reciprocal(gsum[:, 1, :], gsum[:, 0, :]))
                tt(e, e, broad(gsum[:, 1, :], [P, NT * PEER_HEADS, TOPK], 2), ALU.mult).then_inc(sel_ready, 1)
                dve.wait_ge(cols_done, layer + 1)
                for s in range(2):
                    nc.vector.tensor_copy(col_key[:, s, :], ps[:, ACC + s, 0:T])
                g = ps[:, ACC + 2, 0:T]
                settle(nc.vector.tensor_copy(col_b, g))
                settle(nc.vector.tensor_copy(col_g[:, 0, :], col_b))
                settle(tt(col_g[:, 2, :], g, col_g[:, 0, :], ALU.subtract))
                settle(nc.vector.tensor_copy(col_b, col_g[:, 2, :]))
                settle(nc.vector.tensor_copy(col_g[:, 1, :], col_b))
                settle(tt(col_g[:, 2, :], col_g[:, 2, :], col_g[:, 1, :], ALU.subtract))

            def one_hots(layer):
                base = layer * GBLOCKS

                def table_rows(i):
                    for j in range(2 * SETS):
                        b = j % HOTS
                        since(dve, g_done, i * (2 * SETS) + (base + j - HOTS + 1))
                        for q in range(TOK):
                            tok = bass.ds(i * (2 * CHUNK) + (j * TOK + q), 1)
                            ts(oh2[:, b, q, :], iota_b[:, :], col_key[:, 1, tok], None, ALU.is_equal)
                            for part in range(3):
                                last = ts(oh1[:, b, part, q, :], iota_b[:, :], col_key[:, 0, tok],
                                          col_g[:, part, tok], ALU.is_equal, ALU.mult)
                        last.then_inc(hot_ready, 1)

                rounds(dve, GBLOCKS // (2 * SETS), table_rows, peel=layer == 0)

            def sweep(layer):
                base = layer * N_KEYS
                def eight(i, mods):
                    for j in range(8):
                        dve.wait_ge(a_loaded[j % 4], i * 32 + (16 * (base // 4 + j // 4 + 1)))
                        if j % 4 == 0:
                            dve.wait_ge(g_loaded[j // 4], i * 16 + 16 * (base // 8 + 1))
                        tt(wf[:, j % 2, :].rearrange("p (c t) -> p c t", t=CHUNK),
                           a_in[:, j % 4, :].rearrange("p (c t) -> p c t", t=CHUNK),
                           g_in[:, j // 4, :, (j % 4) * CHUNK:(j % 4 + 1) * CHUNK], ALU.mult).then_inc(w_ready, 1)
                        if mods:
                            mod_group(i, MSLOTS, MOD_EARLY - MSLOTS, j // 2, j % 2)
                        dve.wait_ge(whi_ready, i * 8 + (base + j + 1))
                        tt(g_lo[:, j % 2, :], wf[:, j % 2, :], g_hi[:, j % 2, :].bitcast(F32),
                           ALU.subtract).then_inc(wlo_ready, 1)
                    if mods:
                        mod_bias(i, MSLOTS, MOD_EARLY - MSLOTS)

                if layer == 0:
                    eight(0, False)
                    settle(nc.vector.memset(a_pad, 0.0))
                    dve.wait_ge(c_ready, 2)
                    for j in range(4):
                        dve.wait_ge(a_stored[j], 16 * (N_KEYS // 4))
                    with dve.Fori(1, MOD_ROUNDS + 1) as i:
                        eight(i, True)
                with dve.Fori(0 if layer else MOD_ROUNDS + 1, N_KEYS // 8) as i:
                    eight(i, False)
                if layer == 0:
                    dve.wait_ge(mod_ready, MOD_BLOCKS // MSLOTS)
                    at = (6 + 2) * KC
                    settle(tt(gb2[:, :, :], mod[:, at:at + KC, :], broad(cvecs[:, 3, :], [P, KC, 2], 2), ALU.mult))
                    mod_scales([2, 3])
                for k in range(KC):
                    if k < KC - 1:
                        dve.wait_ge(y_done, layer * (KC - 1) + k + 1)
                    else:
                        dve.wait_ge(block_done, M0[f"v{layer}"] + N_KEYS)
                    for g, start, n in SEGS:
                        cols = slice(start, start + n)
                        last = stt(x[:, k, cols], ps[:, (ACC + k) % 8, cols], mod_col(layer, 5, k, g), x[:, k, cols],
                                   ALU.mult, ALU.add)
                    last.then_inc(x_ready, 1)
                dve.wait_ge(x_ready, (layer + 1) * KC)

            for k in range(KC):
                square(k)
            for layer in range(DEPTH):
                normalise(2 * layer)
                [attention, convolution][layer]()
                normalise(2 * layer + 1)
                top_keys(layer)
                one_hots(layer)
                sweep(layer)
            normalise(2 * DEPTH)

        @block.tensor
        def _(pe):
            mm = nc.tensor.matmul
            pe.wait_ge(consts_ready, 1)

            operands = [0]

            def project(i, step, m, r, fresh=False):
                pe.wait_ge(lo_ready, i * step + (m + 1))
                if r >= 2:
                    pe.wait_ge(proj_taken, i * step + (r - 1))
                out, s = ps[:, PROJ + r % 2, 0:T], m % RING
                for k in range(KC):
                    if fresh:
                        operands[0] += 1
                        pe.wait_ge(operand_ready, operands[0])
                    cols = slice(k * P, (k + 1) * P)
                    mm(out, w_hi[:, s, cols], h_hi[:, k, :], start=k == 0, stop=False)
                    mm(out, w_hi[:, s, cols], h_lo[:, k, :], start=False, stop=False)
                    last = mm(out, w_lo[:, s, cols], h_hi[:, k, :], start=False, stop=k == KC - 1)
                last.then_inc(block_done, 1)

            def blocks(name):
                def four(i):
                    for j in range(4):
                        project(i, 4, M0[name] + j, R0[name] + j, fresh=isinstance(i, int) and i + j == 0)

                rounds(pe, dict(SEGMENTS)[name] // 4, four, peel=True)

            def column_sums(n):
                for k in range(KC):
                    pe.wait_ge(sq_ready, n * KC + k + 1)
                    last = mm(ps[:, ACC, 0:T], ones[:, :], hf[:, k, :], start=k == 0, stop=k == KC - 1)
                last.then_inc(stat_ready, 1)

            def attention():
                for c in range(9):
                    project(0, 0, M0["in"] + c, R0["in"] + c, fresh=c == 0)
                m, r = M0["in"] + 9, R0["in"] + 9
                pe.wait_ge(lo_ready, m + 1)
                pe.wait_ge(proj_taken, r - 1)
                for t in range(NT):
                    out = ps[:, PROJ + r % 2, t * P:(t + 1) * P]
                    rows = slice(t * P, (t + 1) * P)
                    for k in range(KC):
                        cols = slice(k * P, (k + 1) * P)
                        mm(out, h_hi[:, k, rows], w_hi[:, m % RING, cols], start=k == 0, stop=False)
                        mm(out, h_hi[:, k, rows], w_lo[:, m % RING, cols], start=False, stop=False)
                        last = mm(out, h_lo[:, k, rows], w_hi[:, m % RING, cols], start=False, stop=k == KC - 1)
                last.then_inc(block_done, 1)
                pe.wait_ge(small_loaded, 16 * len(small))
                pe.wait_ge(proj_taken, R0["in"] + 5)
                for c in range(5):
                    last = mm(ps[:, ACC + c // 2, (c % 2) * LAT:(c % 2 + 1) * LAT], turn[:, :], qk[:, c, CTX:T],
                              start=True, stop=True)
                last.then_inc(turn_done, 1)
                pe.wait_ge(proj_taken, R0["in"] + 10)
                pe.wait_ge(roped, 1)

                def scores_of(n):
                    c, kv = n // 2, n % 2
                    rows = slice(HEAD_DIM * kv, HEAD_DIM * (kv + 1))
                    if n >= 2:
                        pe.wait_ge(logits_read, n - 1)
                    bank = ACC + 2 * (n % 2)
                    mm(ps[:, bank, 0:CTX], qk[rows, c, 0:CTX], qk[rows, 4, 0:CTX], start=True, stop=True)
                    for b in range(2):
                        out = ps[:, bank, CTX:CTX + T] if b == 0 else ps[:, bank + 1, 0:T]
                        q = qk[rows, c, CTX + b * P:CTX + (b + 1) * P]
                        mm(out[:, 0:PAST], q, cache_k[rows, :], start=True, stop=True)
                        last = mm(out[:, PAST:], q, qk[rows, 4, CTX:T], start=True, stop=True)
                    last.then_inc(logits_done, 1)

                def values_of(n):
                    c, kv = n // 2, n % 2
                    rows = slice(HEAD_DIM * kv, HEAD_DIM * (kv + 1))
                    pe.wait_ge(p_ready, n + 1)
                    if n >= 1:
                        pe.wait_ge(pt_copied, n)
                    flat = ps[:, 6:8, :].rearrange("p a b -> p (a b)")
                    for s in range(7):
                        last = nc.tensor.transpose(flat[:, s * P:(s + 1) * P], logits[:, n % 2, s * P:(s + 1) * P],
                                                   ident[:, :])
                    last.then_inc(pt_done, 1)
                    pe.wait_ge(pt_copied, n + 1)
                    if kv == 0 and c >= 2:
                        pe.wait_ge(att_taken, c - 1)
                    lat = (cache_v[:, rows], v_nat[:, 1, rows], v_nat[:, 2, rows])
                    s = 0
                    for piece, vs in enumerate(((v_nat[:, 0, rows],), lat, lat)):
                        for a, v in enumerate(vs):
                            last = mm(ps[rows, PROJ + c % 2, piece * P:(piece + 1) * P], v, p_t[:, s * P:(s + 1) * P],
                                      start=a == 0, stop=a == len(vs) - 1)
                            s += 1
                    last.then_inc(att_done, 1)

                scores_of(0)
                for n in range(1, N_HEADS):
                    scores_of(n)
                    values_of(n - 1)
                values_of(N_HEADS - 1)
                pe.wait_ge(logits_read, N_HEADS)
                for g in range(NG):
                    pe.wait_ge(pooled_ready, g + 1)
                    mm(ps[:, ACC + g, 0:T], w_pool[:, g, :], pooled[:, g, :],
                       start=True, stop=True).then_inc(mixed_done, 1)
                blocks("out")

            def convolution():
                blocks("w1")
                for c in range(KC - CONV_DVE):
                    k = CONV_DVE + c
                    pe.wait_ge(glu_out, k + 1)
                    for j in range(CONV_WIDTH):
                        pe.wait_ge(diag_ready, c * CONV_WIDTH + j + 1)
                        last = mm(ps[:, ACC + 2 + c, 0:CONV_OUT], diag[:, j, :], a_pad[:, k, j:j + CONV_OUT],
                                  start=j == 0, stop=j == CONV_WIDTH - 1)
                        if j < CONV_WIDTH - 1:
                            last.then_inc(diag_used, 1)
                    last.then_inc(conv_done, 1)
                for n, k in enumerate([*range(CONV_DVE, KC), *range(CONV_DVE)]):
                    if k >= CONV_DVE:
                        pe.wait_ge(conv_taken, k - CONV_DVE + 1)
                    else:
                        pe.wait_ge(conv_ready, k + 1)
                    last = mm(ps[:, ACC, 0:CONV_OUT], ones[:, :], conv[:, k, :], start=n == 0, stop=n == KC - 1)
                last.then_inc(mean_done, 1)
                for k in range(KC):
                    pe.wait_ge(csq_ready, k + 1)
                    last = mm(ps[:, ACC + 1, 0:CONV_OUT], ones[:, :], conv_sq[:, k, :], start=k == 0, stop=k == KC - 1)
                last.then_inc(mean_done, 1)
                blocks("w2")

            def scores(layer):
                m0, r0 = M0[f"wq{layer}"], R0[f"wq{layer}"]
                pe.wait_ge(keys_loaded, 16 * (layer + 1))
                def queries(i):
                    def score(j):
                        pe.wait_ge(proj_taken, i * 4 + (r0 + j + 1))
                        if j == 0:
                            since(pe, s_taken, i * 4 + layer * HS)
                        for t in range(NT):
                            last = mm(ps[:, ACC + j, t * P:(t + 1) * P], ga[:, j, t * P:(t + 1) * P],
                                      keys[:, bass.ds(i * 4 + j, 1), :].rearrange("p a k -> p (a k)"),
                                      start=True, stop=True)
                        last.then_inc(s_done, 1)

                    project(i, 4, m0, r0, fresh=isinstance(i, int) and i == 0)
                    for j in range(1, 4):
                        project(i, 4, m0 + j, r0 + j)
                        score(j - 1)
                    score(3)

                rounds(pe, HS // 4, queries, peel=True)

            def experts(layer):
                m0, r0 = M0[f"u{layer}"], R0[f"u{layer}"]
                with pe.Fori(0, UBLOCKS // 4) as i:
                    for j in range(4):
                        project(i, 4, m0 + j, r0 + j)
                for j in range(UBLOCKS // 4 * 4, UBLOCKS):
                    project(0, 0, m0 + j, r0 + j)
                pe.wait_ge(sel_ready, layer + 1)
                for a, s in enumerate((1, 2, 3)):
                    for t in range(NT):
                        last = nc.tensor.transpose(ps[:, ACC + a, t * P:(t + 1) * P], sel[:, s, t, :], ident[:, :])
                last.then_inc(cols_done, 1)
                def with_table(i):
                    for j in range(2 * SETS):
                        project(i, 2 * SETS, m0 + UBLOCKS + j, r0 + UBLOCKS + j)
                        b = j % HOTS
                        base = layer * GBLOCKS + j
                        pe.wait_ge(hot_ready, i * (2 * SETS) + (base + 1))
                        since(pe, g_taken, i * (2 * SETS) + (base - HOTS + 1))
                        for q in range(TOK):
                            for part in range(3):
                                last = mm(ps[:, ACC + b, q * P:(q + 1) * P], oh2[:, b, q, :], oh1[:, b, part, q, :],
                                          start=part == 0, stop=part == 2)
                        last.then_inc(g_done, 1)

                rounds(pe, GBLOCKS // (2 * SETS), with_table, peel=layer == 0)
                for j in range(UBLOCKS + GBLOCKS, N_KEYS):
                    project(0, 0, m0 + j, r0 + j)
                pe.wait_ge(g_taken, (layer + 1) * GBLOCKS)
                v0 = M0[f"v{layer}"]

                def block_of(i, j, first=False, final=False):
                    s, b = (v0 + j) % RING, j % 2
                    pe.wait_ge(lo_ready, i * 8 + (v0 + j + 1))
                    pe.wait_ge(wlo_ready, i * 8 + (layer * N_KEYS + j + 1))
                    for k in range(KC):
                        if first and k == KC - ACC:
                            pe.wait_ge(proj_taken, r0 + N_KEYS)
                        cols = slice(k * P, (k + 1) * P)
                        out = ps[:, (ACC + k) % 8, 0:T]
                        mm(out, w_hi[:, s, cols], g_hi[:, b, :], start=first, stop=False)
                        mm(out, w_lo[:, s, cols], g_hi[:, b, :], start=False, stop=False)
                        last = mm(out, w_hi[:, s, cols], g_lo[:, b, :], start=False, stop=final)
                        if final and k < KC - 1:
                            last.then_inc(y_done, 1)
                    last.then_inc(block_done, 1)

                for j in range(8):
                    block_of(0, j, first=j == 0)
                with pe.Fori(1, N_KEYS // 8 - 1) as i:
                    for j in range(8):
                        block_of(i, j)
                for j in range(8):
                    block_of(N_KEYS // 8 - 1, j, final=j == 7)

            for layer in range(DEPTH):
                column_sums(2 * layer)
                [attention, convolution][layer]()
                column_sums(2 * layer + 1)
                scores(layer)
                experts(layer)
            column_sums(2 * DEPTH)


def laid_out(i):
    def chunks(w):
        rows, cols = w.shape
        return w.reshape(KC, P, cols // P, P).transpose(2, 1, 0, 3).reshape(cols // P, P, rows)

    def columns(v):
        return np.moveaxis(v.reshape(v.shape[:-1] + (KC, P)), -1, 0)

    heads = [h for c in range(PAIRS) for h in (c, c + PAIRS)]
    w_in = i["w_in"][0]
    q = w_in[:, :512].reshape(D, N_HEADS, HEAD_DIM)[:, heads].reshape(D, 512)
    w_in = np.concatenate([q, w_in[:, 512:640], w_in[:, 768:], w_in[:, 640:768]], 1)
    w_out = i["w_out"][0]
    w_out = np.concatenate([w_out[:512].reshape(N_HEADS, HEAD_DIM, D)[heads].reshape(512, D), w_out[512:]], 0)
    w1 = i["conv_w1"][0].reshape(D, 2, KC, P)[:, ::-1].transpose(0, 2, 1, 3).reshape(D, 2 * D)
    x = np.concatenate([i["x_prompt"][0], i["x_sample"][0]], 0)
    gains = np.stack([i["norm_mix_g"][0], i["norm_ffn_g"][0], i["norm_mix_g"][1], i["norm_ffn_g"][1], i["final_norm_g"]])
    a = {
        "x": x.T.reshape(KC, P, T).transpose(1, 0, 2),
        "c": np.tile(np.stack([i["c_ctx"], i["c"][0]])[None], (P, 1, 1)),
        "mod_b": columns(i["mod_b"].reshape(DEPTH, 6, D)).reshape(P, MOD_BLOCKS),
        "gains": columns(gains),
        "sink": np.tile(i["attn_sink"][0][None, :], (P, 1)),
        "pool_scale": i["pool_scale"][0].reshape(NG, P).T,
        "b1": columns(i["conv_b1"][0].reshape(2, D)).reshape(P, 2 * KC),
        "dw": i["conv_dw"][0].reshape(CONV_WIDTH, KC, P).transpose(2, 1, 0),
        "cvecs": columns(np.stack([i["conv_dw_b"][0], i["conv_ln_g"][0], i["conv_ln_b"][0], i["conv_b2"][0]])),
        "w_pool": i["w_pool"][0].transpose(1, 0, 2),
        "cache_k": i["cache_k"][0, 0].reshape(PAST, P).T,
        "cache_v": i["cache_v"][0, 0].reshape(PAST, P),
        "keys": i["peer_keys"].reshape(DEPTH, HS, N_KEYS, P).transpose(0, 3, 1, 2),
        "mod_w": i["mod_w"].transpose(0, 2, 1).reshape(MOD_BLOCKS, P, D),
        "in": chunks(w_in), "out": chunks(w_out), "w1": chunks(w1), "w2": chunks(i["conv_w2"][0]),
    }
    for layer in range(DEPTH):
        a[f"wq{layer}"] = chunks(i["peer_wq"][layer])
        a[f"u{layer}"] = i["peer_u"][layer].reshape(N_KEYS, P, KC, P).transpose(0, 3, 2, 1).reshape(N_KEYS, P, D)
        a[f"v{layer}"] = i["peer_v"][layer].reshape(N_KEYS, P, D)
    a.update(constants())
    return {n: np.ascontiguousarray(v) for n, v in a.items()}


OUTS = {"y": (P, KC, T), "state_k": (P, CTX), "state_v": (CTX, P)}


def kernel(**inputs):
    import concourse.bacc as bacc
    from concourse.bass_utils import run_bass_kernel_spmd

    arrays = laid_out({n: np.asarray(v) for n, v in inputs.items()})
    nc = bacc.Bacc("TRN2", target_bir_lowering=False, num_devices=1)
    io = {n: nc.dram_tensor(f"in_{n}", a.shape, mybir.dt.from_np(a.dtype), kind="ExternalInput").ap()
          for n, a in arrays.items()}
    for n, shape in OUTS.items():
        io[n] = nc.dram_tensor(f"out_{n}", shape, F32, kind="ExternalOutput").ap()
    build(nc, io)
    r = run_bass_kernel_spmd(nc, [{f"in_{n}": a for n, a in arrays.items()}], core_ids=[0]).results[0]
    y = r["out_y"].transpose(1, 0, 2).reshape(D, T).T
    state_k = r["out_state_k"].T.reshape(1, 1, CTX, 2, HEAD_DIM)
    state_v = r["out_state_v"].reshape(1, 1, CTX, 2, HEAD_DIM)
    return (np.ascontiguousarray(y[None, :CTX]), np.ascontiguousarray(y[None, CTX:]),
            np.ascontiguousarray(state_k), np.ascontiguousarray(state_v))
```

```python
from contextlib import ExitStack

import concourse.bass as bass
from concourse import mybir
import numpy as np

ALU = mybir.AluOpType
ACT = mybir.ActivationFunctionType
AX = mybir.AxisListType
F32 = mybir.dt.float32
F32R = mybir.dt.float32r
BF16 = mybir.dt.bfloat16
U32 = mybir.dt.uint32

P = 128
D = 1024
KC = D // P
CTX = 128
LAT = 256
T = CTX + LAT
NT = T // P
DEPTH = 2
EPS = 1e-6
NEG = -1e30
GRID_W = 64
HEAD_DIM = 64
N_HEADS = 8
PAIRS = N_HEADS // 2
SCALE = HEAD_DIM ** -0.5
WINDOW = 128
PAST = 128
ROW = CTX + 2 * (PAST + LAT)
POOL_SIZES = (2, 4, 8, 16)
NG = len(POOL_SIZES)
PAD = max(POOL_SIZES) // 2
POOL_W = PAD + CTX + PAD + LAT + PAD
CONV_WIDTH = 31
CPAD = CONV_WIDTH // 2
CONV_IN = CPAD + CTX + CPAD + LAT + CPAD
CONV_OUT = CONV_IN - 2 * CPAD
CONV_DVE = 6
N_KEYS = 128
PEER_HEADS = 8
HS = 2 * PEER_HEADS
TOPK = 16
LOWEST = -3.0e38

TOK = 4
CHUNK = 32
NCHUNK = T // CHUNK
GBLOCKS = T // TOK
TAIL = 4
UBLOCKS = N_KEYS - GBLOCKS - TAIL
QUAD = 4
HEAD = 2 * QUAD * CHUNK
HOTS = 4
SETS = CHUNK // TOK

WORK = 16600

RING = 4
LEAD = 2
MOD_BLOCKS = DEPTH * 6 * KC
SUM_BLOCKS = MOD_BLOCKS - KC
MSLOTS = 4
MOD_EARLY = 4 * KC
MOD_FIRST = KC
LATE_MODS = MOD_EARLY - 12
MOD_ROUNDS = (SUM_BLOCKS - MOD_EARLY) // MSLOTS

SEGMENTS = [("in", 10), ("out", 8), ("wq0", HS), ("u0", N_KEYS), ("v0", N_KEYS),
            ("w1", 16), ("w2", 8), ("wq1", HS), ("u1", N_KEYS), ("v1", N_KEYS)]
M0, R0 = {}, {}
_m = _r = 0
for _name, _count in SEGMENTS:
    M0[_name], R0[_name] = _m, _r
    _m += _count
    _r += 0 if _name[0] == "v" else _count
BLOCKS = _m
AHEAD = 10 + LEAD

SEGS = ((0, 0, CTX), (1, CTX, LAT))


def since(engine, semaphore, count):
    if isinstance(count, int) and count <= 0:
        return
    engine.wait_ge(semaphore, count)


def rounds(engine, count, body, peel=False):
    if peel:
        body(0)
    with engine.Fori(int(peel), count) as i:
        body(i)


def constants():
    quarter = HEAD_DIM // 4
    freqs = (np.float32(10000.0) ** (-np.arange(quarter, dtype=np.float32) / np.float32(quarter))).astype(np.float32)
    t = np.arange(LAT)
    rows = (t // GRID_W).astype(np.float32)[None, :] * freqs[:, None]
    cols = (t % GRID_W).astype(np.float32)[None, :] * freqs[:, None]
    ang = np.concatenate([rows, rows, cols, cols, rows, rows, cols, cols], 0).astype(np.float32)
    turn = np.zeros((P, P), np.float32)
    for base in range(0, P, 2 * quarter):
        for j in range(quarter):
            turn[base + quarter + j, base + j] = -1.0
            turn[base + j, base + quarter + j] = 1.0
    q = np.arange(P)[:, None]
    keys = np.arange(LAT)[None, :]
    mask = np.zeros((P, 2, PAST + LAT), np.float32)
    for b in range(2):
        mask[:, b, PAST:] = np.where(np.abs(q + b * P - keys) <= WINDOW, 0.0, NEG)
    inv = np.zeros((P, NG, T), np.float32)
    for g, w in enumerate(POOL_SIZES):
        for _, start, n in SEGS:
            s = np.arange(n)
            count = np.clip(s + (w - w // 2), 0, n) - np.clip(s - w // 2, 0, n)
            inv[:, g, start:start + n] = (np.float32(1.0) / count.astype(np.float32))[None, :]
    return {
        "c_cos": np.cos(ang).astype(np.float32), "c_sin": np.sin(ang).astype(np.float32), "c_turn": turn,
        "c_ident": np.eye(P, dtype=np.float32), "c_mask": mask, "c_inv": inv,
    }


def build(nc, io):
    ctx = ExitStack()
    with ctx:
        def sb(name, shape, dt=F32):
            return ctx.enter_context(nc.sbuf_tensor(name, shape, dt))

        def sem(name):
            return ctx.enter_context(nc.semaphore(name))

        x = sb("x", [P, KC, T])
        hf = sb("hf", [P, KC, T])
        h_hi = sb("h_hi", [P, KC, T], F32R)
        h_lo = sb("h_lo", [P, KC, T], F32R)
        raw = sb("raw", [P, RING, D])
        w_hi = sb("w_hi", [P, RING, D], F32R)
        w_lo = sb("w_lo", [P, RING, D], F32R)
        ga = sb("ga", [P, 4, T])
        g_hi = sb("g_hi", [P, 2, T], F32R)
        g_lo = sb("g_lo", [P, 2, T], F32R)
        hots = sb("hots", [P, HOTS * D])
        sums = sb("sums", [P, MSLOTS, 2])
        cvec = sb("cvec", [P, KC, 2])
        keys = sb("keys", [P, HS, N_KEYS])
        mod = sb("mod", [P, MOD_BLOCKS, 2])
        mod_b = sb("mod_b", [P, MOD_BLOCKS])
        gains = sb("gains", [P, 2 * DEPTH + 1, KC])
        scales = sb("scales", [P, 2 * DEPTH, KC, 2])
        sink = sb("sink", [P, N_HEADS])
        pool_scale = sb("pool_scale", [P, NG])
        b1 = sb("b1", [P, 2 * KC])
        dw = sb("dw", [P, KC, CONV_WIDTH])
        cvecs = sb("cvecs", [P, 4, KC])
        gb2 = sb("gb2", [P, KC, 2])
        turn = sb("turn", [P, P])
        ident = sb("ident", [P, P])
        ones = sb("ones", [P, P])
        iota_b = sb("iota_b", [P, P], BF16)
        iota16 = sb("iota16", [P, TOPK])
        unused = sb("unused", [P, 1])
        stat = sb("stat", [P, 4, CONV_OUT])
        work = sb("work", [P, WORK])
        ps = ctx.enter_context(nc.psum_tensor("ps", [P, 8, 512], F32))
        PROJ = 0
        ACC = 2

        oh2 = hots[:, 0:D].bitcast(BF16).rearrange("p (b q k) -> p b q k", b=HOTS, k=P)
        oh1 = hots[:, D:4 * D].bitcast(BF16).rearrange("p (b a q k) -> p b a q k", b=HOTS, a=3, k=P)
        diag = hots[:, 0:CONV_WIDTH * P].rearrange("p (j k) -> p j k", k=P)
        mod_w = hots[:, :].rearrange("p (s d) -> p s d", s=MSLOTS)
        c_all = keys[:, :, :].rearrange("p a k -> p (a k)").rearrange("p (g d) -> p g d", g=2)
        unread = ga[:, :, :].rearrange("p a t -> p (a t)")[:, 0:D].bitcast(BF16).rearrange("p (g d) -> p g d", g=2)

        place = [0]

        def region(*shape, at=None):
            if at is not None:
                place[0] = at
            n = int(np.prod(shape))
            v = work[:, place[0]:place[0] + n]
            place[0] += n
            assert place[0] <= WORK, place[0]
            names = "abcd"[:len(shape)]
            return v if len(shape) == 1 else v.rearrange(
                f"p ({' '.join(names)}) -> p {' '.join(names)}", **dict(zip(names, shape)))

        cos = region(LAT, at=0)
        sin = region(LAT)
        mask = region(2, PAST + LAT)
        inv = region(NG, T)
        w_pool = region(NG, P)
        cache_k = region(PAST)
        cache_v = region(P)
        qk_at = place[0]
        qk = region(5, T)
        turned = region(5, LAT)
        v_at = place[0]
        v_nat = region(NT, P)
        u_pad = region(NG, POOL_W)
        sums_at = place[0]
        sum_a = region(NG, POOL_W)
        sum_b = region(NG, POOL_W)
        idle = turned.rearrange("p c t -> p (c t)")
        logits = (region(ROW), region(ROW), idle[:, 0:ROW])
        p_t = ((region(512), region(ROW - 512)),
               (ga[:, :, :].rearrange("p a t -> p (a t)")[:, D:D + 512], idle[:, ROW:ROW + ROW - 512]))
        sm = region(3, 5, 3)
        pooled = region(NG, T)
        shift_w = [work[:, start + n * D:start + (n + 1) * D] for start, count in ((qk_at, 3), (sums_at, 5))
                   for n in range(count)]
        shift_rows = work[0:2, sums_at + 5 * D:sums_at + 6 * D]
        assert qk_at + 3 * D <= v_at and sums_at + 6 * D <= place[0]
        a_pad = region(KC, CONV_IN, at=0)
        conv = region(KC, CONV_OUT)
        conv_sq = region(KC, CONV_OUT)
        glu = region(2, 2, T)
        odd = region(2, CONV_OUT)
        stage = region(2, N_KEYS, CHUNK, at=0)
        s_all = region(NT, HS, N_KEYS, at=0)
        vals = region(NT, HS, TOPK)
        key_us = region(NT, HS, TOPK)
        key_f = region(HS // 2, TOPK)
        pos_u = region(3, P // 2)
        pos_f = region(2, P // 2)
        top = region(P // 2)
        after_topk = place[0]
        sel = region(4, NT, P, at=max(after_topk, 2 * N_KEYS * CHUNK))
        gsum = region(2, NT * PEER_HEADS)
        col_key = region(2, T)
        col_g = region(3, T)
        col_b = region(T // 2).bitcast(BF16)
        after_cols = place[0]
        cand = hf[:, :, :].rearrange("p k t -> p (k t)")[:, 0:PEER_HEADS // 2 * TOPK * TOPK].rearrange(
            "p (h a b) -> p h a b", a=TOPK, b=TOPK)
        g_in = region(2, NCHUNK, QUAD * CHUNK, at=after_cols)
        wf = region(2, T)
        a_in = region(4, T, at=2 * N_KEYS * CHUNK)

        small_loaded = sem("small_loaded")
        keys_loaded = sem("keys_loaded")
        first_loaded = sem("first_loaded")
        c_loaded = sem("c_loaded")
        mod_raw = [sem(f"mod_raw{j}") for j in range(MSLOTS)]
        raw_ready = [sem(f"raw_ready{j}") for j in range(RING)]
        consts_ready = sem("consts_ready")
        pads_ready = sem("pads_ready")
        iota_ready = sem("iota_ready")
        c_ready = sem("c_ready")
        shift_loaded = [sem(f"shift_loaded{k}") for k in range(KC)]
        shift_summed = sem("shift_summed")
        shift_copied = sem("shift_copied")
        shift_done = sem("shift_done")
        mod_summed = sem("mod_summed")
        mod_ready = sem("mod_ready")
        scales_ready = sem("scales_ready")
        hi_ready = sem("hi_ready")
        lo_ready = sem("lo_ready")
        block_done = sem("block_done")
        proj_taken = sem("proj_taken")
        sq_ready = sem("sq_ready")
        stat_ready = sem("stat_ready")
        var_ready = sem("var_ready")
        std_ready = sem("std_ready")
        z_ready = sem("z_ready")
        hi_part = sem("hi_part")
        operand_ready = sem("operand_ready")
        dve_order = sem("dve_order")
        act_order = sem("act_order")
        turn_done = sem("turn_done")
        v_done = sem("v_done")
        v_taken = sem("v_taken")
        roped = sem("roped")
        logits_done = sem("logits_done")
        max_ready = sem("max_ready")
        exp_ready = sem("exp_ready")
        logits_read = sem("logits_read")
        p_ready = sem("p_ready")
        pt_done = sem("pt_done")
        pt_copied = sem("pt_copied")
        att_done = sem("att_done")
        att_taken = sem("att_taken")
        window_done = sem("window_done")
        pooled_ready = sem("pooled_ready")
        mixed_done = sem("mixed_done")
        mixed_taken = sem("mixed_taken")
        state_out = sem("state_out")
        s_done = sem("s_done")
        s_taken = sem("s_taken")
        a_stored = [sem(f"a_stored{j}") for j in range(4)]
        top_ready = sem("top_ready")
        exp_done = sem("exp_done")
        sel_ready = sem("sel_ready")
        cols_done = sem("cols_done")
        hot_ready = sem("hot_ready")
        g_done = sem("g_done")
        g_taken = sem("g_taken")
        g_begun = [sem(f"g_begun{j}") for j in range(2)]
        g_stored = [sem(f"g_stored{j}") for j in range(2)]
        a_loaded = [sem(f"a_loaded{j}") for j in range(4)]
        g_loaded = [sem(f"g_loaded{j}") for j in range(2)]
        w_ready = sem("w_ready")
        whi_ready = sem("whi_ready")
        wlo_ready = sem("wlo_ready")
        y_done = sem("y_done")
        x_ready = sem("x_ready")
        glu_out = sem("glu_out")
        tap_done = sem("tap_done")
        conv_ready = sem("conv_ready")
        diag_ready = sem("diag_ready")
        diag_used = sem("diag_used")
        conv_done = sem("conv_done")
        conv_taken = sem("conv_taken")
        mean_done = sem("mean_done")
        centred = sem("centred")
        csq_ready = sem("csq_ready")
        out_ready = sem("out_ready")
        out_stored = sem("out_stored")

        a_dram = nc.dram_tensor("a_dram", (N_KEYS, P, T), F32).ap()
        g_dram = nc.dram_tensor("g_dram", (NCHUNK, P, N_KEYS * CHUNK), F32).ap()
        g_quads = g_dram.rearrange("c p (q i t) -> p q c (i t)", i=QUAD, t=CHUNK)

        def one(ap, n):
            return ap[bass.ds(n, 1)].rearrange("a p n -> (a p) n")

        def mod_col(layer, part, k, group):
            return mod[:, (layer * 6 + part) * KC + k, group:group + 1]

        NORMS = [(l, w) for l in range(DEPTH) for w in range(2)]

        small = [
            (sink[:, :], io["sink"]), (pool_scale[:, :], io["pool_scale"]),
            (b1[:, :], io["b1"]), (dw[:, :, :], io["dw"]), (cvecs[:, :, :], io["cvecs"]),
            (turn[:, :], io["c_turn"]), (cos, io["c_cos"]), (sin, io["c_sin"]),
            (mask, io["c_mask"]), (inv, io["c_inv"]), (w_pool, io["w_pool"]), (cache_k, io["cache_k"]),
            (cache_v, io["cache_v"]),
        ]

        block = ctx.enter_context(nc.Block())

        @block.sync
        def _(sp):
            def conditioning():
                sp.dma_start(c_all, io["c"]).then_inc(c_loaded, 16)

            def mod_load(n):
                if n >= MSLOTS:
                    sp.wait_ge(mod_summed, 2 * (n - MSLOTS + 1))
                sp.dma_start(mod_w[:, n % MSLOTS, :], one(io["mod_w"], n)).then_inc(mod_raw[n % MSLOTS], 16)

            def load(name, n, m_mod):
                sp.dma_start(raw[:, m_mod % RING, :], one(io[name], n)).then_inc(raw_ready[m_mod % RING], 16)

            def stream(name, first, count, body):
                m0 = M0[name] + first
                if count == body:
                    for j in range(body):
                        sp.wait_ge(lo_ready, m0 + j - RING + 1)
                        load(name, first + j, m0 + j)
                    return
                with sp.Fori(0, count // body) as i:
                    for j in range(body):
                        sp.wait_ge(lo_ready, i * body + (m0 + j - RING + 1))
                        load(name, i * body + (first + j), m0 + j)

            def mod_load_late(k):
                sp.dma_start(mod_w[:, k, :], one(io["mod_w"], MOD_EARLY + k)).then_inc(mod_raw[k], 16)

            for dst, src in ((x[:, :, :], io["x"]), (mod_b[:, :], io["mod_b"]), (gains[:, :, :], io["gains"]),
                             (ident[:, :], io["c_ident"]), (cvec[:, :, :], io["c_cols"])):
                sp.dma_start(dst, src).then_inc(first_loaded, 16)
            conditioning()
            for k in range(KC):
                if k % 4 == 3:
                    load("in", k // 4, k // 4)
                sp.dma_start(shift_w[k], one(io["shift_w"], k)).then_inc(shift_loaded[k], 16)
                mod_load(k)
            load("in", 2, 2)
            load("in", 3, 3)
            for dst, src in small:
                sp.dma_start(dst, src).then_inc(small_loaded, 16)
            n = MOD_FIRST
            for m in range(RING, 10):
                for _ in range(2):
                    mod_load(n)
                    n += 1
                stream("in", m, 1, 1)
            for m in range(RING):
                if n < MOD_EARLY - 8:
                    mod_load(n)
                    n += 1
                stream("out", m, 1, 1)
            while n < MOD_EARLY - 4:
                mod_load(n)
                n += 1
            for m in range(RING):
                stream("out", RING + m, 1, 1)
                mod_load(n + m)

            for layer in range(DEPTH):
                stream(f"wq{layer}", 0, RING, RING)
                if layer == 0:
                    sp.wait_ge(mod_summed, 2 * MOD_EARLY)
                    sp.dma_start(keys[:, :, :], io["keys"][0]).then_inc(keys_loaded, 16)
                stream(f"wq{layer}", RING, HS - RING, 4)
                stream(f"u{layer}", 0, N_KEYS, 4)
                name, v0 = f"v{layer}", M0[f"v{layer}"]
                after = ["w1", None][layer]
                stream(name, 0, RING, RING)
                sp.wait_ge(cols_done, layer + 1)
                for j in range(4):
                    sp.wait_ge(a_stored[j], 16 * (layer * (N_KEYS // 4) + 1))
                    sp.dma_start(a_in[:, j, :], one(a_dram, j)).then_inc(a_loaded[j], 16)
                for s in range(2):
                    sp.wait_ge(g_begun[s], 16 * (layer + 1) * (NCHUNK // 2))
                for s in range(2):
                    sp.dma_start(g_in[:, s], g_quads[:, s]).then_inc(g_loaded[s], 16)
                for s in range(2):
                    sp.wait_ge(g_stored[s], 16 * (layer + 1) * (NCHUNK // 2))
                for j in range(4):
                    sp.wait_ge(a_stored[j], 16 * (layer + 1) * (N_KEYS // 4))
                if layer == 0:
                    sp.wait_ge(s_done, HS)
                    conditioning()
                    for k in range(MSLOTS):
                        mod_load_late(k)

                def beside(i, j, more):
                    sp.wait_ge(lo_ready, i * 8 + (v0 + j + 1))
                    if more or j < 8 - RING:
                        load(name, i * 8 + (j + RING), v0 + j)
                    elif after:
                        load(after, j - (8 - RING), v0 + j)
                    if more or j < 4:
                        sp.wait_ge(w_ready, i * 8 + (layer * N_KEYS + j + 1))
                        sp.dma_start(a_in[:, j % 4, :], one(a_dram, i * 8 + (j + 4))).then_inc(a_loaded[j % 4], 16)
                    if more and j % 4 == 3:
                        s = j // 4
                        sp.dma_start(g_in[:, s].unsqueeze(1),
                                     g_quads[:, bass.ds(i * 2 + (s + 2), 1)]).then_inc(g_loaded[s], 16)

                if layer == 0:
                    for j in range(8):
                        beside(0, j, True)
                    with sp.Fori(1, MOD_ROUNDS) as i:
                        for j in range(8):
                            beside(i, j, True)
                            if j % 2:
                                sp.wait_ge(mod_summed, i * 8 + (2 * MOD_EARLY - 8 + j + 1))
                                sp.dma_start(mod_w[:, j // 2, :], one(io["mod_w"], i * MSLOTS + (MOD_EARLY + j // 2))
                                             ).then_inc(mod_raw[j // 2], 16)
                with sp.Fori(0 if layer else MOD_ROUNDS, N_KEYS // 8 - 1) as i:
                    for j in range(8):
                        beside(i, j, True)
                for j in range(8):
                    if j < 8 - RING or after:
                        beside(N_KEYS // 8 - 1, j, False)
                if layer == 0:
                    sp.wait_ge(mod_summed, 2 * SUM_BLOCKS)
                    sp.dma_start(keys[:, :, :], io["keys"][1]).then_inc(keys_loaded, 16)
                    stream("w1", RING, 16 - RING, 4)
                    stream("w2", 0, 8, 4)

            for k in range(0, KC, 2):
                sp.wait_ge(out_ready, k + 2)
                sp.dma_start(io["y"][:, k:k + 2], hf[:, k:k + 2, :]).then_inc(out_stored, 16)
            sp.wait_ge(out_stored, 16 * KC // 2)
            sp.wait_ge(state_out, 32)

        @block.gpsimd
        def _(pool):
            nc.gpsimd.iota(iota_b[:, :], pattern=[[1, P]], base=0, channel_multiplier=0,
                           allow_small_or_imprecise_dtypes=True).then_inc(iota_ready, 1)
            nc.gpsimd.iota(iota16[:, :], pattern=[[1, TOPK]], base=0, channel_multiplier=0,
                           allow_small_or_imprecise_dtypes=True).then_inc(iota_ready, 1)

            def low(m, j):
                pool.wait_ge(hi_ready, m + 1)
                nc.gpsimd.tensor_tensor(w_lo[:, j % RING, :], raw[:, j % RING, :],
                                        w_hi[:, j % RING, :].bitcast(F32), ALU.subtract).then_inc(lo_ready, 1)

            for m in range(AHEAD):
                low(m, m)
            pool.wait_ge(small_loaded, 16 * len(small))
            pool.wait_ge(proj_taken, R0["in"] + 9)
            steps = [0]

            def settle(ins):
                steps[0] += 1
                ins.then_inc(window_done, 1)
                pool.wait_ge(window_done, steps[0])

            tt = nc.gpsimd.tensor_tensor
            src, dst = u_pad, sum_a
            for g, w in enumerate(POOL_SIZES):
                half = w // 2
                back, fore = (1, 0) if w == 2 else (half // 2, half // 2)
                settle(tt(dst[:, g:NG, half:POOL_W - half + 1], src[:, g:NG, half - back:POOL_W - half + 1 - back],
                          src[:, g:NG, half + fore:POOL_W - half + 1 + fore], ALU.add))
                for s, start, n in SEGS:
                    at = PAD * (s + 1) + start
                    last = tt(pooled[:, g, start:start + n], dst[:, g, at:at + n], inv[:, g, start:start + n], ALU.mult)
                settle(last)
                for s, start, n in SEGS:
                    at = PAD * (s + 1) + start
                    last = tt(pooled[:, g, start:start + n], pooled[:, g, start:start + n],
                              u_pad[:, g, at:at + n], ALU.subtract)
                last.then_inc(pooled_ready, 1)
                src, dst = dst, (sum_b if dst is sum_a else sum_a)

            with pool.Fori(0, (BLOCKS - AHEAD) // 8) as i:
                for j in range(8):
                    low(i * 8 + (AHEAD + j), j)
            for m in range((BLOCKS - AHEAD) // 8 * 8 + AHEAD, BLOCKS):
                low(m, m)

        @block.scalar
        def _(act):
            order = [0]

            def settle(ins):
                order[0] += 1
                ins.then_inc(act_order, 1)
                act.wait_ge(act_order, order[0])

            def high(i, step, m, wait_free=True):
                count = i * (16 * step // RING) + 16 * (m // RING + 1)
                act.wait_ge(raw_ready[m % RING], count)
                if wait_free:
                    act.wait_ge(block_done, i * step + (m - RING + 1))
                nc.scalar.activation(w_hi[:, m % RING, :], raw[:, m % RING, :], ACT.Copy).then_inc(hi_ready, 1)

            def ahead(i, step, m):
                if m + LEAD < BLOCKS:
                    high(i, step, m + LEAD, wait_free=m + LEAD >= RING)

            def projected(i, step, m):
                act.wait_ge(block_done, i * step + (m + 1))

            def conditioning(n):
                act.wait_ge(c_loaded, 16 * n)
                nc.scalar.activation(c_all, c_all, ACT.Silu).then_inc(c_ready, 1)

            act.wait_ge(consts_ready, 1)
            act.wait_ge(first_loaded, 5 * 16)
            nc.scalar.activation(cvec[:, :, :], cvec[:, :, :], ACT.Silu).then_inc(c_ready, 1)
            conditioning(1)
            roots = [0]

            def preload(function):
                nc.scalar.activation(unused[:, :], ones[:, 0:1], function)

            def root(width):
                roots[0] += 1
                preload(ACT.Ln)
                act.wait_ge(var_ready, roots[0])
                settle(nc.scalar.activation(stat[:, 1, 0:width], stat[:, 0, 0:width], ACT.Ln))
                nc.scalar.activation(stat[:, 2, 0:width], stat[:, 1, 0:width], ACT.Exp, scale=-0.5).then_inc(std_ready, 1)

            def normalise(n):
                root(T)
                if n == 0:
                    for m in range(LEAD):
                        high(0, 0, m, wait_free=False)
                    act.wait_ge(shift_summed, 1)
                    nc.scalar.activation(shift_rows, ps[0:2, ACC + 2:ACC + 4, :].rearrange("p a b -> p (a b)"),
                                         ACT.Copy).then_inc(shift_copied, 1)
                if n == 2 * DEPTH:
                    return
                layer, which = NORMS[n]
                for k in range(KC):
                    act.wait_ge(z_ready, (n + n // 3) * KC + k + 1)
                    for g, start, count in SEGS:
                        last = nc.scalar.activation(h_hi[:, k, start:start + count], hf[:, k, start:start + count],
                                                    ACT.Identity, bias=mod_col(layer, 3 * which, k, g))
                    last.then_inc(hi_part, 1)

            def high_operand(k):
                nc.scalar.activation(h_hi[:, k, :], hf[:, k, :], ACT.Copy).then_inc(hi_part, 1)

            def gated(name, layer, part):
                m0 = M0[name]
                act.wait_ge(mod_ready, [MOD_EARLY - 2 * KC, SUM_BLOCKS][layer] // MSLOTS)
                with act.Fori(0, 2) as i:
                    for j in range(4):
                        ahead(i, 4, m0 + j)
                        projected(i, 4, m0 + j)
                        for g, start, n in SEGS:
                            k = i * 4 + j
                            col = bass.ds(i * 4 + ((layer * 6 + part) * KC + j), 1)
                            bias = gb2[:, bass.ds(k, 1), g:g + 1].rearrange("p a b -> p (a b)") if name == "w2" else 0.0
                            last = nc.scalar.activation(
                                hf[:, bass.ds(k, 1), start:start + n],
                                ps[:, PROJ + (R0[name] + j) % 2, start:start + n].unsqueeze(1), ACT.Identity,
                                scale=mod[:, col, g:g + 1].rearrange("p a b -> p (a b)"), bias=bias)
                        last.then_inc(proj_taken, 1)

            def attention():
                act.wait_ge(small_loaded, 16 * len(small))
                def exponentials(n):
                    b = n % 3
                    head = n // 2 + PAIRS * (n % 2)
                    act.wait_ge(max_ready, n + 1)
                    start = 0
                    for piece, width in enumerate((CTX, T, T)):
                        part = logits[b][:, start:start + width]
                        nc.scalar.activation(part, part, ACT.Exp, bias=sm[:, b, 1, piece:piece + 1],
                                             accum_out=sm[:, b, 2, piece:piece + 1])
                        start += width
                    nc.scalar.activation(sm[:, b, 3, :], sm[:, b, 1, :], ACT.Exp,
                                         bias=sink[:, head:head + 1]).then_inc(exp_ready, 1)

                for c in range(10):
                    ahead(0, 0, M0["in"] + c)
                    if c == 9:
                        preload(ACT.Exp)
                        exponentials(0)
                        exponentials(1)
                    if c == 0:
                        act.wait_ge(pads_ready, 1)
                    projected(0, 0, M0["in"] + c)
                    src = ps[:, PROJ + (R0["in"] + c) % 2, :]
                    if c < 5:
                        last = nc.scalar.activation(qk[:, c, :], src[:, 0:T], ACT.Copy)
                    elif c < 9:
                        for g, start, n in SEGS:
                            at = PAD * (g + 1) + start
                            last = nc.scalar.activation(u_pad[:, c - 5, at:at + n], src[:, start:start + n], ACT.Copy)
                    else:
                        last = nc.scalar.activation(hf[:, 0, :], src[:, 0:T], ACT.Copy)
                    last.then_inc(proj_taken, 1)
                act.wait_ge(v_done, 1)
                nc.scalar.activation(v_nat.rearrange("p n d -> p (n d)"), ps[:, PROJ, 0:T], ACT.Copy).then_inc(v_taken, 1)
                act.wait_ge(v_taken, 1)
                act.dma_start(io["state_k"], qk[:, 4, 0:CTX]).then_inc(state_out, 16)
                act.dma_start(io["state_v"], v_nat[:, 0, :]).then_inc(state_out, 16)

                def transposed(n):
                    act.wait_ge(pt_done, n + 1)
                    if n >= 2:
                        act.wait_ge(att_done, n - 1)
                    first, rest = p_t[n % 2]
                    nc.scalar.activation(first, ps[:, 6, :], ACT.Copy)
                    nc.scalar.activation(rest, ps[:, 7, 0:ROW - 512], ACT.Copy).then_inc(pt_copied, 1)

                def pair(c):
                    act.wait_ge(att_done, 2 * c + 2)
                    nc.scalar.activation(hf[:, c, :], ps[:, PROJ + c % 2, 0:T], ACT.Copy).then_inc(att_taken, 1)
                    act.wait_ge(att_taken, c + 1)
                    high_operand(c)

                def mixed(g):
                    act.wait_ge(mixed_done, g + 1)
                    nc.scalar.activation(hf[:, PAIRS + g, :], ps[:, PROJ + 1, 0:T], ACT.Identity,
                                         scale=pool_scale[:, g:g + 1]).then_inc(mixed_taken, 1)
                    act.wait_ge(mixed_taken, g + 1)
                    high_operand(PAIRS + g)

                for n in range(N_HEADS):
                    if n in (1, 2):
                        mixed(2 * (n - 1))
                        mixed(2 * (n - 1) + 1)
                    if n >= 2 and n % 2 == 0:
                        pair(n // 2 - 1)
                    transposed(n)
                    if n + 2 < N_HEADS:
                        exponentials(n + 2)
                pair(PAIRS - 1)
                gated("out", 0, 2)

            def convolution():
                def gates(i):
                    for j in range(4):
                        ahead(i, 4, M0["w1"] + j)
                        projected(i, 4, M0["w1"] + j)
                        src = ps[:, PROJ + (R0["w1"] + j) % 2, 0:T]
                        s = j // 2
                        if j % 2 == 0:
                            since(act, glu_out, i * 2)
                            nc.scalar.activation(glu[:, s, 0, :], src, ACT.Sigmoid,
                                                 bias=b1[:, bass.ds(i * 2 + (KC + s), 1)]).then_inc(proj_taken, 1)
                        else:
                            nc.scalar.activation(glu[:, s, 1, :], src, ACT.Identity,
                                                 bias=b1[:, bass.ds(i * 2 + s, 1)]).then_inc(proj_taken, 1)

                rounds(act, 4, gates, peel=True)
                for c in range(KC - CONV_DVE):
                    for j in range(CONV_WIDTH):
                        if c and j < CONV_WIDTH - 1:
                            act.wait_ge(diag_used, (c - 1) * (CONV_WIDTH - 1) + j + 1)
                        elif c:
                            act.wait_ge(conv_done, c)
                        nc.scalar.activation(diag[:, j, :], ident[:, :], ACT.Copy,
                                             scale=dw[:, CONV_DVE + c, j:j + 1]).then_inc(diag_ready, 1)
                for c in range(KC - CONV_DVE):
                    k = CONV_DVE + c
                    act.wait_ge(conv_done, c + 1)
                    nc.scalar.activation(conv[:, k, :], ps[:, ACC + 2 + c, 0:CONV_OUT], ACT.Identity,
                                         bias=cvecs[:, 0, k:k + 1]).then_inc(conv_taken, 1)
                for k in range(KC):
                    act.wait_ge(centred, k + 1)
                    nc.scalar.activation(conv_sq[:, k, :], conv[:, k, :], ACT.Square).then_inc(csq_ready, 1)
                root(CONV_OUT)
                for k in range(KC):
                    act.wait_ge(z_ready, 2 * KC + KC + k + 1)
                    for g, start, n in SEGS:
                        at = start + g * CPAD
                        last = nc.scalar.activation(hf[:, k, start:start + n], conv[:, k, at:at + n], ACT.Silu,
                                                    scale=cvecs[:, 1, k:k + 1], bias=cvecs[:, 2, k:k + 1])
                    settle(last)
                    high_operand(k)
                gated("w2", 1, 2)

            def scores(layer):
                m0, r0 = M0[f"wq{layer}"], R0[f"wq{layer}"]
                for j in range(4 if layer else 0):
                    act.wait_ge(a_stored[j], 16 * (N_KEYS // 4))
                if layer == 0:
                    act.wait_ge(state_out, 32)
                def queries(i):
                    def query(j):
                        ahead(i, 4, m0 + j)
                        projected(i, 4, m0 + j)
                        if j == 0:
                            since(act, s_done, i * 4 + layer * HS)
                        nc.scalar.activation(ga[:, j, :], ps[:, PROJ + (r0 + j) % 2, 0:T],
                                             ACT.Copy).then_inc(proj_taken, 1)

                    def take(j):
                        act.wait_ge(s_done, i * 4 + (layer * HS + j + 1))
                        nc.scalar.activation(
                            s_all[:, :, bass.ds(i * 4 + j, 1), :].rearrange("p n a k -> p n (a k)"),
                            ps[:, ACC + j, 0:T].rearrange("p (n k) -> p n k", n=NT), ACT.Copy).then_inc(s_taken, 1)

                    query(0)
                    query(1)
                    take(0)
                    query(2)
                    take(1)
                    query(3)
                    take(2)
                    take(3)

                rounds(act, HS // 4, queries, peel=layer == 0)

            def gelu(layer, i, step, m, r, count):
                j = count % 4
                projected(i, step, m)
                since(act, a_stored[j], i * (4 * step) + 16 * (layer * N_KEYS // 4 + count // 4))
                nc.scalar.activation(ga[:, j, :], ps[:, PROJ + r % 2, 0:T], ACT.Gelu).then_inc(proj_taken, 1)
                act.wait_ge(proj_taken, i * step + (r + 1))
                act.dma_start(one(a_dram, i * step + count), ga[:, j, :]).then_inc(a_stored[j], 16)

            def experts(layer):
                m0, r0 = M0[f"u{layer}"], R0[f"u{layer}"]
                def plain(i, first=0, count=4):
                    for j in range(first, first + count):
                        ahead(i, 4, m0 + j)
                        gelu(layer, i, 4, m0 + j, r0 + j, j)

                rounds(act, UBLOCKS // 4 - 1, plain, peel=layer == 0)
                plain(0, UBLOCKS - 4, 3)
                act.wait_ge(top_ready, layer + 1)
                nc.scalar.activation(sel[:, 3], sel[:, 0], ACT.Exp).then_inc(exp_done, 1)
                plain(0, UBLOCKS - 1, 1)

                def with_table(i):
                    for j in range(2 * SETS):
                        b = UBLOCKS + j
                        ahead(i, 2 * SETS, m0 + b)
                        gelu(layer, i, 2 * SETS, m0 + b, r0 + b, b)
                        s = j // SETS
                        if j % SETS == 0:
                            since(act, g_begun[s], i * 16 + layer * 16 * (NCHUNK // 2))
                            since(act, g_stored[s], i * 16 + layer * 16 * (NCHUNK // 2))
                        act.wait_ge(g_done, i * (2 * SETS) + (layer * GBLOCKS + j + 1))
                        tok = (j % SETS) * TOK
                        nc.scalar.activation(
                            stage[:, s, :, tok:tok + TOK].rearrange("p k t -> p t k"),
                            ps[:, ACC + j % HOTS, :].rearrange("p (t k) -> p t k", k=N_KEYS), ACT.Copy).then_inc(g_taken, 1)
                        if j % SETS == SETS - 1:
                            act.wait_ge(g_taken, i * (2 * SETS) + (layer * GBLOCKS + j + 1))
                            flat = stage[:, s].rearrange("p k t -> p (k t)")
                            chunk = one(g_dram, i * 2 + s)
                            act.dma_start(chunk[:, 0:HEAD], flat[:, 0:HEAD]).then_inc(g_begun[s], 16)
                            act.dma_start(chunk[:, HEAD:], flat[:, HEAD:]).then_inc(g_stored[s], 16)

                rounds(act, GBLOCKS // (2 * SETS), with_table, peel=layer == 0)
                plain(0, UBLOCKS + GBLOCKS, TAIL)

                v0 = M0[f"v{layer}"]

                def sweep(i, j, more=True):
                    act.wait_ge(block_done, i * 8 + (v0 + j - 1))
                    act.wait_ge(w_ready, i * 8 + (layer * N_KEYS + j + 1))
                    nc.scalar.activation(g_hi[:, j % 2, :], wf[:, j % 2, :], ACT.Copy).then_inc(whi_ready, 1)
                    if more:
                        high(i, 8, v0 + j + LEAD)

                if layer == 0:
                    for j in range(8):
                        sweep(0, j)
                    conditioning(2)
                with act.Fori(1 - layer, N_KEYS // 8 - 1) as i:
                    for j in range(8):
                        sweep(i, j)
                for j in range(8):
                    sweep(N_KEYS // 8 - 1, j, more=layer == 0 or j + LEAD < 8)
                for k in range(KC):
                    act.wait_ge(x_ready, layer * KC + k + 1)
                    nc.scalar.activation(hf[:, k, :], x[:, k, :], ACT.Square).then_inc(sq_ready, 1)

            for layer in range(DEPTH):
                normalise(2 * layer)
                [attention, convolution][layer]()
                normalise(2 * layer + 1)
                scores(layer)
                experts(layer)
            normalise(2 * DEPTH)

        @block.vector
        def _(dve):
            order = [0]

            def settle(ins):
                order[0] += 1
                ins.then_inc(dve_order, 1)
                dve.wait_ge(dve_order, order[0])

            tt = nc.vector.tensor_tensor
            ts = nc.vector.tensor_scalar
            stt = nc.vector.scalar_tensor_tensor

            def broad(ap, shape, *axes):
                for a in axes:
                    ap = ap.unsqueeze(a)
                return ap.broadcast_to(shape)

            nc.vector.memset(ones[:, :], 1.0).then_inc(consts_ready, 1)
            nc.vector.memset(u_pad, 0.0).then_inc(pads_ready, 1)
            dve.wait_ge(first_loaded, 5 * 16)

            def mod_group(i, step, block, k, g):
                if k == 0 and g == 0:
                    since(dve, mod_ready, i * (step // MSLOTS) + block // MSLOTS)
                if g == 0:
                    dve.wait_ge(mod_raw[k], i * (16 * step // MSLOTS) + 16 * (block // MSLOTS + 1))
                since(dve, mod_summed, i * (2 * step) + (2 * (block + k) + g - 1))
                nc.vector.tensor_tensor_reduce(unread[:, g, :], mod_w[:, k, :], c_all[:, g, :], 1.0, 0.0,
                                               ALU.mult, ALU.add, accum_out=sums[:, k, g:g + 1]).then_inc(mod_summed, 1)

            def mod_bias(i, step, block):
                dve.wait_ge(mod_summed, i * (2 * step) + (2 * (block + MSLOTS)))
                at = bass.ds(i * step + (block + KC), MSLOTS)
                tt(mod[:, at, :], sums[:, :, :], broad(mod_b[:, at], [P, MSLOTS, 2], 2), ALU.add).then_inc(mod_ready, 1)

            def mod_four(i):
                for k in range(MSLOTS):
                    for g in range(2):
                        mod_group(i, MSLOTS, 0, k, g)
                mod_bias(i, MSLOTS, 0)

            def mod_scales(norms):
                for n in norms:
                    layer, which = NORMS[n]
                    at = (layer * 6 + 3 * which + 1) * KC
                    last = stt(scales[:, n], mod[:, at:at + KC, :], 1.0, broad(gains[:, n, :], [P, KC, 2], 2),
                               ALU.add, ALU.mult)
                last.then_inc(scales_ready, 1)

            parts = [0]

            def pipelined(first, second):
                for k in range(KC + 1):
                    if k < KC:
                        first(k)
                    if k:
                        second(k - 1)

            def inverse_root(n, width):
                v, r, t = (stat[:, s, 0:width] for s in (0, 2, 3))
                dve.wait_ge(std_ready, n + 1)
                settle(stt(t, r, -0.5, r, ALU.mult, ALU.mult))
                settle(tt(t, t, v, ALU.mult))
                settle(stt(r, t, 1.5, r, ALU.add, ALU.mult))

            roots = [0]

            def scale_of(bank, width):
                ts(stat[:, 0, 0:width], ps[:, bank, 0:width], 1.0 / D, EPS, ALU.mult, ALU.add).then_inc(var_ready, 1)
                inverse_root(roots[0], width)
                roots[0] += 1

            def normalise(n):
                dve.wait_ge(stat_ready, n + 1)
                scale_of(ACC, T)
                r = stat[:, 2, 0:T]
                if n == 2 * DEPTH:
                    for k in range(KC):
                        stt(hf[:, k, :], x[:, k, :], gains[:, n, k:k + 1], r, ALU.mult, ALU.mult).then_inc(out_ready, 1)
                    return
                if n == 0:
                    dve.wait_ge(c_ready, 2)
                    rounds(dve, MOD_FIRST // MSLOTS, mod_four, peel=True)
                    dve.wait_ge(mod_ready, MOD_FIRST // MSLOTS)
                    mod_scales([0])
                    dve.wait_ge(shift_done, 1)
                    settle(tt(mod[:, 0:KC, :], ps[:, ACC + 1, 0:2 * KC].rearrange("p (a b) -> p a b", b=2),
                              broad(mod_b[:, 0:KC], [P, KC, 2], 2), ALU.add))
                dve.wait_ge(scales_ready, min(n, 2) + 1)
                layer, which = NORMS[n]

                def scaled(k):
                    for g, start, count in SEGS:
                        cols = slice(start, start + count)
                        last = stt(hf[:, k, cols], x[:, k, cols], scales[:, n, k, g:g + 1], r[:, cols], ALU.mult, ALU.mult)
                    last.then_inc(z_ready, 1)

                def low(k):
                    parts[0] += 1
                    dve.wait_ge(hi_part, parts[0])
                    for g, start, count in SEGS:
                        cols = slice(start, start + count)
                        last = stt(h_lo[:, k, cols], hf[:, k, cols], mod_col(layer, 3 * which, k, g),
                                   h_hi[:, k, cols].bitcast(F32), ALU.add, ALU.subtract)
                    last.then_inc(operand_ready, 1)

                pipelined(scaled, low)

            def low_operand(k):
                parts[0] += 1
                dve.wait_ge(hi_part, parts[0])
                tt(h_lo[:, k, :], hf[:, k, :], h_hi[:, k, :].bitcast(F32), ALU.subtract).then_inc(operand_ready, 1)

            def square(k):
                tt(hf[:, k, :], x[:, k, :], x[:, k, :], ALU.mult).then_inc(sq_ready, 1)

            def residual(name, k):
                dve.wait_ge(proj_taken, R0[name] + k + 1)
                settle(tt(x[:, k, :], x[:, k, :], hf[:, k, :], ALU.add))
                square(k)

            def attention():
                with dve.Fori(MOD_FIRST // MSLOTS, LATE_MODS // MSLOTS) as i:
                    mod_four(i)
                dve.wait_ge(small_loaded, 16 * len(small))
                dve.wait_ge(turn_done, 1)
                rot = ps[:, ACC:ACC + 3, :].rearrange("p a b -> p (a b)")[:, 0:5 * LAT].rearrange(
                    "p (c t) -> p c t", c=5)
                tt(turned, rot, broad(sin, [P, 5, LAT], 1), ALU.mult)
                settle(tt(qk[:, :, CTX:T], qk[:, :, CTX:T], broad(cos, [P, 5, LAT], 1), ALU.mult))
                tt(qk[:, :, CTX:T], qk[:, :, CTX:T], turned, ALU.add).then_inc(roped, 1)

                def late_mod(n):
                    block, k = LATE_MODS + n // MSLOTS * MSLOTS, n % MSLOTS
                    for g in range(2):
                        mod_group(0, 0, block, k, g)
                    if k == MSLOTS - 1:
                        mod_bias(0, 0, block)

                def front(n):
                    b = n % 3
                    head = n // 2 + PAIRS * (n % 2)
                    dve.wait_ge(logits_done, n + 1)
                    if n >= 3:
                        dve.wait_ge(pt_done, n - 2)
                    bank = ACC + 2 * (n % 2)
                    ts(logits[b][:, 0:CTX], ps[:, bank, 0:CTX], SCALE, None, ALU.mult)
                    stt(logits[b][:, CTX:CTX + T], ps[:, bank, CTX:CTX + T], SCALE, mask[:, 0, :], ALU.mult, ALU.add)
                    stt(logits[b][:, CTX + T:CTX + 2 * T], ps[:, bank + 1, 0:T], SCALE, mask[:, 1, :],
                        ALU.mult, ALU.add).then_inc(logits_read, 1)
                    dve.wait_ge(logits_read, n + 1)
                    nc.vector.tensor_reduce(sm[:, b, 0, 0:1], logits[b][:, 0:CTX], AX.X, ALU.max)
                    settle(nc.vector.tensor_reduce(sm[:, b, 0, 1:3], logits[b][:, CTX:].rearrange(
                        "p (a k) -> p a k", a=2), AX.X, ALU.max))
                    settle(ts(sm[:, b, 1, :], sm[:, b, 0, :], sink[:, head:head + 1], None, ALU.max))
                    ts(sm[:, b, 1, :], sm[:, b, 1, :], -1.0, None, ALU.mult).then_inc(max_ready, 1)

                def back(n):
                    b = n % 3
                    dve.wait_ge(exp_ready, n + 1)
                    settle(tt(sm[:, b, 4, :], sm[:, b, 2, :], sm[:, b, 3, :], ALU.add))
                    settle(nc.vector.reciprocal(sm[:, b, 4, :], sm[:, b, 4, :]))
                    start = 0
                    for piece, width in enumerate((CTX, T, T)):
                        part = logits[b][:, start:start + width]
                        last = ts(part, part, sm[:, b, 4, piece:piece + 1], None, ALU.mult)
                        start += width
                    last.then_inc(p_ready, 1)

                front(0)
                front(1)
                for n in range(N_HEADS):
                    back(n)
                    if n + 2 < N_HEADS:
                        front(n + 2)
                    if n % 2:
                        late_mod(n // 2)
                    if n == 3:
                        for g in range(NG):
                            low_operand(PAIRS + g)
                    if n >= 3 and n % 2:
                        low_operand((n - 3) // 2)
                low_operand(PAIRS - 1)
                for k in range(KC):
                    late_mod(MSLOTS + k)
                    if k == KC - 1:
                        dve.wait_ge(mod_ready, MOD_EARLY // MSLOTS)
                        mod_scales([1])
                    residual("out", k)

            def convolution():
                def product(i, s):
                    dve.wait_ge(proj_taken, i * 4 + (R0["w1"] + 2 * s + 2))
                    for g, start, n in SEGS:
                        at = CPAD * (g + 1) + start
                        last = tt(a_pad[:, bass.ds(i * 2 + s, 1), at:at + n],
                                  glu[:, s, 0:1, start:start + n], glu[:, s, 1:2, start:start + n], ALU.mult)
                    last.then_inc(glu_out, 1)

                def taps(k, first, end):
                    if first == 0:
                        dve.wait_ge(glu_out, k + 1)
                    for j in range(first, end):
                        src = a_pad[:, bass.ds(k, 1), j:j + CONV_OUT]
                        out = odd[:, 0:1, :] if j % 2 else conv[:, bass.ds(k, 1), :]
                        w = dw[:, bass.ds(k, 1), j:j + 1].rearrange("p a b -> p (a b)")
                        if j == 1:
                            since(dve, conv_ready, k)
                        since(dve, tap_done, k * CONV_WIDTH + (j - 1))
                        if j == 0:
                            last = ts(out, src, w, cvecs[:, 0, bass.ds(k, 1)], ALU.mult, ALU.add)
                        elif j == 1:
                            last = ts(out, src, w, None, ALU.mult)
                        else:
                            last = stt(out, src, w, out, ALU.mult, ALU.add)
                        last.then_inc(tap_done, 1)

                def joined(k):
                    dve.wait_ge(tap_done, (k + 1) * CONV_WIDTH)
                    tt(conv[:, bass.ds(k, 1), :], conv[:, bass.ds(k, 1), :], odd[:, 0:1, :], ALU.add).then_inc(conv_ready, 1)

                def beside(i):
                    product(i, 0)
                    taps(i, 0, CONV_WIDTH // 2)
                    product(i, 1)
                    taps(i, CONV_WIDTH // 2, CONV_WIDTH)
                    joined(i)

                def alone(i):
                    taps(i, 0, CONV_WIDTH)
                    joined(i)

                rounds(dve, KC // 2, beside, peel=True)
                with dve.Fori(KC // 2, CONV_DVE) as i:
                    alone(i)
                dve.wait_ge(mean_done, 1)
                settle(ts(stat[:, 0, :], ps[:, ACC, 0:CONV_OUT], 1.0 / D, None, ALU.mult))
                for k in range(KC):
                    tt(conv[:, k, :], conv[:, k, :], stat[:, 0, :], ALU.subtract).then_inc(centred, 1)
                dve.wait_ge(mean_done, 2)
                scale_of(ACC + 1, CONV_OUT)

                def scaled(k):
                    tt(conv[:, k, :], conv[:, k, :], stat[:, 2, :], ALU.mult).then_inc(z_ready, 1)

                pipelined(scaled, low_operand)
                for k in range(KC):
                    residual("w2", k)

            def top_keys(layer):
                dve.wait_ge(iota_ready, 2)
                key_u = key_us.bitcast(U32)
                half = PEER_HEADS // 2

                def candidates(part):
                    shape = [P, half, TOPK, TOPK]
                    heads = slice(part * half, (part + 1) * half)
                    chosen = slice(part * half * TOPK, (part + 1) * half * TOPK)
                    iota = iota16[:, :].unsqueeze(1).unsqueeze(1).broadcast_to(shape)
                    pos = pos_u.bitcast(U32)
                    flat = cand.rearrange("p h a b -> p h (a b)")
                    for t in range(NT):
                        nc.vector.tensor_copy(key_f, key_u[:, t, 2 * part * half:2 * (part + 1) * half])
                        pairs = vals[:, t].rearrange("p (h s) k -> p h s k", s=2)[:, heads]
                        settle(tt(cand, broad(pairs[:, :, 0, :], shape, 3), broad(pairs[:, :, 1, :], shape, 2), ALU.add))
                        low = [slice(h * TOPK, h * TOPK + 8) for h in range(half)]
                        high = [slice(h * TOPK + 8, (h + 1) * TOPK) for h in range(half)]
                        for h in range(half):
                            last = nc.vector.max(top[:, low[h]], flat[:, h, :])
                        settle(last)
                        for h in range(half):
                            last = nc.vector.max_index(pos[:, 0, low[h]], top[:, low[h]], flat[:, h, :])
                        settle(last)
                        for h in range(half):
                            last = nc.vector.match_replace(flat[:, h, :], top[:, low[h]], flat[:, h, :], LOWEST)
                        settle(last)
                        for h in range(half):
                            last = nc.vector.max(top[:, high[h]], flat[:, h, :])
                        settle(last)
                        for h in range(half):
                            last = nc.vector.max_index(pos[:, 0, high[h]], top[:, high[h]], flat[:, h, :])
                        settle(last)
                        ts(pos[:, 1, :], pos[:, 0, :], 4, None, ALU.logical_shift_right)
                        settle(ts(pos[:, 2, :], pos[:, 0, :], TOPK - 1, None, ALU.bitwise_and))
                        settle(nc.vector.tensor_copy(pos_f, pos[:, 1:3, :]))
                        keys_of = key_f.rearrange("p (h s) k -> p h s k", s=2)
                        hot = cand
                        for side in range(2):
                            rank = pos_f[:, side, :].rearrange("p (h k) -> p h k", h=half)
                            settle(tt(hot, broad(rank, shape, 3), iota, ALU.is_equal))
                            settle(tt(hot, hot, broad(keys_of[:, :, side, :], shape, 2), ALU.mult))
                            settle(nc.vector.tensor_reduce(
                                sel[:, 1 + side, t, chosen].rearrange("p (h k) -> p h k", h=half), hot, AX.X, ALU.add))
                        best = top.rearrange("p (h k) -> p h k", h=half)
                        last = tt(sel[:, 0, t, chosen].rearrange("p (h k) -> p h k", h=half), best,
                                  best[:, :, 0:1].broadcast_to([P, half, TOPK]), ALU.subtract)
                        if t < NT - 1:
                            settle(last)
                    return last

                for q in range(HS // 4):
                    dve.wait_ge(s_taken, layer * HS + 4 * (q + 1))
                    each = [(t, c) for t in range(NT) for c in range(4 * q, 4 * q + 4)]
                    for t, c in each:
                        last = nc.vector.max(vals[:, t, c, 0:8], s_all[:, t, c, :])
                    settle(last)
                    for t, c in each:
                        last = nc.vector.max_index(key_u[:, t, c, 0:8], vals[:, t, c, 0:8], s_all[:, t, c, :])
                    settle(last)
                    for t, c in each:
                        last = nc.vector.match_replace(s_all[:, t, c, :], vals[:, t, c, 0:8], s_all[:, t, c, :], LOWEST)
                    settle(last)
                    for t, c in each:
                        last = nc.vector.max(vals[:, t, c, 8:16], s_all[:, t, c, :])
                    settle(last)
                    for t, c in each:
                        last = nc.vector.max_index(key_u[:, t, c, 8:16], vals[:, t, c, 8:16], s_all[:, t, c, :])
                    settle(last)
                    if q == 1:
                        settle(candidates(0))
                last = candidates(1)
                last.then_inc(top_ready, 1)
                dve.wait_ge(exp_done, layer + 1)
                e = sel[:, 3].rearrange("p n (h k) -> p (n h) k", k=TOPK)
                settle(nc.vector.tensor_reduce(gsum[:, 0, :], e, AX.X, ALU.add))
                settle(nc.vector.reciprocal(gsum[:, 1, :], gsum[:, 0, :]))
                tt(e, e, broad(gsum[:, 1, :], [P, NT * PEER_HEADS, TOPK], 2), ALU.mult).then_inc(sel_ready, 1)
                dve.wait_ge(cols_done, layer + 1)
                for s in range(2):
                    nc.vector.tensor_copy(col_key[:, s, :], ps[:, ACC + s, 0:T])
                g = ps[:, ACC + 2, 0:T]
                settle(nc.vector.tensor_copy(col_b, g))
                settle(nc.vector.tensor_copy(col_g[:, 0, :], col_b))
                settle(tt(col_g[:, 2, :], g, col_g[:, 0, :], ALU.subtract))
                settle(nc.vector.tensor_copy(col_b, col_g[:, 2, :]))
                settle(nc.vector.tensor_copy(col_g[:, 1, :], col_b))
                settle(tt(col_g[:, 2, :], col_g[:, 2, :], col_g[:, 1, :], ALU.subtract))

            def one_hots(layer):
                base = layer * GBLOCKS

                def table_rows(i):
                    for j in range(2 * SETS):
                        b = j % HOTS
                        since(dve, g_done, i * (2 * SETS) + (base + j - HOTS + 1))
                        for q in range(TOK):
                            tok = bass.ds(i * (2 * CHUNK) + (j * TOK + q), 1)
                            ts(oh2[:, b, q, :], iota_b[:, :], col_key[:, 1, tok], None, ALU.is_equal)
                            for part in range(3):
                                last = ts(oh1[:, b, part, q, :], iota_b[:, :], col_key[:, 0, tok],
                                          col_g[:, part, tok], ALU.is_equal, ALU.mult)
                        last.then_inc(hot_ready, 1)

                rounds(dve, GBLOCKS // (2 * SETS), table_rows, peel=layer == 0)

            def sweep(layer):
                base = layer * N_KEYS
                def eight(i, mods):
                    for j in range(8):
                        dve.wait_ge(a_loaded[j % 4], i * 32 + (16 * (base // 4 + j // 4 + 1)))
                        if j % 4 == 0:
                            dve.wait_ge(g_loaded[j // 4], i * 16 + 16 * (base // 8 + 1))
                        tt(wf[:, j % 2, :].rearrange("p (c t) -> p c t", t=CHUNK),
                           a_in[:, j % 4, :].rearrange("p (c t) -> p c t", t=CHUNK),
                           g_in[:, j // 4, :, (j % 4) * CHUNK:(j % 4 + 1) * CHUNK], ALU.mult).then_inc(w_ready, 1)
                        if mods:
                            mod_group(i, MSLOTS, MOD_EARLY - MSLOTS, j // 2, j % 2)
                        dve.wait_ge(whi_ready, i * 8 + (base + j + 1))
                        tt(g_lo[:, j % 2, :], wf[:, j % 2, :], g_hi[:, j % 2, :].bitcast(F32),
                           ALU.subtract).then_inc(wlo_ready, 1)
                    if mods:
                        mod_bias(i, MSLOTS, MOD_EARLY - MSLOTS)

                if layer == 0:
                    eight(0, False)
                    settle(nc.vector.memset(a_pad, 0.0))
                    dve.wait_ge(c_ready, 3)
                    for j in range(4):
                        dve.wait_ge(a_stored[j], 16 * (N_KEYS // 4))
                    with dve.Fori(1, MOD_ROUNDS + 1) as i:
                        eight(i, True)
                with dve.Fori(0 if layer else MOD_ROUNDS + 1, N_KEYS // 8) as i:
                    eight(i, False)
                if layer == 0:
                    dve.wait_ge(mod_ready, SUM_BLOCKS // MSLOTS)
                    at = (6 + 2) * KC
                    settle(tt(gb2[:, :, :], mod[:, at:at + KC, :], broad(cvecs[:, 3, :], [P, KC, 2], 2), ALU.mult))
                    mod_scales([2, 3])
                for k in range(KC):
                    if k < KC - 1:
                        dve.wait_ge(y_done, layer * (KC - 1) + k + 1)
                    else:
                        dve.wait_ge(block_done, M0[f"v{layer}"] + N_KEYS)
                    for g, start, n in SEGS:
                        cols = slice(start, start + n)
                        last = stt(x[:, k, cols], ps[:, (ACC + k) % 8, cols], mod_col(layer, 5, k, g), x[:, k, cols],
                                   ALU.mult, ALU.add)
                    last.then_inc(x_ready, 1)
                dve.wait_ge(x_ready, (layer + 1) * KC)

            for k in range(KC):
                square(k)
            for layer in range(DEPTH):
                normalise(2 * layer)
                [attention, convolution][layer]()
                normalise(2 * layer + 1)
                top_keys(layer)
                one_hots(layer)
                sweep(layer)
            normalise(2 * DEPTH)

        @block.tensor
        def _(pe):
            mm = nc.tensor.matmul
            pe.wait_ge(consts_ready, 1)

            operands = [0]

            def project(i, step, m, r, chunks=()):
                pe.wait_ge(lo_ready, i * step + (m + 1))
                if r >= 2:
                    pe.wait_ge(proj_taken, i * step + (r - 1))
                out, s = ps[:, PROJ + r % 2, 0:T], m % RING
                for n, k in enumerate(chunks or range(KC)):
                    if chunks:
                        operands[0] += 1
                        pe.wait_ge(operand_ready, operands[0])
                    cols = slice(k * P, (k + 1) * P)
                    mm(out, w_hi[:, s, cols], h_hi[:, k, :], start=n == 0, stop=False)
                    mm(out, w_hi[:, s, cols], h_lo[:, k, :], start=False, stop=False)
                    last = mm(out, w_lo[:, s, cols], h_hi[:, k, :], start=False, stop=n == KC - 1)
                last.then_inc(block_done, 1)

            def project_pair(m, r):
                pe.wait_ge(lo_ready, m + 2)
                if r >= 2:
                    pe.wait_ge(proj_taken, r)
                for k in range(KC):
                    operands[0] += 1
                    pe.wait_ge(operand_ready, operands[0])
                    cols = slice(k * P, (k + 1) * P)
                    for b in range(2):
                        out, s = ps[:, PROJ + (r + b) % 2, 0:T], (m + b) % RING
                        mm(out, w_hi[:, s, cols], h_hi[:, k, :], start=k == 0, stop=False)
                        mm(out, w_hi[:, s, cols], h_lo[:, k, :], start=False, stop=False)
                        last = mm(out, w_lo[:, s, cols], h_hi[:, k, :], start=False, stop=k == KC - 1)
                        if k == KC - 1:
                            last.then_inc(block_done, 1)

            def blocks(name, chunks=()):
                m, r = M0[name], R0[name]
                if chunks:
                    project(0, 4, m, r, chunks)
                    project(0, 4, m + 1, r + 1)
                else:
                    project_pair(m, r)
                for j in range(2, 4):
                    project(0, 4, m + j, r + j)
                with pe.Fori(1, dict(SEGMENTS)[name] // 4) as i:
                    for j in range(4):
                        project(i, 4, m + j, r + j)

            def column_sums(n):
                for k in range(KC):
                    pe.wait_ge(sq_ready, n * KC + k + 1)
                    last = mm(ps[:, ACC, 0:T], ones[:, :], hf[:, k, :], start=k == 0, stop=k == KC - 1)
                last.then_inc(stat_ready, 1)

            def attention():
                def scores_of(n):
                    c, kv = n // 2, n % 2
                    rows = slice(HEAD_DIM * kv, HEAD_DIM * (kv + 1))
                    if n >= 2:
                        pe.wait_ge(logits_read, n - 1)
                    bank = ACC + 2 * (n % 2)
                    mm(ps[:, bank, 0:CTX], qk[rows, c, 0:CTX], qk[rows, 4, 0:CTX], start=True, stop=True)
                    for b in range(2):
                        out = ps[:, bank, CTX:CTX + T] if b == 0 else ps[:, bank + 1, 0:T]
                        q = qk[rows, c, CTX + b * P:CTX + (b + 1) * P]
                        mm(out[:, 0:PAST], q, cache_k[rows, :], start=True, stop=True)
                        last = mm(out[:, PAST:], q, qk[rows, 4, CTX:T], start=True, stop=True)
                    last.then_inc(logits_done, 1)

                project_pair(M0["in"], R0["in"])
                for c in range(2, 9):
                    project(0, 0, M0["in"] + c, R0["in"] + c)
                    if c == 5:
                        pe.wait_ge(small_loaded, 16 * len(small))
                        pe.wait_ge(proj_taken, R0["in"] + 5)
                        for q in range(5):
                            last = mm(ps[:, ACC + q // 2, (q % 2) * LAT:(q % 2 + 1) * LAT], turn[:, :],
                                      qk[:, q, CTX:T], start=True, stop=True)
                        last.then_inc(turn_done, 1)
                pe.wait_ge(roped, 1)
                scores_of(0)
                scores_of(1)
                project(0, 0, M0["in"] + 9, R0["in"] + 9)

                def v_transposed():
                    pe.wait_ge(proj_taken, R0["in"] + 10)
                    for t in range(NT):
                        last = nc.tensor.transpose(ps[:, PROJ, t * P:(t + 1) * P], hf[:, 0, t * P:(t + 1) * P], ident[:, :])
                    last.then_inc(v_done, 1)

                def transposes_of(n):
                    pe.wait_ge(p_ready, n + 1)
                    if n >= 1:
                        pe.wait_ge(pt_copied, n)
                    flat = ps[:, 6:8, :].rearrange("p a b -> p (a b)")
                    for s in range(7):
                        last = nc.tensor.transpose(flat[:, s * P:(s + 1) * P], logits[n % 3][:, s * P:(s + 1) * P],
                                                   ident[:, :])
                    last.then_inc(pt_done, 1)

                def values_of(n):
                    c, kv = n // 2, n % 2
                    rows = slice(HEAD_DIM * kv, HEAD_DIM * (kv + 1))
                    pe.wait_ge(pt_copied, n + 1)
                    if kv == 0 and c >= 2:
                        pe.wait_ge(att_taken, c - 1)
                    if n == 2:
                        pe.wait_ge(mixed_taken, NG)
                    lat = (cache_v[:, rows], v_nat[:, 1, rows], v_nat[:, 2, rows])
                    s = 0
                    for piece, vs in enumerate(((v_nat[:, 0, rows],), lat, lat)):
                        for a, v in enumerate(vs):
                            last = mm(ps[rows, PROJ + c % 2, piece * P:(piece + 1) * P], v,
                                      p_t[n % 2][s // 4][:, s % 4 * P:(s % 4 + 1) * P], start=a == 0, stop=a == len(vs) - 1)
                            s += 1
                    last.then_inc(att_done, 1)

                def mix(g):
                    pe.wait_ge(pooled_ready, g + 1)
                    if g >= 1:
                        pe.wait_ge(mixed_taken, g)
                    mm(ps[:, PROJ + 1, 0:T], w_pool[:, g, :], pooled[:, g, :], start=True, stop=True).then_inc(mixed_done, 1)

                for n in range(N_HEADS):
                    if n == 1:
                        pe.wait_ge(v_taken, 1)
                    if n in (1, 2):
                        mix(2 * (n - 1))
                    if n + 2 < N_HEADS:
                        scores_of(n + 2)
                    if n >= 1:
                        values_of(n - 1)
                    if n in (1, 2):
                        mix(2 * (n - 1) + 1)
                    if n == 0:
                        v_transposed()
                    transposes_of(n)
                values_of(N_HEADS - 1)
                pe.wait_ge(att_taken, PAIRS - 1)
                blocks("out", [*range(PAIRS, KC), *range(PAIRS)])

            def convolution():
                blocks("w1")
                for c in range(KC - CONV_DVE):
                    k = CONV_DVE + c
                    pe.wait_ge(glu_out, k + 1)
                    for j in range(CONV_WIDTH):
                        pe.wait_ge(diag_ready, c * CONV_WIDTH + j + 1)
                        last = mm(ps[:, ACC + 2 + c, 0:CONV_OUT], diag[:, j, :], a_pad[:, k, j:j + CONV_OUT],
                                  start=j == 0, stop=j == CONV_WIDTH - 1)
                        if j < CONV_WIDTH - 1:
                            last.then_inc(diag_used, 1)
                    last.then_inc(conv_done, 1)
                for n, k in enumerate([*range(CONV_DVE, KC), *range(CONV_DVE)]):
                    if k >= CONV_DVE:
                        pe.wait_ge(conv_taken, k - CONV_DVE + 1)
                    else:
                        pe.wait_ge(conv_ready, k + 1)
                    last = mm(ps[:, ACC, 0:CONV_OUT], ones[:, :], conv[:, k, :], start=n == 0, stop=n == KC - 1)
                last.then_inc(mean_done, 1)
                for k in range(KC):
                    pe.wait_ge(csq_ready, k + 1)
                    last = mm(ps[:, ACC + 1, 0:CONV_OUT], ones[:, :], conv_sq[:, k, :], start=k == 0, stop=k == KC - 1)
                last.then_inc(mean_done, 1)
                blocks("w2")

            def scores(layer):
                m0, r0 = M0[f"wq{layer}"], R0[f"wq{layer}"]
                pe.wait_ge(keys_loaded, 16 * (layer + 1))
                def queries(i):
                    def score(j):
                        pe.wait_ge(proj_taken, i * 4 + (r0 + j + 1))
                        if j == 0:
                            since(pe, s_taken, i * 4 + layer * HS)
                        for t in range(NT):
                            last = mm(ps[:, ACC + j, t * P:(t + 1) * P], ga[:, j, t * P:(t + 1) * P],
                                      keys[:, bass.ds(i * 4 + j, 1), :].rearrange("p a k -> p (a k)"),
                                      start=True, stop=True)
                        last.then_inc(s_done, 1)

                    if isinstance(i, int) and i == 0:
                        project_pair(m0, r0)
                    else:
                        project(i, 4, m0, r0)
                        project(i, 4, m0 + 1, r0 + 1)
                        score(0)
                    for j in range(2, 4):
                        project(i, 4, m0 + j, r0 + j)
                        if isinstance(i, int) and i == 0 and j == 2:
                            score(0)
                        score(j - 1)
                    score(3)

                rounds(pe, HS // 4, queries, peel=True)

            def experts(layer):
                m0, r0 = M0[f"u{layer}"], R0[f"u{layer}"]
                with pe.Fori(0, UBLOCKS // 4) as i:
                    for j in range(4):
                        project(i, 4, m0 + j, r0 + j)
                pe.wait_ge(sel_ready, layer + 1)
                for a, s in enumerate((1, 2, 3)):
                    for t in range(NT):
                        last = nc.tensor.transpose(ps[:, ACC + a, t * P:(t + 1) * P], sel[:, s, t, :], ident[:, :])
                last.then_inc(cols_done, 1)
                def with_table(i):
                    for j in range(2 * SETS):
                        project(i, 2 * SETS, m0 + UBLOCKS + j, r0 + UBLOCKS + j)
                        b = j % HOTS
                        base = layer * GBLOCKS + j
                        pe.wait_ge(hot_ready, i * (2 * SETS) + (base + 1))
                        since(pe, g_taken, i * (2 * SETS) + (base - HOTS + 1))
                        for q in range(TOK):
                            for part in range(3):
                                last = mm(ps[:, ACC + b, q * P:(q + 1) * P], oh2[:, b, q, :], oh1[:, b, part, q, :],
                                          start=part == 0, stop=part == 2)
                        last.then_inc(g_done, 1)

                rounds(pe, GBLOCKS // (2 * SETS), with_table, peel=layer == 0)
                for j in range(UBLOCKS + GBLOCKS, N_KEYS):
                    project(0, 0, m0 + j, r0 + j)
                pe.wait_ge(g_taken, (layer + 1) * GBLOCKS)
                v0 = M0[f"v{layer}"]

                def block_of(i, j, first=False, final=False):
                    s, b = (v0 + j) % RING, j % 2
                    pe.wait_ge(lo_ready, i * 8 + (v0 + j + 1))
                    pe.wait_ge(wlo_ready, i * 8 + (layer * N_KEYS + j + 1))
                    for k in range(KC):
                        if first and k == KC - ACC:
                            pe.wait_ge(proj_taken, r0 + N_KEYS)
                        cols = slice(k * P, (k + 1) * P)
                        out = ps[:, (ACC + k) % 8, 0:T]
                        mm(out, w_hi[:, s, cols], g_hi[:, b, :], start=first, stop=False)
                        mm(out, w_lo[:, s, cols], g_hi[:, b, :], start=False, stop=False)
                        last = mm(out, w_hi[:, s, cols], g_lo[:, b, :], start=False, stop=final)
                        if final and k < KC - 1:
                            last.then_inc(y_done, 1)
                    last.then_inc(block_done, 1)

                for j in range(8):
                    block_of(0, j, first=j == 0)
                with pe.Fori(1, N_KEYS // 8 - 1) as i:
                    for j in range(8):
                        block_of(i, j)
                for j in range(8):
                    block_of(N_KEYS // 8 - 1, j, final=j == 7)

            def first_shift():
                pe.wait_ge(c_ready, 1)
                for k in range(KC):
                    pe.wait_ge(shift_loaded[k], 16)
                    for half in range(2):
                        last = mm(ps[0:2, ACC + 2 + half, :], cvec[:, k, :], shift_w[k][:, half * 512:(half + 1) * 512],
                                  start=k == 0, stop=k == KC - 1)
                last.then_inc(shift_summed, 1)
                pe.wait_ge(shift_copied, 1)
                for k in range(KC):
                    last = mm(ps[:, ACC + 1, 2 * k:2 * k + 2], shift_rows[:, k * P:(k + 1) * P], ident[0:2, 0:2],
                              start=True, stop=True)
                last.then_inc(shift_done, 1)

            for layer in range(DEPTH):
                column_sums(2 * layer)
                if layer == 0:
                    first_shift()
                [attention, convolution][layer]()
                column_sums(2 * layer + 1)
                scores(layer)
                experts(layer)
            column_sums(2 * DEPTH)


def laid_out(i):
    def chunks(w):
        rows, cols = w.shape
        return w.reshape(KC, P, cols // P, P).transpose(2, 1, 0, 3).reshape(cols // P, P, rows)

    def columns(v):
        return np.moveaxis(v.reshape(v.shape[:-1] + (KC, P)), -1, 0)

    heads = [h for c in range(PAIRS) for h in (c, c + PAIRS)]
    w_in = i["w_in"][0]
    q = w_in[:, :512].reshape(D, N_HEADS, HEAD_DIM)[:, heads].reshape(D, 512)
    w_in = np.concatenate([q, w_in[:, 512:640], w_in[:, 768:], w_in[:, 640:768]], 1)
    w_out = i["w_out"][0]
    w_out = np.concatenate([w_out[:512].reshape(N_HEADS, HEAD_DIM, D)[heads].reshape(512, D), w_out[512:]], 0)
    w1 = i["conv_w1"][0].reshape(D, 2, KC, P)[:, ::-1].transpose(0, 2, 1, 3).reshape(D, 2 * D)
    x = np.concatenate([i["x_prompt"][0], i["x_sample"][0]], 0)
    gains = np.stack([i["norm_mix_g"][0], i["norm_ffn_g"][0], i["norm_mix_g"][1], i["norm_ffn_g"][1], i["final_norm_g"]])
    a = {
        "x": x.T.reshape(KC, P, T).transpose(1, 0, 2),
        "c": np.tile(np.stack([i["c_ctx"], i["c"][0]])[None], (P, 1, 1)),
        "mod_b": columns(i["mod_b"].reshape(DEPTH, 6, D)).reshape(P, MOD_BLOCKS),
        "gains": columns(gains),
        "sink": np.tile(i["attn_sink"][0][None, :], (P, 1)),
        "pool_scale": i["pool_scale"][0].reshape(NG, P).T,
        "b1": columns(i["conv_b1"][0].reshape(2, D)).reshape(P, 2 * KC),
        "dw": i["conv_dw"][0].reshape(CONV_WIDTH, KC, P).transpose(2, 1, 0),
        "cvecs": columns(np.stack([i["conv_dw_b"][0], i["conv_ln_g"][0], i["conv_ln_b"][0], i["conv_b2"][0]])),
        "w_pool": i["w_pool"][0].transpose(1, 0, 2),
        "cache_k": i["cache_k"][0, 0].reshape(PAST, P).T,
        "cache_v": i["cache_v"][0, 0].reshape(PAST, P),
        "keys": i["peer_keys"].reshape(DEPTH, HS, N_KEYS, P).transpose(0, 3, 1, 2),
        "mod_w": i["mod_w"].transpose(0, 2, 1).reshape(MOD_BLOCKS, P, D)[KC:],
        "shift_w": i["mod_w"][0, :, :D].reshape(KC, P, D),
        "c_cols": columns(np.stack([i["c_ctx"], i["c"][0]])).transpose(0, 2, 1),
        "in": chunks(w_in), "out": chunks(w_out), "w1": chunks(w1), "w2": chunks(i["conv_w2"][0]),
    }
    for layer in range(DEPTH):
        a[f"wq{layer}"] = chunks(i["peer_wq"][layer])
        a[f"u{layer}"] = i["peer_u"][layer].reshape(N_KEYS, P, KC, P).transpose(0, 3, 2, 1).reshape(N_KEYS, P, D)
        a[f"v{layer}"] = i["peer_v"][layer].reshape(N_KEYS, P, D)
    a.update(constants())
    return {n: np.ascontiguousarray(v) for n, v in a.items()}


OUTS = {"y": (P, KC, T), "state_k": (P, CTX), "state_v": (CTX, P)}


def kernel(**inputs):
    import concourse.bacc as bacc
    from concourse.bass_utils import run_bass_kernel_spmd

    arrays = laid_out({n: np.asarray(v) for n, v in inputs.items()})
    nc = bacc.Bacc("TRN2", target_bir_lowering=False, num_devices=1)
    io = {n: nc.dram_tensor(f"in_{n}", a.shape, mybir.dt.from_np(a.dtype), kind="ExternalInput").ap()
          for n, a in arrays.items()}
    for n, shape in OUTS.items():
        io[n] = nc.dram_tensor(f"out_{n}", shape, F32, kind="ExternalOutput").ap()
    build(nc, io)
    r = run_bass_kernel_spmd(nc, [{f"in_{n}": a for n, a in arrays.items()}], core_ids=[0]).results[0]
    y = r["out_y"].transpose(1, 0, 2).reshape(D, T).T
    state_k = r["out_state_k"].T.reshape(1, 1, CTX, 2, HEAD_DIM)
    state_v = r["out_state_v"].reshape(1, 1, CTX, 2, HEAD_DIM)
    return (np.ascontiguousarray(y[None, :CTX]), np.ascontiguousarray(y[None, CTX:]),
            np.ascontiguousarray(state_k), np.ascontiguousarray(state_v))
```
